# Optimizing a Trainium2 kernel written in Bass

```python
import math
import jax
import jax.numpy as jnp
from jax import lax
import numpy as np

D_MODEL = 1024
BATCH = 1
SEQ = 512
DEPTH = 2

N_MIXERS = 2
MEM_LEN = 256
EPS = 1e-6

A_HEADS = 12
A_KV_HEADS = 2
A_HEAD_DIM = 64
WINDOW = 128
BLOCK = 128
N_BUCKETS = 32
MAX_DISTANCE = 128

B_QK_HEADS = 3
B_V_HEADS = 6
B_HEAD_DIM = 128
B_CONV = 4
CHUNK = 64

X_HEADS = 4
X_HEAD_DIM = 64

D_FF = 2816
FFN_CONV = 3

A_Q = A_HEADS * A_HEAD_DIM
A_KV = A_KV_HEADS * A_HEAD_DIM
X_Q = X_HEADS * X_HEAD_DIM
B_QK = B_QK_HEADS * B_HEAD_DIM
B_V = B_V_HEADS * B_HEAD_DIM
B_QKV = 2 * B_QK + B_V
IN_A = A_Q + 2 * A_KV + X_Q
IN_B = B_QKV + B_V + 2 * B_V_HEADS + X_Q
MIX_WIDTH = A_Q + X_Q
N_A_LAYERS = (DEPTH + 1) // 2
N_B_LAYERS = DEPTH // 2

kernel_name = "hybrid_swa_sink_deltanet_memxattn_convglu"

def rms_norm(x, g):
    xf = x.astype(jnp.float32)
    y = xf * lax.rsqrt(jnp.mean(xf * xf, axis=-1, keepdims=True) + EPS)
    return (y * g.astype(jnp.float32)).astype(x.dtype)

def l2_normalize(x):
    xf = x.astype(jnp.float32)
    return xf * lax.rsqrt(jnp.sum(xf * xf, axis=-1, keepdims=True) + EPS)

def causal_depthwise_conv(x, w):
    k = w.shape[0]
    return lax.conv_general_dilated(
        x, w[:, None, :].astype(x.dtype), window_strides=(1,), padding=[(k - 1, 0)],
        dimension_numbers=('NWC', 'WIO', 'NWC'), feature_group_count=x.shape[-1])

def t5_causal_bucket(dist):
    n = jnp.maximum(dist, 0)
    max_exact = N_BUCKETS // 2
    nf = jnp.maximum(n, 1).astype(jnp.float32)
    large = max_exact + (jnp.log(nf / max_exact) / math.log(MAX_DISTANCE / max_exact)
                         * (N_BUCKETS - max_exact)).astype(jnp.int32)
    large = jnp.minimum(large, N_BUCKETS - 1)
    return jnp.where(n < max_exact, n, large)

def swa_sink_attention(q, k, v, sinks, rel_bias):
    b, s, _, dh = q.shape
    nb = s // BLOCK
    grp = A_HEADS // A_KV_HEADS
    qb = q.reshape(b, nb, BLOCK, A_KV_HEADS, grp, dh)

    def band(t):
        tb = t.reshape(b, nb, BLOCK, A_KV_HEADS, dh)
        prev = jnp.concatenate([jnp.zeros_like(tb[:, :1]), tb[:, :-1]], axis=1)
        return jnp.concatenate([prev, tb], axis=2)

    kb, vb = band(k), band(v)
    qi = jnp.arange(BLOCK)[:, None]
    kj = jnp.arange(2 * BLOCK)[None, :]
    dist = BLOCK + qi - kj
    band_ok = (dist >= 0) & (dist < WINDOW)
    blk_ok = (jnp.arange(nb)[:, None, None] > 0) | (kj[None] >= BLOCK)
    mask = band_ok[None] & blk_ok
    bias = rel_bias[t5_causal_bucket(dist)]
    bias = jnp.transpose(bias, (2, 0, 1)).reshape(A_KV_HEADS, grp, BLOCK, 2 * BLOCK)

    scores = jnp.einsum('bnqhgd,bnkhd->bnhgqk', qb, kb,
                        preferred_element_type=jnp.float32) * (dh ** -0.5)
    scores = scores + bias.astype(jnp.float32)
    scores = jnp.where(mask[None, :, None, None], scores, -jnp.inf)
    sink = sinks.astype(jnp.float32).reshape(1, 1, A_KV_HEADS, grp, 1, 1)
    m = jnp.maximum(jnp.max(scores, axis=-1, keepdims=True), sink)
    p = jnp.exp(scores - m)
    probs = p / (jnp.sum(p, axis=-1, keepdims=True) + jnp.exp(sink - m))
    out = jnp.einsum('bnhgqk,bnkhd->bnqhgd', probs.astype(v.dtype), vb)
    return out.reshape(b, s, A_HEADS * dh)

def memory_cross_attention(q, mem_k, mem_v):
    b, s = q.shape[0], q.shape[1]
    scores = jnp.einsum('bshd,bmhd->bhsm', q, mem_k,
                        preferred_element_type=jnp.float32) * (X_HEAD_DIM ** -0.5)
    probs = jax.nn.softmax(scores, axis=-1).astype(mem_v.dtype)
    out = jnp.einsum('bhsm,bmhd->bshd', probs, mem_v)
    return out.reshape(b, s, X_Q)

def gated_delta_rule(q, k, v, g, beta):
    b, s, h, dk = q.shape
    dv = v.shape[-1]
    nc = s // CHUNK
    f32 = jnp.float32

    def chunks(t):
        t = t.astype(f32).reshape((b, nc, CHUNK, h) + t.shape[3:])
        return jnp.moveaxis(t, 3, 1)

    qc = chunks(q) * (dk ** -0.5)
    kc = chunks(k)
    vc = chunks(v)
    bc = chunks(beta)
    gc = jnp.cumsum(chunks(g), axis=-1)
    idx = jnp.arange(CHUNK)
    strict = idx[:, None] > idx[None, :]
    incl = idx[:, None] >= idx[None, :]
    gdiff = gc[..., :, None] - gc[..., None, :]
    decay_incl = jnp.exp(jnp.where(incl, gdiff, -jnp.inf))
    kk = jnp.einsum('bhntd,bhnsd->bhnts', kc, kc)
    a_mat = bc[..., :, None] * kk * jnp.where(strict, decay_incl, 0.0)
    eye = jnp.eye(CHUNK, dtype=f32)
    rhs = jnp.concatenate([bc[..., None] * vc, (bc * jnp.exp(gc))[..., None] * kc], axis=-1)
    sol = lax.linalg.triangular_solve(eye + a_mat, rhs, left_side=True, lower=True,
                                      unit_diagonal=True)
    u, w = sol[..., :dv], sol[..., dv:]
    attn_qk = jnp.einsum('bhntd,bhnsd->bhnts', qc, kc) * decay_incl
    q_decay = qc * jnp.exp(gc)[..., None]
    k_tail = kc * jnp.exp(gc[..., -1:] - gc)[..., None]
    decay_chunk = jnp.exp(gc[..., -1])

    def step(state, xs):
        u_n, w_n, a_n, qd_n, kt_n, dc_n = xs
        delta = u_n - jnp.einsum('bhtk,bhkv->bhtv', w_n, state)
        out = (jnp.einsum('bhtk,bhkv->bhtv', qd_n, state)
               + jnp.einsum('bhts,bhsv->bhtv', a_n, delta))
        state = dc_n[..., None, None] * state + jnp.einsum('bhsk,bhsv->bhkv', kt_n, delta)
        return state, out

    xs = tuple(jnp.moveaxis(t, 2, 0) for t in (u, w, attn_qk, q_decay, k_tail, decay_chunk))
    state0 = jnp.zeros((b, h, dk, dv), f32)
    _, out = lax.scan(step, state0, xs)
    return jnp.transpose(out, (1, 0, 3, 2, 4)).reshape(b, s, h, dv)

def swa_group(proj, sinks, rel_bias):
    b, s, _ = proj.shape
    q, k, v = jnp.split(proj, [A_Q, A_Q + A_KV], axis=-1)
    q = q.reshape(b, s, A_HEADS, A_HEAD_DIM)
    k = k.reshape(b, s, A_KV_HEADS, A_HEAD_DIM)
    v = v.reshape(b, s, A_KV_HEADS, A_HEAD_DIM)
    return swa_sink_attention(q, k, v, sinks, rel_bias)

def deltanet_group(proj, conv_w, a_log, dt_bias, norm_g):
    b, s, _ = proj.shape
    f32 = jnp.float32
    qkv, z, beta_logit, a_logit = jnp.split(
        proj, [B_QKV, B_QKV + B_V, B_QKV + B_V + B_V_HEADS], axis=-1)
    qkv = jax.nn.silu(causal_depthwise_conv(qkv, conv_w))
    q, k, v = jnp.split(qkv, [B_QK, 2 * B_QK], axis=-1)
    rep = B_V_HEADS // B_QK_HEADS
    q = jnp.repeat(l2_normalize(q.reshape(b, s, B_QK_HEADS, B_HEAD_DIM)), rep, axis=2)
    k = jnp.repeat(l2_normalize(k.reshape(b, s, B_QK_HEADS, B_HEAD_DIM)), rep, axis=2)
    v = v.reshape(b, s, B_V_HEADS, B_HEAD_DIM)
    beta = jax.nn.sigmoid(beta_logit.astype(f32))
    g = -jnp.exp(a_log.astype(f32)) * jax.nn.softplus(a_logit.astype(f32) + dt_bias.astype(f32))
    o = gated_delta_rule(q, k, v, g, beta)
    o = o * lax.rsqrt(jnp.mean(o * o, axis=-1, keepdims=True) + EPS) * norm_g.astype(f32)
    o = o * jax.nn.silu(z.reshape(b, s, B_V_HEADS, B_HEAD_DIM).astype(f32))
    return o.reshape(b, s, B_V).astype(proj.dtype)

def conv_glu(hn, w_gate_up, conv_w, conv_b, w_down):
    gate, up = jnp.split(hn @ w_gate_up, [D_FF], axis=-1)
    gate = causal_depthwise_conv(gate, conv_w) + conv_b
    return (jax.nn.silu(gate) * up) @ w_down

def setup_inputs(seed: int = 0) -> dict:
    key = jax.random.key(seed)
    ks = jax.random.split(key, 24)
    f32 = jnp.float32

    def dense(k, shape, fan_in):
        return jax.random.normal(k, shape, f32) * (fan_in ** -0.5)

    def gain(k, shape):
        return 1.0 + 0.02 * jax.random.normal(k, shape, f32)

    dt = jnp.exp(jax.random.uniform(ks[13], (N_B_LAYERS, B_V_HEADS), f32,
                                    math.log(1e-3), math.log(1e-1)))
    return {
        'x': jax.random.normal(ks[0], (BATCH, SEQ, D_MODEL), f32),
        'mem': jax.random.normal(ks[1], (BATCH, MEM_LEN, D_MODEL), f32),
        'rel_bias': 0.5 * jax.random.normal(ks[2], (N_BUCKETS, A_HEADS), f32),
        'norm_mix_g': gain(ks[3], (DEPTH, D_MODEL)),
        'norm_mem_g': gain(ks[4], (DEPTH, D_MODEL)),
        'w_mem_kv': dense(ks[5], (DEPTH, D_MODEL, 2 * X_Q), D_MODEL),
        'w_out': dense(ks[6], (DEPTH, MIX_WIDTH, D_MODEL), MIX_WIDTH),
        'w_in_a': dense(ks[7], (N_A_LAYERS, D_MODEL, IN_A), D_MODEL),
        'sinks_a': 0.5 * jax.random.normal(ks[8], (N_A_LAYERS, A_HEADS), f32),
        'w_in_b': dense(ks[9], (N_B_LAYERS, D_MODEL, IN_B), D_MODEL),
        'conv_qkv_b': dense(ks[10], (N_B_LAYERS, B_CONV, B_QKV), B_CONV),
        'a_log_b': jnp.log(jax.random.uniform(ks[11], (N_B_LAYERS, B_V_HEADS), f32, 1.0, 16.0)),
        'dt_bias_b': dt + jnp.log(-jnp.expm1(-dt)),
        'out_norm_g_b': gain(ks[12], (N_B_LAYERS, B_HEAD_DIM)),
        'norm_ffn_g': gain(ks[14], (DEPTH, D_MODEL)),
        'w_gate_up': dense(ks[15], (DEPTH, D_MODEL, 2 * D_FF), D_MODEL),
        'ffn_conv_w': dense(ks[16], (DEPTH, FFN_CONV, D_FF), FFN_CONV),
        'ffn_conv_b': 0.02 * jax.random.normal(ks[17], (DEPTH, D_FF), f32),
        'w_down': dense(ks[18], (DEPTH, D_FF, D_MODEL), D_FF),
        'final_norm_g': gain(ks[19], (D_MODEL,)),
    }

def reference(x, mem, rel_bias, norm_mix_g, norm_mem_g, w_mem_kv, w_out, w_in_a, sinks_a,
              w_in_b, conv_qkv_b, a_log_b, dt_bias_b, out_norm_g_b, norm_ffn_g, w_gate_up,
              ffn_conv_w, ffn_conv_b, w_down, final_norm_g):
    b, s, _ = x.shape
    h = x
    for i in range(DEPTH):
        j = i // N_MIXERS
        hn = rms_norm(h, norm_mix_g[i])
        mem_kv = rms_norm(mem, norm_mem_g[i]) @ w_mem_kv[i]
        mem_k = mem_kv[..., :X_Q].reshape(b, MEM_LEN, X_HEADS, X_HEAD_DIM)
        mem_v = mem_kv[..., X_Q:].reshape(b, MEM_LEN, X_HEADS, X_HEAD_DIM)
        if i % N_MIXERS == 0:
            proj = hn @ w_in_a[j]
            self_out = swa_group(proj[..., :IN_A - X_Q], sinks_a[j], rel_bias)
        else:
            proj = hn @ w_in_b[j]
            self_out = deltanet_group(proj[..., :IN_B - X_Q], conv_qkv_b[j], a_log_b[j],
                                      dt_bias_b[j], out_norm_g_b[j])
        xq = proj[..., -X_Q:].reshape(b, s, X_HEADS, X_HEAD_DIM)
        cross_out = memory_cross_attention(xq, mem_k, mem_v)
        h = h + jnp.concatenate([self_out, cross_out], axis=-1) @ w_out[i]
        h = h + conv_glu(rms_norm(h, norm_ffn_g[i]), w_gate_up[i], ffn_conv_w[i],
                         ffn_conv_b[i], w_down[i])
    return rms_norm(h, final_norm_g)


_drawn_inputs = setup_inputs


def setup_inputs(seed=0):
    import zlib

    import numpy as np

    out = dict(_drawn_inputs(seed))
    spreads = {}
    factors = {'norm_mix_g': 3.614,
     'norm_mem_g': 8.0,
     'sinks_a': 8.0,
     'out_norm_g_b': 23.719,
     'ffn_conv_b': 11.119,
     'final_norm_g': 8.057,
     'norm_ffn_g': 7.537}
    for name, (base, spread) in spreads.items():
        noise = np.random.default_rng([zlib.crc32(name.encode()), seed]).standard_normal(out[name].shape)
        drawn = base * np.exp(spread * noise) if base else spread * noise
        out[name] = jnp.asarray(drawn.astype(out[name].dtype))
    for name, factor in factors.items():
        out[name] = (out[name] * factor).astype(out[name].dtype)
    return out
```

```python
import math
from contextlib import ExitStack

import concourse.bass as bass
import concourse.mybir as mybir
import numpy as np

F32 = mybir.dt.float32
F32R = mybir.dt.float32r
ACT = mybir.ActivationFunctionType
ALU = mybir.AluOpType
AX = mybir.AxisListType

P = 128
D_MODEL, SEQ, MEM, D_FF = 1024, 512, 256, 2816
KD = D_MODEL // P
NB = SEQ // P
MT = MEM // P
FT = D_FF // P
EPS = 1e-6
A_HEADS, A_KV, DH = 12, 2, 64
AJ = A_HEADS // A_KV
N_BUCKETS, MAX_DISTANCE, WINDOW = 32, 128, 128
X_HEADS = 4
QKH, VH, DK = 3, 6, 128
B_TAPS, F_TAPS = 4, 3
NQKV = 2 * QKH + VH
LEVELS = 7
BIG = 1e30

RAW = 4
CUT = 2
DOWN_K = [6, 6, 5, 5]
DOWN_AT = [sum(DOWN_K[:i]) for i in range(4)]

_widths = [("mix_g", 2 * KD), ("mem_g", 2 * KD), ("ffn_g", 2 * KD), ("fin_g", KD),
           ("conv_b", B_TAPS * NQKV), ("conv_f", 2 * F_TAPS * FT), ("bias_f", 2 * FT), ("out_g", 1),
           ("sinks", A_HEADS), ("dt_bias", VH), ("a_log", VH)]
COL = {}
_at = 0
for _name, _w in _widths:
    COL[_name] = _at
    _at += _w
NPAR = _at

IDENT, ONES, TRI, CAUSAL, FLIP, LEVEL0 = range(6)
NCONST = LEVEL0 + LEVELS
BIAS_PAD = 384

STREAM = [("mem0", 4), ("mem1", 4), ("in0", 10), ("out0", KD), ("gu0", 2 * FT), ("dn0", 4 * KD),
          ("in1", 20), ("out1", KD), ("gu1", 2 * FT), ("dn1", 4 * KD)]
SLAB0, TILE0 = {}, {}
_n = _g = 0
for _name, _c in STREAM:
    SLAB0[_name], TILE0[_name] = _n, _g
    _n += _c
    _g += _c // 4 if _name[:2] == "dn" else _c
SLABS = _n


def slab_k(n):
    for name, count in STREAM:
        if SLAB0[name] <= n < SLAB0[name] + count:
            return DOWN_K[(n - SLAB0[name]) % 4] if name[:2] == "dn" else KD
    raise ValueError(n)


def program(nc, xT, memT, params, consts, rel_bias, onehot, w_mem, w_in_a, w_in_b, w_ba, w_out, w_gu,
            w_dn, outT):
    ctx = ExitStack()
    with ctx:
        def sb(name, shape, dt=F32, at=None):
            return (at or ctx).enter_context(nc.sbuf_tensor(name, shape, dt))

        def psum(name):
            return ctx.enter_context(nc.psum_tensor(name, [P, 512], F32))

        def sem(name):
            return ctx.enter_context(nc.semaphore(name))

        h = sb("h", [P, KD, SEQ])
        with ExitStack() as at:
            (decay, grow, qdec, amat, tmat, umat, zneg, attn, attn_t, vbeta) = (
                sb(x, [P, VH, P], at=at) for x in (
                    "decay", "grow", "qdec", "amat", "tmat", "umat", "zneg", "attn", "attn_t", "vbeta"))
        with ExitStack() as at:
            s1 = sb("s1", [P, 3, 4, 2 * P], at=at)
            pt1 = sb("pt1", [P, 2, 2, 4, P], at=at)
            small1 = sb("small1", [P, 3, 6, 4], at=at)
        xh = sb("xh", [P, KD, SEQ], F32R)
        xl = sb("xl", [P, KD, SEQ], F32R)
        sq = sb("sq", [P, SEQ])
        rms = sq
        ssq = sb("ssq", [P, SEQ])
        rinv = sb("rinv", [P, SEQ])
        raw = sb("raw", [P, RAW, KD * P])
        wh = sb("wh", [P, CUT, KD * P], F32R)
        wl = sb("wl", [P, CUT, KD * P], F32R)
        wba = sb("wba", [P, KD, 2 * VH])
        wbah = sb("wbah", [P, KD, 2 * VH], F32R)
        wbal = sb("wbal", [P, KD, 2 * VH], F32R)
        par = sb("par", [P, NPAR])
        con = sb("con", [P, NCONST, P])
        eps = sb("eps", [P, 1])
        mem_k = sb("mem_k", [P, 2, MT, MEM])
        mem_v = sb("mem_v", [P, 2, MT, 2 * P])
        ident, ones = con[:, IDENT, :], con[:, ONES, :]

        def col(name, i=0, n=1):
            a = COL[name] + i
            return par[:, a:a + n] if isinstance(a, int) else par[:, bass.ts(a, 1)]

        with ExitStack() as at:
            mT = sb("mT", [P, KD, MEM], at=at)
            m_sq = sb("m_sq", [P, KD, MEM], at=at)
            m_ss = sb("m_ss", [P, MEM], at=at)
            m_rms = sb("m_rms", [P, MEM], at=at)
            mn = sb("mn", [P, 2, KD, MEM], at=at)
            mh = sb("mh", [P, 2, KD, MEM], F32R, at=at)
            ml = sb("ml", [P, 2, KD, MEM], F32R, at=at)
            relb = sb("relb", [N_BUCKETS, A_HEADS], at=at)
            oneh = sb("oneh", [N_BUCKETS, WINDOW], at=at)
            brow = sb("brow", [A_HEADS, BIAS_PAD], at=at)
            bias_rev = sb("bias_rev", [P, A_HEADS, 2 * P], at=at)
        with ExitStack() as at:
            ch0 = sb("ch0", [P, KD, SEQ], F32R, at=at)
            cl0 = sb("cl0", [P, KD, SEQ], F32R, at=at)
            pa = sb("pa", [P, 10, SEQ], at=at)
            vtok = sb("vtok", [P, NB, P], at=at)
            s0 = sb("s0", [P, 3, 4, 2 * P], at=at)
            pt0 = sb("pt0", [P, 2, 2, 4, P], at=at)
            small0 = sb("small0", [P, 3, 6, 4], at=at)
            sb("under_bias_rev", [P, 3 * P * 2 * 3 + 1024], at=at)
            bias = sb("bias", [P, A_HEADS, 2 * P], at=at)
        with ExitStack() as at:
            ah = sb("ah", [P, FT, SEQ], F32R, at=at)
            al = sb("al", [P, FT, SEQ], F32R, at=at)
            graw = sb("graw", [P, 2, SEQ + 2], at=at)
            gacc = sb("gacc", [P, 2, SEQ], at=at)
            gsil = sb("gsil", [P, 2, SEQ], at=at)
            gup = sb("gup", [P, 2, SEQ], at=at)
        with ExitStack() as at:
            ch1 = sb("ch1", [P, KD, SEQ], F32R, at=at)
            cl1 = sb("cl1", [P, KD, SEQ], F32R, at=at)
            zt = sb("zt", [P, 8, SEQ], at=at)
            qkv = sb("qkv", [P, NQKV, SEQ], at=at)
            with ExitStack() as early:
                craw = sb("craw", [P, 2, SEQ + 3], at=early)
                cacc = sb("cacc", [P, 2, SEQ], at=early)
            gate = sb("gate", [P, 12, NB, VH], at=at)
            tail = sb("tail", [P, 2, VH], at=at)
            ba = sb("ba", [P, NB, 2 * VH], at=at)
            rtok = sb("rtok", [P, 2, NB], at=at)
            state, ktail, delta = (sb(x, [P, VH, P], at=at) for x in ("state", "ktail", "delta"))
            am = sb("am", [P, 2, VH, P], at=at)
        concat = {0: (ch0, cl0), 1: (ch1, cl1)}
        softmax_bufs = {0: (s0, pt0, small0), 1: (s1, pt1, small1)}
        MAXI, NEG, TOTAL, INV, SINK_D, SINK_E = range(6)
        LOGIT, ABS, EXP_ABS, EXP_B, EXP_A, LN, BETA, SOFT, NEG_G, GC, EXP_GC, NBE = range(12)

        banks = [psum(f"bank{i}") for i in range(8)]
        gemm_out = banks[0:2]
        score_banks = [banks[2:4], banks[0:2]]
        turned = banks[4:6]
        mixed = banks[6:8]
        stats = banks[7]

        par_in, x_in, mem_in, rel_in, ba_in = (sem(x) for x in ("par_in", "x_in", "mem_in", "rel_in", "ba_in"))
        w_in = [sem(f"w_in{i}") for i in range(RAW)]
        hi_cut, lo_cut = sem("hi_cut"), sem("lo_cut")
        slab_done = sem("slab_done")
        tile_out = sem("tile_out")
        sq_ready, sq_summed = sem("sq_ready"), sem("sq_summed")
        x_hi, x_lo = sem("x_hi"), sem("x_lo")
        stat_sum, stat_root, r_ready = sem("stat_sum"), sem("stat_root"), sem("r_ready")
        mem_sq, mem_sum, mem_stat, mem_root = (sem(x) for x in ("mem_sq", "mem_sum", "mem_stat", "mem_root"))
        mem_norm, mem_hi, mem_lo = sem("mem_norm"), sem("mem_hi"), sem("mem_lo")
        bias_mm, bias_row, bias_out, bias_in = (sem(x) for x in ("bias_mm", "bias_row", "bias_out", "bias_in"))
        bias_set = sem("bias_set")
        eps_set, v_turned, v_tok = sem("eps_set"), sem("v_turned"), sem("v_tok")
        sc_ready, max_ready, p_ready, pn_ready = (sem(x) for x in ("sc_ready", "max_ready", "p_ready", "pn_ready"))
        tp_ready, pt_ready, ov_ready = sem("tp_ready"), sem("pt_ready"), sem("ov_ready")
        c_hi, c_lo = sem("c_hi"), sem("c_lo")
        tap0, conv_ready, silu_ready = sem("tap0"), sem("conv_ready"), sem("silu_ready")
        a_ready, a_hi, a_lo = sem("a_ready"), sem("a_hi"), sem("a_lo")
        ba_hi, ba_lo = sem("ba_hi"), sem("ba_lo")
        d_pe, d_act, d_dve, d_pool = sem("d_pe"), sem("d_act"), sem("d_dve"), sem("d_pool")
        v_step, tap_step = sem("v_step"), sem("tap_step")
        out_ready, out_sent = sem("out_ready"), sem("out_sent")
        bias_rows = nc.dram_tensor("bias_rows", [A_HEADS, BIAS_PAD], F32, kind="Internal").ap()

        def gain(e, m):
            name = ("mix_g", "ffn_g", "mix_g", "ffn_g", "fin_g")[e]
            return col(name, m + (0 if e == 4 else (e // 2) * KD))

        def row(t, m):
            return t[:, m, :] if isinstance(m, int) else t[:, bass.ts(m, 1), :].rearrange("p a t -> p (a t)")

        groups = {0: [("self", b, jp) for b in range(NB) for jp in range(AJ // 2)]
                  + [("cross", b, None) for b in range(NB)],
                  1: [("cross", b, None) for b in range(NB)]}
        GROUP0 = {0: 0, 1: len(groups[0])}
        CONV0 = {"gu0": 0, "in1": FT, "gu1": FT + NQKV}

        L2 = range(2 * QKH)
        LV = range(1, LEVELS)
        HALF = range(2)
        ORDER = {
            "pe": (d_pe, ["ba"] + [f"l2 {j}" for j in L2] + ["cumsum"],
                   ["negcum", "kk", "qk", "k turned", "v turned", "attn turned", "T turned"]
                   + [f"{s} {lv} {hf}" for lv in LV for s in ("Z", "TU") for hf in HALF]
                   + ["kS", "delta", "out", "state", "norm"]),
            "act": (d_act, ["silu z", "ba root"] + [f"l2 square {j}" for j in L2]
                    + [f"l2 root {j}" for j in L2] + ["gate abs", "gate exp", "gate ln", "exp cumsum"],
                    ["decay", "grow", "tail", "ktail", "attnT", "U0"]
                    + [f"Z {lv} {hf}" for lv in LV for hf in HALF] + ["delta", "square", "root", "hi"]),
            "dve": (d_dve, ["ba scaled"] + [f"l2 {j}" for j in L2]
                    + ["gate in", "beta", "g", "cumsum", "nbe"],
                    ["NG", "log decay", "tail", "A", "attn", "vbeta", "T0"]
                    + [f"TU {lv} {hf}" for lv in LV for hf in HALF] + ["R", "state", "r", "out", "gated", "lo"]),
            "pool": (d_pool, [], ["qdec"] + [f"AM {lv}" for lv in LV]),
        }
        SKIPPED = [("pe", "kS", 0), ("dve", "R", 0), ("pe", "state", NB - 1), ("dve", "state", NB - 1)]
        told = dict.fromkeys(ORDER, 0)

        def number(who, name, c):
            _, pre, chunk = ORDER[who]
            if c is None:
                return pre.index(name)
            n = c * len(chunk) + chunk.index(name)
            return len(pre) + n - sum(w == who and k * len(chunk) + chunk.index(x) < n for w, x, k in SKIPPED)

        def step(who, name, c, ins):
            assert told[who] == number(who, name, c), (who, name, c)
            told[who] += 1
            ins.then_inc(ORDER[who][0], 1)

        def after(eng, who, name, c=None):
            eng.wait_ge(ORDER[who][0], number(who, name, c) + 1)

        def slab_steps(eng, name, cut, post, take=lambda j, i: None):
            n0, count = SLAB0[name], dict(STREAM)[name]
            per = 8 if name[:2] == "dn" else 4
            trips = count // per

            def trip(i, last):
                for j in range(per):
                    take(j, i)
                    if not last:
                        cut(n0 + j + CUT, per * i)
                    elif n0 + per * i + j + CUT < SLABS:
                        cut(n0 + per * i + j + CUT)
                    post(j, i)
            if count % per == 0:
                with eng.Fori(0, trips - 1) as i:
                    trip(i, False)
                trip(trips - 1, True)
            else:
                with eng.Fori(0, trips) as i:
                    trip(i, False)
                for k in range(per * trips, count):
                    take(k, 0)
                    cut(n0 + k + CUT)
                    post(k, 0)

        block = ctx.enter_context(nc.Block())

        @block.sync
        def _(sp):
            def load_slab(n, src, it=0):
                if n >= RAW:
                    sp.wait_ge(lo_cut, n - RAW + 1 + 4 * it)
                sp.dma_start(raw[:, n % RAW, :slab_k(n) * P], src).then_inc(w_in[n % RAW], 16)

            def stream(name, src):
                count = dict(STREAM)[name]
                if count > 4:
                    with sp.Fori(0, count // 4) as i:
                        at = [sp.snap(4 * i + j) for j in range(4)]
                        for j in range(4):
                            load_slab(SLAB0[name] + j, src(at[j]), i)
                for k in range(count - count % 4 if count > 4 else 0, count):
                    load_slab(SLAB0[name] + k, src(k))

            def stream_down(layer):
                with sp.Fori(0, KD) as i:
                    for j in range(4):
                        a = DOWN_AT[j] * P
                        load_slab(SLAB0[f"dn{layer}"] + j, w_dn[layer, i, :, a:a + DOWN_K[j] * P], i)

            sp.dma_start(mT[:], memT).then_inc(mem_in, 16)
            sp.dma_start(con[:], consts).then_inc(par_in, 16)
            sp.dma_start(par[:], params).then_inc(par_in, 16)
            stream("mem0", lambda k: w_mem[0, k])
            sp.dma_start(h[:], xT).then_inc(x_in, 16)
            sp.dma_start(relb[:], rel_bias).then_inc(rel_in, 16)
            sp.dma_start(oneh[:], onehot).then_inc(rel_in, 16)
            sp.dma_start(wba[:], w_ba).then_inc(ba_in, 16)
            stream("mem1", lambda k: w_mem[1, k])
            stream("in0", lambda k: w_in_a[k])
            stream("out0", lambda k: w_out[0, k])
            stream("gu0", lambda k: w_gu[0, k])
            stream_down(0)
            stream("in1", lambda k: w_in_b[k])
            stream("out1", lambda k: w_out[1, k])
            stream("gu1", lambda k: w_gu[1, k])
            stream_down(1)
            for m in range(KD):
                sp.wait_ge(out_ready, m + 1)
                sp.dma_start(outT[:, m, :], h[:, m, :]).then_inc(out_sent, 16)
            sp.wait_ge(out_sent, 16 * KD)

        @block.gpsimd
        def _(pool):
            pool.wait_ge(bias_row, 1)
            pool.dma_start(bias_rows, brow[:]).then_inc(bias_out, 16)
            pool.wait_ge(bias_out, 16)
            for s in range(A_HEADS):
                rows = bass.AP(bias_rows.tensor, s * BIAS_PAD, [[1, P], [1, 2 * P]])
                pool.dma_start(bias_rev[:, s, :], rows).then_inc(bias_in, 16)

            for c in range(NB):
                t = slice(c * P, (c + 1) * P)
                after(pool, "act", "grow", c)
                if c == 0:
                    after(pool, "dve", f"l2 {QKH - 1}")
                else:
                    after(pool, "pe", "out", c - 1)
                for j in range(QKH):
                    q = qkv[:, j, t].unsqueeze(1).to_broadcast([P, 2, P])
                    ins = pool.tensor_tensor(qdec[:, 2 * j:2 * j + 2, :], q, grow[:, 2 * j:2 * j + 2, :],
                                             ALU.mult)
                step("pool", "qdec", c, ins)
                after(pool, "dve", "A", c)
                after(pool, "pe", "negcum", c)
                for lv in LV:
                    if lv > 2:
                        after(pool, "pe", f"Z {lv - 2} 1", c)
                    m = con[:, LEVEL0 + lv, :].unsqueeze(1).to_broadcast([P, VH, P])
                    step("pool", f"AM {lv}", c, pool.tensor_tensor(am[:, lv % 2], amat[:], m, ALU.mult))

        @block.scalar
        def _(act):
            def cut_hi(n, more=0):
                act.wait_ge(w_in[n % RAW], 16 * (n // RAW + 1) + (16 // RAW) * more)
                if n >= CUT:
                    act.wait_ge(slab_done, n - CUT + 1 + more)
                w = slab_k(n) * P
                act.activation(wh[:, n % CUT, :w], raw[:, n % RAW, :w], ACT.Copy).then_inc(hi_cut, 1)

            def square_and_hi(e, m):
                if not (e == 0 and isinstance(m, int) and m == 0):
                    act.wait_ge(sq_summed, KD * e + m)
                act.activation(sq[:], row(h, m), ACT.Square).then_inc(sq_ready, 1)
                if e < 4:
                    act.activation(row(xh, m), row(h, m), ACT.Copy, scale=gain(e, m)).then_inc(x_hi, 1)

            def root(e):
                act.wait_ge(stat_sum, e + 1)
                act.activation(rms[:], stats[:], ACT.Sqrt, bias=eps[:], scale=1.0 / D_MODEL)\
                   .then_inc(stat_root, 1)

            def residual(name, e):
                g0 = TILE0[name]

                def post(j, i):
                    if name[:2] == "dn":
                        if j % 4 == 3:
                            act.wait_ge(tile_out, g0 + j // 4 + 1 + 2 * i)
                            square_and_hi(e, 2 * i + j // 4)
                    else:
                        act.wait_ge(tile_out, g0 + j + 1 + 4 * i)
                        square_and_hi(e, 4 * i + j)
                slab_steps(act, name, cut_hi, post)

            def attention(layer):
                s, pt, small = softmax_bufs[layer]
                ch = concat[layer][0]
                n, g0 = len(groups[layer]), GROUP0[layer]
                for t in range(n + 3):
                    if 2 <= t < n + 2:
                        u = t - 2
                        kind, b, _ = groups[layer][u]
                        act.wait_ge(tp_ready, g0 + u + 1)
                        if u >= 2:
                            act.wait_ge(ov_ready, g0 + u - 1)
                        for kc in range(1 if kind == "self" and b == 0 else 0, 2):
                            ins = act.activation(pt[:, u % 2, kc].rearrange("p a q -> p (a q)"),
                                                 turned[kc][:], ACT.Copy)
                        ins.then_inc(pt_ready, 1)
                    if t < n:
                        kind, b, jp = groups[layer][t]
                        lo = P if kind == "self" and b == 0 else 0
                        sm = small[:, t % 3]
                        act.wait_ge(max_ready, g0 + t + 1)
                        if kind == "self":
                            act.activation(sm[:, SINK_E, :], sm[:, SINK_D, :], ACT.Exp)
                        for i in range(4):
                            src = s[:, t % 3, i, lo:] if kind == "self" else \
                                score_banks[t % 2][i // 2][:, (i % 2) * 256:(i % 2) * 256 + 256]
                            ins = act.activation(s[:, t % 3, i, lo:], src, ACT.Exp, bias=sm[:, NEG, i:i + 1],
                                                 accum_out=sm[:, TOTAL, i:i + 1])
                        ins.then_inc(p_ready, 1)
                    if t >= 3:
                        u = t - 3
                        kind, b, jp = groups[layer][u]
                        first = 2 * jp if kind == "self" else 6
                        act.wait_ge(ov_ready, g0 + u + 1)
                        act.activation(ch[:, first:first + 2, b * P:(b + 1) * P],
                                       mixed[u % 2][:, 0:2 * P].rearrange("p (a q) -> p a q", a=2),
                                       ACT.Copy).then_inc(c_hi, 1)

            def mixer(layer):
                name = f"gu{layer}"
                g0, f0 = TILE0[name], layer * FT

                def post(j, i):
                    q, f = j // 2, 2 * i + j // 2
                    if j % 2 == 0:
                        act.wait_ge(tile_out, g0 + j + 1 + 4 * i)
                        act.activation(gacc[:, q, :], graw[:, q, 0:SEQ], ACT.Identity,
                                       bias=col("bias_f", f + f0),
                                       scale=col("conv_f", f + layer * F_TAPS * FT)).then_inc(tap0, 1)
                        act.wait_ge(conv_ready, CONV0[name] + q + 1 + 2 * i)
                        act.activation(gsil[:, q, :], gacc[:, q, :], ACT.Silu).then_inc(silu_ready, 1)
                    else:
                        act.wait_ge(a_ready, f0 + q + 1 + 2 * i)
                        act.activation(row(ah, f), gup[:, q, :], ACT.Copy).then_inc(a_hi, 1)
                slab_steps(act, name, cut_hi, post)

            def deltanet():
                squares, roots = (decay, grow, qdec, amat, tmat, umat), (attn, zneg, attn_t, vbeta, ktail, delta)
                flat = lambda t: t[:].rearrange("p a t -> p (a t)")[:, 0:SEQ]
                for j in L2:
                    step("act", f"l2 square {j}", None, act.activation(flat(squares[j]), qkv[:, j, :], ACT.Square))
                for j in L2:
                    after(act, "pe", f"l2 {j}")
                    step("act", f"l2 root {j}", None, act.activation(flat(roots[j]), banks[j][:], ACT.Sqrt, bias=eps[:]))
                after(act, "dve", "gate in")
                step("act", "gate abs", None, act.activation(gate[:, ABS], gate[:, LOGIT], ACT.Abs))
                after(act, "act", "gate abs")
                act.activation(gate[:, EXP_ABS], gate[:, ABS], ACT.Exp, scale=-1.0)
                act.activation(gate[:, EXP_A, 0, :], col("a_log", 0, VH), ACT.Exp)
                step("act", "gate exp", None, act.activation(gate[:, EXP_B], ba[:, :, 0:VH], ACT.Exp, scale=-1.0))
                after(act, "act", "gate exp")
                step("act", "gate ln", None, act.activation(gate[:, LN], gate[:, EXP_ABS], ACT.Ln, bias=ones[:, 0:1]))
                after(act, "dve", "cumsum")
                step("act", "exp cumsum", None, act.activation(gate[:, EXP_GC], gate[:, GC], ACT.Exp))
                for c in range(NB):
                    t = slice(c * P, (c + 1) * P)
                    after(act, "dve", "log decay", c)
                    step("act", "decay", c, act.activation(decay[:], decay[:], ACT.Exp))
                    after(act, "dve", "tail", c)
                    for hf in HALF:
                        ins = act.activation(grow[:, 3 * hf:3 * hf + 3, :].rearrange("p a t -> p (a t)"),
                                             banks[hf][:, 0:3 * P], ACT.Exp, scale=-1.0)
                    step("act", "grow", c, ins)
                    step("act", "tail", c, act.activation(tail[:, 1, :], tail[:, 0, :], ACT.Exp, scale=-1.0))
                    after(act, "act", "tail", c)
                    after(act, "pe", "k turned", c)
                    for v in range(VH):
                        ins = act.activation(ktail[:, v, :], banks[4][:, (v // 2) * P:(v // 2 + 1) * P],
                                             ACT.Copy, scale=tail[:, 1, v:v + 1])
                    step("act", "ktail", c, ins)
                    after(act, "pe", "attn turned", c)
                    for hf in HALF:
                        ins = act.activation(attn_t[:, 3 * hf:3 * hf + 3, :].rearrange("p a t -> p (a t)"),
                                             banks[hf][:, 0:3 * P], ACT.Copy)
                    step("act", "attnT", c, ins)
                    after(act, "pe", "T turned", c)
                    for hf in HALF:
                        ins = act.activation(umat[:, 3 * hf:3 * hf + 3, :].rearrange("p a t -> p (a t)"),
                                             banks[2 + hf][:, 0:3 * P], ACT.Copy)
                    step("act", "U0", c, ins)
                    for lv in LV:
                        for hf in HALF:
                            after(act, "pe", f"Z {lv} {hf}", c)
                            step("act", f"Z {lv} {hf}", c, act.activation(
                                zneg[:, 3 * hf:3 * hf + 3, :].rearrange("p a t -> p (a t)"),
                                banks[4 + hf][:, 0:3 * P], ACT.Copy, scale=-1.0))
                    after(act, "pe", "delta", c)
                    for hf in HALF:
                        ins = act.activation(delta[:, 3 * hf:3 * hf + 3, :].rearrange("p a t -> p (a t)"),
                                             banks[4 + hf][:, 0:3 * P], ACT.Copy)
                    step("act", "delta", c, ins)
                    after(act, "pe", "out", c)
                    for hf in HALF:
                        ins = act.activation(zneg[:, 3 * hf:3 * hf + 3, :].rearrange("p a t -> p (a t)"),
                                             banks[hf][:, 0:3 * P], ACT.Square)
                    step("act", "square", c, ins)
                    after(act, "pe", "norm", c)
                    for hf in HALF:
                        ins = act.activation(attn[:, 3 * hf:3 * hf + 3, :].rearrange("p a t -> p (a t)"),
                                             banks[6 + hf][:, 0:3 * P], ACT.Sqrt, bias=eps[:], scale=1.0 / DK)
                    step("act", "root", c, ins)
                    after(act, "dve", "gated", c)
                    step("act", "hi", c, act.activation(ch1[:, 0:VH, t], amat[:], ACT.Copy))

            act.wait_ge(mem_in, 16)
            act.activation(m_sq[:], mT[:], ACT.Square).then_inc(mem_sq, 1)
            cut_hi(0)
            cut_hi(1)
            act.wait_ge(mem_stat, 1)
            act.wait_ge(eps_set, 1)
            act.activation(m_rms[:], stats[:, 0:MEM], ACT.Sqrt, bias=eps[:], scale=1.0 / D_MODEL)\
               .then_inc(mem_root, 1)
            for layer in range(2):
                act.wait_ge(mem_norm, layer + 1)
                act.activation(mh[:, layer], mn[:, layer], ACT.Copy).then_inc(mem_hi, 1)
            act.wait_ge(x_in, 16)
            act.wait_ge(par_in, 32)
            for k in range(KD):
                cut_hi(k + CUT)
                square_and_hi(0, k)
            root(0)
            slab_steps(act, "in0", cut_hi, lambda j, i: None)
            attention(0)
            residual("out0", 1)
            root(1)
            mixer(0)
            residual("dn0", 2)
            root(2)

            def conv_post(k, i):
                act.wait_ge(tile_out, TILE0["in1"] + k + 1 + 4 * i)
                act.activation(cacc[:, k % 2, :], craw[:, k % 2, 0:SEQ], ACT.Copy,
                               scale=col("conv_b", 4 * i + k)).then_inc(tap0, 1)
                act.wait_ge(conv_ready, CONV0["in1"] + k + 1 + 4 * i)
                act.activation(row(qkv, 4 * i + k), cacc[:, k % 2, :], ACT.Silu).then_inc(silu_ready, 1)
            n0 = SLAB0["in1"]
            with act.Fori(0, NQKV // 4) as i:
                for j in range(4):
                    cut_hi(n0 + j + CUT, 4 * i)
                    conv_post(j, i)
            for k in range(NQKV, 20):
                cut_hi(n0 + k + CUT)
            act.wait_ge(ba_in, 16)
            act.activation(wbah[:], wba[:], ACT.Copy).then_inc(ba_hi, 1)
            act.wait_ge(tile_out, TILE0["out1"])
            step("act", "silu z", None, act.activation(zt[:, 0:VH, :], zt[:, 0:VH, :], ACT.Silu))
            after(act, "pe", "ba")
            step("act", "ba root", None, act.activation(rtok[:, 0, :], stats[:, 64:64 + NB], ACT.Sqrt,
                                                        bias=eps[:], scale=1.0 / D_MODEL))
            attention(1)
            deltanet()
            residual("out1", 3)
            root(3)
            mixer(1)
            residual("dn1", 4)
            root(4)

        @block.vector
        def _(dve):
            steps = [0]

            def then_wait(ins):
                steps[0] += 1
                ins.then_inc(v_step, 1)
                dve.wait_ge(v_step, steps[0])

            def cut_lo(n, more=0):
                dve.wait_ge(hi_cut, n + 1 + more)
                w = slab_k(n) * P
                dve.tensor_tensor(wl[:, n % CUT, :w], raw[:, n % RAW, :w], wh[:, n % CUT, :w].bitcast(F32),
                                  ALU.subtract).then_inc(lo_cut, 1)

            def sum_and_lo(e, m):
                dve.wait_ge(sq_ready, KD * e + 1 + m)
                dve.tensor_tensor(ssq[:], ssq[:], sq[:], ALU.add).then_inc(sq_summed, 1)
                if e < 4:
                    dve.wait_ge(x_hi, KD * e + 1 + m)
                    dve.scalar_tensor_tensor(out=row(xl, m), in0=row(h, m), scalar=gain(e, m),
                                             in1=row(xh, m).bitcast(F32), op0=ALU.mult, op1=ALU.subtract)\
                       .then_inc(x_lo, 1)

            def inverse_rms(e):
                dve.wait_ge(stat_root, e + 1)
                dve.reciprocal(rinv[:], rms[:]).then_inc(r_ready, 1)
                dve.wait_ge(r_ready, e + 1)

            def residual(name, e):
                n0, g0 = SLAB0[name], TILE0[name]
                then_wait(dve.memset(ssq[:], 0.0))

                down = name[:2] == "dn"

                def which(j, i):
                    return (2 * i + j // 4, j // 4) if down else (4 * i + j, j)

                def add(j, i):
                    if down and j % 4 < 3:
                        return
                    m, tile = which(j, i)
                    dve.wait_ge(slab_done, n0 + j + 1 + (8 if down else 4) * i)
                    dve.tensor_tensor(row(h, m), gemm_out[(g0 + tile) % 2][:], row(h, m), ALU.add)\
                       .then_inc(tile_out, 1)

                def post(j, i):
                    if down and j % 4 < 3:
                        return
                    m, tile = which(j, i)
                    dve.wait_ge(tile_out, g0 + tile + 1 + (2 if down else 4) * i)
                    dve.wait_ge(sq_summed, KD * e + m)
                    sum_and_lo(e, m)
                slab_steps(dve, name, cut_lo, post, add)

            def take(name, k, i, out):
                dve.wait_ge(slab_done, SLAB0[name] + k + 1 + 4 * i)
                dve.tensor_tensor(out, gemm_out[(TILE0[name] + k) % 2][:], rinv[:], ALU.mult)\
                   .then_inc(tile_out, 1)

            def taps(name, raw_tile, acc, k, i, weight, count):
                c0 = CONV0[name]
                per = 2 if name[:2] == "gu" else 4
                dve.wait_ge(tap0, c0 + k + 1 + per * i)
                for tap in range(1, count):
                    ins = dve.scalar_tensor_tensor(out=acc, in0=raw_tile[:, tap:tap + SEQ], scalar=weight(tap),
                                                   in1=acc, op0=ALU.mult, op1=ALU.add)
                    if tap < count - 1:
                        ins.then_inc(tap_step, 1)
                        dve.wait_ge(tap_step, tap_steps[name] + (count - 2) * k + tap + (count - 2) * per * i)
                ins.then_inc(conv_ready, 1)

            tap_steps = {"gu0": 0, "in1": FT, "gu1": FT + 2 * NQKV}

            def attention(layer):
                s, pt, small = softmax_bufs[layer]
                ch, cl = concat[layer]
                n, g0 = len(groups[layer]), GROUP0[layer]
                for t in range(n + 3):
                    if t < n:
                        kind, b, jp = groups[layer][t]
                        lo = P if kind == "self" and b == 0 else 0
                        sm = small[:, t % 3]
                        dve.wait_ge(sc_ready, g0 + t + 1)
                        if t >= 3:
                            dve.wait_ge(tp_ready, g0 + t - 2)
                        if kind == "self":
                            for i in range(4):
                                slot = 2 * (2 * jp + i % 2) + i // 2
                                src = score_banks[t % 2][i // 2][:, (i % 2) * 256 + lo:(i % 2) * 256 + 256]
                                ins = dve.tensor_tensor_reduce(
                                    s[:, t % 3, i, lo:], src, bias[:, slot, lo:], 1.0, col("sinks", slot),
                                    ALU.add, ALU.max, sm[:, MAXI, i:i + 1])
                            then_wait(ins)
                            then_wait(dve.tensor_scalar(sm[:, NEG, :], sm[:, MAXI, :], -1.0, None, ALU.mult))
                            sinks = col("sinks", 4 * jp, 4).rearrange("p (j kv) -> p kv j", kv=2)
                            dve.tensor_tensor(sm[:, SINK_D, :].rearrange("p (kv j) -> p kv j", kv=2), sinks,
                                              sm[:, NEG, :].rearrange("p (kv j) -> p kv j", kv=2), ALU.add)\
                               .then_inc(max_ready, 1)
                        else:
                            for half in range(2):
                                ins = dve.tensor_reduce(
                                    sm[:, MAXI, 2 * half:2 * half + 2],
                                    score_banks[t % 2][half][:].rearrange("p (a k) -> p a k", a=2), AX.X, ALU.max)
                            then_wait(ins)
                            dve.tensor_scalar(sm[:, NEG, :], sm[:, MAXI, :], -1.0, None, ALU.mult)\
                               .then_inc(max_ready, 1)
                    if 1 <= t <= n:
                        kind, b, jp = groups[layer][t - 1]
                        lo = P if kind == "self" and b == 0 else 0
                        sm = small[:, (t - 1) % 3]
                        dve.wait_ge(p_ready, g0 + t)
                        total = TOTAL
                        if kind == "self":
                            then_wait(dve.tensor_tensor(sm[:, SINK_D, :], sm[:, TOTAL, :], sm[:, SINK_E, :], ALU.add))
                            total = SINK_D
                        then_wait(dve.reciprocal(sm[:, INV, :], sm[:, total, :]))
                        for i in range(4):
                            p = s[:, (t - 1) % 3, i, lo:]
                            ins = dve.tensor_scalar(p, p, sm[:, INV, i:i + 1], None, ALU.mult)
                        ins.then_inc(pn_ready, 1)
                    if t >= 3:
                        kind, b, jp = groups[layer][t - 3]
                        first = 2 * jp if kind == "self" else 6
                        q = slice(b * P, (b + 1) * P)
                        dve.wait_ge(c_hi, g0 + t - 2)
                        dve.tensor_tensor(cl[:, first:first + 2, q],
                                          mixed[(t - 3) % 2][:, 0:2 * P].rearrange("p (a q) -> p a q", a=2),
                                          ch[:, first:first + 2, q].bitcast(F32), ALU.subtract).then_inc(c_lo, 1)

            def mixer(layer):
                name = f"gu{layer}"
                f0 = layer * FT
                then_wait(dve.memset(graw[:, :, 0:F_TAPS - 1], 0.0))

                def take_tile(j, i):
                    take(name, j, i, graw[:, j // 2, F_TAPS - 1:] if j % 2 == 0 else gup[:, j // 2, :])

                def post(j, i):
                    q, f = j // 2, 2 * i + j // 2
                    if j % 2 == 0:
                        dve.wait_ge(tile_out, TILE0[name] + j + 1 + 4 * i)
                        taps(name, graw[:, q], gacc[:, q, :], q, i,
                             lambda tap: col("conv_f", f + (layer * F_TAPS + tap) * FT), F_TAPS)
                    else:
                        dve.wait_ge(tile_out, TILE0[name] + j + 1 + 4 * i)
                        dve.wait_ge(silu_ready, CONV0[name] + q + 1 + 2 * i)
                        dve.tensor_tensor(gup[:, q, :], gsil[:, q, :], gup[:, q, :], ALU.mult).then_inc(a_ready, 1)
                        dve.wait_ge(a_ready, f0 + q + 1 + 2 * i)
                        dve.wait_ge(a_hi, f0 + q + 1 + 2 * i)
                        dve.tensor_tensor(row(al, f), gup[:, q, :], row(ah, f).bitcast(F32), ALU.subtract)\
                           .then_inc(a_lo, 1)
                slab_steps(dve, name, cut_lo, post, take_tile)

            def deltanet():
                tokens = lambda t: t.unsqueeze(2).to_broadcast([P, NB, VH])
                roots = (attn, zneg, attn_t, vbeta, ktail, delta)
                for j in L2:
                    r = roots[j][:].rearrange("p a t -> p (a t)")[:, 0:SEQ]
                    after(dve, "act", f"l2 root {j}")
                    then_wait(dve.reciprocal(r, r))
                    if j < QKH:
                        ins = dve.scalar_tensor_tensor(out=qkv[:, j, :], in0=qkv[:, j, :], scalar=DK ** -0.5,
                                                       in1=r, op0=ALU.mult, op1=ALU.mult)
                    else:
                        ins = dve.tensor_tensor(qkv[:, j, :], qkv[:, j, :], r, ALU.mult)
                    step("dve", f"l2 {j}", None, ins)
                dt = col("dt_bias", 0, VH).unsqueeze(1).to_broadcast([P, NB, VH])
                step("dve", "gate in", None, dve.tensor_tensor(gate[:, LOGIT], ba[:, :, VH:], dt, ALU.add))
                after(dve, "act", "gate exp")
                then_wait(dve.tensor_scalar(gate[:, BETA], gate[:, EXP_B], 1.0, None, ALU.add))
                step("dve", "beta", None, dve.reciprocal(gate[:, BETA], gate[:, BETA]))
                after(dve, "act", "gate ln")
                then_wait(dve.scalar_tensor_tensor(out=gate[:, SOFT], in0=gate[:, LOGIT], scalar=0.0,
                                                   in1=gate[:, LN], op0=ALU.max, op1=ALU.add))
                ea = gate[:, EXP_A, 0, :].unsqueeze(1).to_broadcast([P, NB, VH])
                step("dve", "g", None, dve.tensor_tensor(gate[:, NEG_G], gate[:, SOFT], ea, ALU.mult))
                after(dve, "pe", "cumsum")
                step("dve", "cumsum", None, dve.tensor_scalar(
                    gate[:, GC].rearrange("p c v -> p (c v)"), stats[:, 128:128 + NB * VH], -1.0, None, ALU.mult))
                after(dve, "act", "exp cumsum")
                step("dve", "nbe", None, dve.scalar_tensor_tensor(
                    out=gate[:, NBE], in0=gate[:, BETA], scalar=-1.0, in1=gate[:, EXP_GC], op0=ALU.mult, op1=ALU.mult))
                for c in range(NB):
                    t = slice(c * P, (c + 1) * P)
                    beta = gate[:, BETA, c, :].unsqueeze(2)

                    def third(bank, hf=0):
                        return bank[:, 0:3 * P].rearrange("p (a t) -> p a t", a=3)

                    def heads(hf):
                        return slice(3 * hf, 3 * hf + 3)
                    for v in range(VH):
                        ins = dve.tensor_scalar(am[:, 0, v, :], con[:, TRI, :], gate[:, NEG_G, c, v:v + 1], None, ALU.mult)
                    step("dve", "NG", c, ins)
                    after(dve, "pe", "negcum", c)
                    for v in range(VH):
                        ins = dve.scalar_tensor_tensor(
                            out=decay[:, v, :], in0=banks[v // 3][:, (v % 3) * P:(v % 3 + 1) * P],
                            scalar=gate[:, GC, c, v:v + 1], in1=con[:, CAUSAL, :], op0=ALU.add, op1=ALU.add)
                    step("dve", "log decay", c, ins)
                    for hf in HALF:
                        last = third(banks[hf])[:, :, P - 1]
                        ins = dve.tensor_tensor(tail[:, 0, heads(hf)], last, gate[:, GC, c, heads(hf)], ALU.add)
                    step("dve", "tail", c, ins)
                    after(dve, "act", "decay", c)
                    then_wait(dve.tensor_tensor(amat[:], decay[:], beta.to_broadcast([P, VH, P]), ALU.mult))
                    after(dve, "pe", "qk", c)
                    pair = lambda x: x[:].rearrange("p (j e) t -> p j e t", e=2)
                    both = lambda bank: third(bank).unsqueeze(2).to_broadcast([P, 3, 2, P])
                    ins = dve.tensor_tensor(pair(amat), both(banks[2]), pair(amat), ALU.mult)
                    step("dve", "A", c, ins)
                    step("dve", "attn", c, dve.tensor_tensor(pair(attn), both(banks[3]), pair(decay), ALU.mult))
                    after(dve, "pe", "v turned", c)
                    for hf in HALF:
                        ins = dve.tensor_tensor(vbeta[:, heads(hf), :], third(banks[5 + hf]),
                                                gate[:, BETA, c, heads(hf)].unsqueeze(2).to_broadcast([P, 3, P]), ALU.mult)
                    step("dve", "vbeta", c, ins)
                    after(dve, "dve", "A", c)
                    m0 = con[:, LEVEL0, :].unsqueeze(1).to_broadcast([P, VH, P])
                    idb = ident.unsqueeze(1).to_broadcast([P, VH, P])
                    then_wait(dve.tensor_tensor(tmat[:], amat[:], m0, ALU.mult))
                    step("dve", "T0", c, dve.tensor_tensor(tmat[:], idb, tmat[:], ALU.subtract))
                    for lv in LV:
                        for hf in HALF:
                            after(dve, "pe", f"TU {lv} {hf}", c)
                            ins = dve.tensor_tensor(umat[:, heads(hf), :], third(banks[hf]), umat[:, heads(hf), :], ALU.add)
                            if lv < LEVELS - 1:
                                ins = dve.tensor_tensor(tmat[:, heads(hf), :], third(banks[2 + hf]),
                                                        tmat[:, heads(hf), :], ALU.add)
                            step("dve", f"TU {lv} {hf}", c, ins)
                    if c:
                        after(dve, "pe", "kS", c)
                        for v in range(VH):
                            ins = dve.scalar_tensor_tensor(
                                out=vbeta[:, v, :], in0=banks[6 + v // 3][:, (v % 3) * P:(v % 3 + 1) * P],
                                scalar=gate[:, NBE, c, v:v + 1], in1=vbeta[:, v, :], op0=ALU.mult, op1=ALU.add)
                        step("dve", "R", c, ins)
                    if c < NB - 1:
                        after(dve, "pe", "state", c)
                        for v in range(VH):
                            ps = banks[2 + v // 3][:, (v % 3) * P:(v % 3 + 1) * P]
                            if c:
                                ins = dve.scalar_tensor_tensor(out=state[:, v, :], in0=state[:, v, :],
                                                               scalar=grow[:, v, P - 1:P], in1=ps,
                                                               op0=ALU.mult, op1=ALU.add)
                            else:
                                ins = dve.tensor_copy(state[:, v, :], ps)
                        step("dve", "state", c, ins)
                    after(dve, "act", "root", c)
                    step("dve", "r", c, dve.reciprocal(attn[:], attn[:]))
                    after(dve, "dve", "r", c)
                    for hf in HALF:
                        ins = dve.scalar_tensor_tensor(out=amat[:, heads(hf), :], in0=third(banks[hf]),
                                                       scalar=col("out_g"), in1=attn[:, heads(hf), :],
                                                       op0=ALU.mult, op1=ALU.mult)
                    step("dve", "out", c, ins)
                    after(dve, "dve", "out", c)
                    step("dve", "gated", c, dve.tensor_tensor(amat[:], amat[:], zt[:, 0:VH, t], ALU.mult))
                    after(dve, "act", "hi", c)
                    step("dve", "lo", c, dve.tensor_tensor(cl1[:, 0:VH, t], amat[:], ch1[:, 0:VH, t].bitcast(F32),
                                                           ALU.subtract))

            dve.memset(eps[:], EPS).then_inc(eps_set, 1)
            then_wait(dve.memset(brow[:], -BIG))
            dve.wait_ge(mem_sq, 1)
            then_wait(dve.tensor_tensor(m_ss[:], m_sq[:, 0, :], m_sq[:, 1, :], ALU.add))
            for k in range(2, KD):
                ins = dve.tensor_tensor(m_ss[:], m_ss[:], m_sq[:, k, :], ALU.add)
                then_wait(ins) if k < KD - 1 else ins.then_inc(mem_sum, 1)
            cut_lo(0)
            cut_lo(1)
            dve.wait_ge(mem_root, 1)
            dve.wait_ge(par_in, 32)
            then_wait(dve.reciprocal(m_rms[:], m_rms[:]))
            for layer in range(2):
                for k in range(KD):
                    ins = dve.scalar_tensor_tensor(out=mn[:, layer, k, :], in0=mT[:, k, :],
                                                   scalar=col("mem_g", layer * KD + k), in1=m_rms[:],
                                                   op0=ALU.mult, op1=ALU.mult)
                ins.then_inc(mem_norm, 1)
                dve.wait_ge(mem_norm, layer + 1)
                dve.wait_ge(mem_hi, layer + 1)
                dve.tensor_tensor(ml[:, layer], mn[:, layer], mh[:, layer].bitcast(F32), ALU.subtract)\
                   .then_inc(mem_lo, 1)
            dve.wait_ge(bias_mm, 1)
            dve.tensor_copy(brow[:, P:2 * P], mixed[0][0:A_HEADS, 0:WINDOW]).then_inc(bias_row, 1)
            then_wait(dve.memset(ssq[:], 0.0))
            dve.wait_ge(x_in, 16)
            for k in range(8):
                layer, part = k // 4, k % 4
                dve.wait_ge(slab_done, k + 1)
                bank = gemm_out[k % 2]
                if part < 2:
                    dve.tensor_scalar(mem_k[:, layer, part, :], bank[:, 0:MEM], DH ** -0.5, None, ALU.mult)\
                       .then_inc(tile_out, 1)
                else:
                    dve.tensor_copy(mem_v[:, layer, :, (part - 2) * P:(part - 1) * P],
                                    bank[:, 0:MT * P].rearrange("p (a d) -> p a d", a=MT)).then_inc(tile_out, 1)
                cut_lo(k + CUT)
                if k:
                    dve.wait_ge(sq_summed, k)
                sum_and_lo(0, k)
            dve.wait_ge(bias_out, 16)
            inverse_rms(0)
            slab_steps(dve, "in0", cut_lo, lambda j, i: None, lambda j, i: take(
                "in0", j, i, row(pa, 4 * i + j if j < 4 else j)))
            dve.wait_ge(tile_out, TILE0["out0"])
            then_wait(dve.tensor_scalar(pa[:, 0, :], pa[:, 0, :], DH ** -0.5, None, ALU.mult))
            dve.wait_ge(v_turned, 1)
            dve.tensor_copy(vtok[:].rearrange("p b d -> p (b d)"), turned[0][:]).then_inc(v_tok, 1)
            for n in range(6):
                dve.wait_ge(bias_mm, n + 2)
                dve.tensor_copy(bias[:, 2 * n:2 * n + 2, :].rearrange("p a k -> p (a k)"), banks[2 + n][:])\
                   .then_inc(bias_set, 1)
            dve.wait_ge(bias_set, 6)
            attention(0)
            residual("out0", 1)
            inverse_rms(1)
            mixer(0)
            residual("dn0", 2)
            inverse_rms(2)
            then_wait(dve.memset(craw[:, :, 0:B_TAPS - 1], 0.0))

            def conv_post(k, i):
                dve.wait_ge(tile_out, TILE0["in1"] + k + 1 + 4 * i)
                taps("in1", craw[:, k % 2], cacc[:, k % 2, :], k, i,
                     lambda tap: col("conv_b", 4 * i + (k + tap * NQKV)), B_TAPS)
            with dve.Fori(0, NQKV // 4) as i:
                for j in range(4):
                    take("in1", j, i, craw[:, j % 2, B_TAPS - 1:])
                    cut_lo(SLAB0["in1"] + j + CUT, 4 * i)
                    conv_post(j, i)
            for k in range(NQKV, 20):
                take("in1", k, 0, zt[:, k - NQKV, :])
                cut_lo(SLAB0["in1"] + k + CUT)
            dve.wait_ge(ba_hi, 1)
            dve.tensor_tensor(wbal[:], wba[:], wbah[:].bitcast(F32), ALU.subtract).then_inc(ba_lo, 1)
            after(dve, "act", "ba root")
            then_wait(dve.reciprocal(rtok[:, 1, :], rtok[:, 0, :]))
            for b in range(NB):
                ins = dve.tensor_scalar(ba[:, b, :], stats[:, 2 * VH * b:2 * VH * (b + 1)],
                                        rtok[:, 1, b:b + 1], None, ALU.mult)
            step("dve", "ba scaled", None, ins)
            attention(1)
            deltanet()
            residual("out1", 3)
            inverse_rms(3)
            mixer(1)
            residual("dn1", 4)
            inverse_rms(4)
            for m in range(KD):
                dve.scalar_tensor_tensor(out=h[:, m, :], in0=h[:, m, :], scalar=gain(4, m), in1=rinv[:],
                                         op0=ALU.mult, op1=ALU.mult).then_inc(out_ready, 1)

        @block.tensor
        def _(pe):
            def slab(n, more, out, moving, first=True, last=True, k0=0):
                pe.wait_ge(lo_cut, n + 1 + more)
                count = slab_k(n)
                for k in range(count):
                    w = slice(k * P, (k + 1) * P)
                    xhi, xlo = moving(k0 + k)
                    pe.matmul(out, wh[:, n % CUT, w], xhi, start=first and k == 0, stop=False)
                    pe.matmul(out, wh[:, n % CUT, w], xlo, start=False, stop=False)
                    ins = pe.matmul(out, wl[:, n % CUT, w], xhi, start=False, stop=last and k == count - 1)
                ins.then_inc(slab_done, 1)

            def of(hi, lo):
                return lambda k: (hi[:, k, :], lo[:, k, :])

            def products(name, moving):
                n0, g0, count = SLAB0[name], TILE0[name], dict(STREAM)[name]

                def one(j, i):
                    pe.wait_ge(tile_out, g0 + j - 1 + 4 * i)
                    slab(n0 + j, 4 * i, gemm_out[(g0 + j) % 2][:], moving)
                with pe.Fori(0, count // 4) as i:
                    for j in range(4):
                        one(j, i)
                for k in range(count - count % 4, count):
                    one(k, 0)

            def down(layer):
                n0, g0 = SLAB0[f"dn{layer}"], TILE0[f"dn{layer}"]
                pe.wait_ge(a_lo, FT * (layer + 1))
                with pe.Fori(0, KD // 2) as i:
                    for j in range(8):
                        if j % 4 == 0:
                            pe.wait_ge(tile_out, g0 + j // 4 - 1 + 2 * i)
                        slab(n0 + j, 8 * i, gemm_out[(g0 + j // 4) % 2][:], of(ah, al), first=j % 4 == 0,
                             last=j % 4 == 3, k0=DOWN_AT[j % 4])

            def norm(e):
                if e < 4:
                    pe.wait_ge(x_lo, KD * (e + 1))
                pe.wait_ge(sq_summed, KD * (e + 1))
                pe.matmul(stats[:], ones, ssq[:], start=True, stop=True).then_inc(stat_sum, 1)

            def attention(layer):
                s, pt, small = softmax_bufs[layer]
                n, g0 = len(groups[layer]), GROUP0[layer]
                queries = pa[:, 8:10] if layer == 0 else zt[:, 6:8]
                for t in range(n + 3):
                    if t < n:
                        kind, b, jp = groups[layer][t]
                        q = slice(b * P, (b + 1) * P)
                        if t >= 2:
                            used = max_ready if groups[layer][t - 2][0] == "self" else p_ready
                            pe.wait_ge(used, g0 + t - 1)
                        for i in range(4):
                            half, side = slice((i // 2) * DH, (i // 2 + 1) * DH), (i % 2) * 256
                            out = score_banks[t % 2][i // 2]
                            if kind == "self":
                                lo = P if b == 0 else 0
                                ins = pe.matmul(out[:, side + lo:side + 256], pa[half, 2 + 2 * jp + i % 2, q],
                                                pa[half, 0, (b - 1) * P + lo:(b + 1) * P], start=True, stop=True)
                            else:
                                ins = pe.matmul(out[:, side:side + 256], queries[half, i % 2, q],
                                                mem_k[half, layer, i % 2, :], start=True, stop=True)
                        ins.then_inc(sc_ready, 1)
                    if 2 <= t < n + 2:
                        u = t - 2
                        kind, b, jp = groups[layer][u]
                        pe.wait_ge(pn_ready, g0 + u + 1)
                        if u:
                            pe.wait_ge(pt_ready, g0 + u)
                        for kc in range(1 if kind == "self" and b == 0 else 0, 2):
                            for i in range(4):
                                ins = pe.transpose(turned[kc][:, i * P:(i + 1) * P],
                                                   s[:, u % 3, i, kc * P:(kc + 1) * P], ident)
                        ins.then_inc(tp_ready, 1)
                    if t >= 3:
                        u = t - 3
                        kind, b, jp = groups[layer][u]
                        pe.wait_ge(pt_ready, g0 + u + 1)
                        if u >= 2:
                            pe.wait_ge(c_lo, g0 + u - 1)
                        out, p = mixed[u % 2], pt[:, u % 2]
                        for half in range(2):
                            if kind == "self":
                                d = slice(half * DH, (half + 1) * DH)
                                parts = range(1 if b == 0 else 0, 2)
                                for kc in parts:
                                    ins = pe.matmul(out[d, 0:2 * P], vtok[:, b - 1 + kc, d],
                                                    p[:, kc, 2 * half:2 * half + 2, :].rearrange("p a q -> p (a q)"),
                                                    start=kc == parts[0], stop=kc == 1)
                                continue
                            for a in range(2):
                                hd = 2 * a + half
                                for kc in range(2):
                                    ins = pe.matmul(out[half * DH:(half + 1) * DH, a * P:(a + 1) * P],
                                                    mem_v[:, layer, kc, hd * DH:(hd + 1) * DH],
                                                    p[:, kc, 2 * half + a, :], start=kc == 0, stop=kc == 1)
                        ins.then_inc(ov_ready, 1)
                pe.wait_ge(c_lo, g0 + n)

            def gates():
                pe.wait_ge(ba_lo, 1)
                for b in range(NB):
                    t, o = slice(b * P, (b + 1) * P), stats[:, 2 * VH * b:2 * VH * (b + 1)]
                    for k in range(KD):
                        pe.matmul(o, xh[:, k, t], wbah[:, k, :], start=k == 0, stop=False)
                        pe.matmul(o, xl[:, k, t], wbah[:, k, :], start=False, stop=False)
                        pe.matmul(o, xh[:, k, t], wbal[:, k, :], start=False, stop=k == KD - 1)
                for b in range(NB):
                    ins = pe.matmul(stats[:, 64 + b:65 + b], ssq[:, b * P:(b + 1) * P], ones[:, 0:1],
                                    start=True, stop=True)
                step("pe", "ba", None, ins)

            def deltanet():
                squares = (decay, grow, qdec, amat, tmat, umat)
                for j in L2:
                    after(pe, "act", f"l2 square {j}")
                    step("pe", f"l2 {j}", None, pe.matmul(
                        banks[j][:], ones, squares[j][:].rearrange("p a t -> p (a t)")[:, 0:SEQ], start=True, stop=True))
                after(pe, "dve", "g")
                step("pe", "cumsum", None, pe.matmul(stats[:, 128:128 + NB * VH], con[:, TRI, :],
                                                     gate[:, NEG_G].rearrange("p c v -> p (c v)"), start=True, stop=True))
                for c in range(NB):
                    t = slice(c * P, (c + 1) * P)
                    tile = lambda bank, v: bank[:, v * P:(v + 1) * P]
                    after(pe, "dve", "NG", c)
                    if c:
                        after(pe, "dve", "out", c - 1)
                        after(pe, "dve", "state", c - 1)
                    for hf in HALF:
                        ins = pe.matmul(banks[hf][:, 0:3 * P], ones,
                                        am[:, 0, 3 * hf:3 * hf + 3, :].rearrange("p a t -> p (a t)"), start=True, stop=True)
                    step("pe", "negcum", c, ins)
                    after(pe, "dve", f"l2 {2 * QKH - 1}")
                    for j in range(QKH):
                        ins = pe.matmul(tile(banks[2], j), qkv[:, QKH + j, t], qkv[:, QKH + j, t], start=True, stop=True)
                    step("pe", "kk", c, ins)
                    for j in range(QKH):
                        ins = pe.matmul(tile(banks[3], j), qkv[:, j, t], qkv[:, QKH + j, t], start=True, stop=True)
                    step("pe", "qk", c, ins)
                    for j in range(QKH):
                        ins = pe.transpose(tile(banks[4], j), qkv[:, QKH + j, t], ident)
                    step("pe", "k turned", c, ins)
                    for v in range(VH):
                        ins = pe.transpose(tile(banks[5 + v // 3], v % 3), qkv[:, 2 * QKH + v, t], ident)
                    step("pe", "v turned", c, ins)
                    after(pe, "dve", "attn", c)
                    after(pe, "act", "grow", c)
                    for v in range(VH):
                        ins = pe.transpose(tile(banks[v // 3], v % 3), attn[:, v, :], ident)
                    step("pe", "attn turned", c, ins)
                    after(pe, "dve", "T0", c)
                    for v in range(VH):
                        ins = pe.transpose(tile(banks[2 + v // 3], v % 3), tmat[:, v, :], ident)
                    step("pe", "T turned", c, ins)
                    after(pe, "act", "U0", c)
                    for lv in LV:
                        for hf in HALF:
                            if hf == 0:
                                after(pe, "pool", f"AM {lv}", c)
                            if lv == 1:
                                after(pe, "dve", "vbeta", c)
                            else:
                                after(pe, "dve", f"TU {lv - 1} {hf}", c)
                            for v in range(3 * hf, 3 * hf + 3):
                                ins = pe.matmul(tile(banks[4 + hf], v % 3), am[:, lv % 2, v, :], umat[:, v, :],
                                                start=True, stop=True)
                            step("pe", f"Z {lv} {hf}", c, ins)
                        for hf in HALF:
                            after(pe, "act", f"Z {lv} {hf}", c)
                            for v in range(3 * hf, 3 * hf + 3):
                                ins = pe.matmul(tile(banks[hf], v % 3), tmat[:, v, :], zneg[:, v, :], start=True, stop=True)
                            if lv < LEVELS - 1:
                                for v in range(3 * hf, 3 * hf + 3):
                                    ins = pe.matmul(tile(banks[2 + hf], v % 3), zneg[:, v, :], tmat[:, v, :],
                                                    start=True, stop=True)
                            step("pe", f"TU {lv} {hf}", c, ins)
                    if c:
                        for v in range(VH):
                            ins = pe.matmul(tile(banks[6 + v // 3], v % 3), qkv[:, QKH + v // 2, t], state[:, v, :],
                                            start=True, stop=True)
                        step("pe", "kS", c, ins)
                    after(pe, "dve", f"TU {LEVELS - 1} 1", c)
                    if c:
                        after(pe, "dve", "R", c)
                    for v in range(VH):
                        ins = pe.matmul(tile(banks[4 + v // 3], v % 3), umat[:, v, :], vbeta[:, v, :], start=True, stop=True)
                    step("pe", "delta", c, ins)
                    after(pe, "pool", "qdec", c)
                    after(pe, "act", "delta", c)
                    for v in range(VH):
                        o = tile(banks[v // 3], v % 3)
                        if c:
                            pe.matmul(o, state[:, v, :], qdec[:, v, :], start=True, stop=False)
                        ins = pe.matmul(o, delta[:, v, :], attn_t[:, v, :], start=c == 0, stop=True)
                    step("pe", "out", c, ins)
                    if c < NB - 1:
                        for v in range(VH):
                            ins = pe.matmul(tile(banks[2 + v // 3], v % 3), ktail[:, v, :], delta[:, v, :], start=True, stop=True)
                        step("pe", "state", c, ins)
                    after(pe, "act", "square", c)
                    for hf in HALF:
                        ins = pe.matmul(banks[6 + hf][:, 0:3 * P], ones,
                                        zneg[:, 3 * hf:3 * hf + 3, :].rearrange("p a t -> p (a t)"), start=True, stop=True)
                    step("pe", "norm", c, ins)
                after(pe, "dve", "lo", NB - 1)

            pe.wait_ge(par_in, 32)
            pe.wait_ge(mem_sum, 1)
            pe.matmul(stats[:, 0:MEM], ones, m_ss[:], start=True, stop=True).then_inc(mem_stat, 1)
            pe.wait_ge(rel_in, 32)
            pe.matmul(mixed[0][0:A_HEADS, 0:WINDOW], relb[:], oneh[:], start=True, stop=True).then_inc(bias_mm, 1)
            for k in range(8):
                layer, part = k // 4, k % 4
                if part == 0:
                    pe.wait_ge(mem_lo, layer + 1)
                if k >= 2:
                    pe.wait_ge(tile_out, k - 1)
                bank = gemm_out[k % 2]
                if part < 2:
                    slab(k, 0, bank[:, 0:MEM], of(mh[:, layer], ml[:, layer]))
                    continue
                pe.wait_ge(lo_cut, k + 1)
                for mt in range(MT):
                    t, o = slice(mt * P, (mt + 1) * P), bank[:, mt * P:(mt + 1) * P]
                    for kk in range(KD):
                        w = slice(kk * P, (kk + 1) * P)
                        hi, lo = wh[:, k % CUT, w], wl[:, k % CUT, w]
                        pe.matmul(o, mh[:, layer, kk, t], hi, start=kk == 0, stop=False)
                        pe.matmul(o, mh[:, layer, kk, t], lo, start=False, stop=False)
                        ins = pe.matmul(o, ml[:, layer, kk, t], hi, start=False, stop=kk == KD - 1)
                ins.then_inc(slab_done, 1)
            norm(0)
            products("in0", of(xh, xl))
            pe.wait_ge(tile_out, TILE0["in0"] + 2)
            for b in range(NB):
                ins = pe.transpose(turned[0][:, b * P:(b + 1) * P], pa[:, 1, b * P:(b + 1) * P], ident)
            ins.then_inc(v_turned, 1)
            pe.wait_ge(tile_out, TILE0["out0"])
            pe.wait_ge(v_tok, 1)
            pe.wait_ge(bias_in, 16 * A_HEADS)
            for n in range(6):
                pe.matmul(banks[2 + n][:], con[:, FLIP, :],
                          bias_rev[:, 2 * n:2 * n + 2, :].rearrange("p a k -> p (a k)"), start=True, stop=True)\
                  .then_inc(bias_mm, 1)
            pe.wait_ge(bias_set, 6)
            attention(0)
            products("out0", of(ch0, cl0))
            norm(1)
            products("gu0", of(xh, xl))
            down(0)
            norm(2)
            products("in1", of(xh, xl))
            pe.wait_ge(tile_out, TILE0["out1"])
            gates()
            after(pe, "dve", "ba scaled")
            attention(1)
            deltanet()
            products("out1", of(ch1, cl1))
            norm(3)
            products("gu1", of(xh, xl))
            down(1)
            norm(4)


def head_order():
    return [kv * AJ + j for j in range(AJ) for kv in range(A_KV)]


def bucket_onehot():
    d = np.arange(WINDOW)
    half = N_BUCKETS // 2
    far = half + (np.log(np.maximum(d, 1).astype(np.float32) / np.float32(half))
                  / np.float32(math.log(MAX_DISTANCE / half)) * np.float32(N_BUCKETS - half)).astype(np.int32)
    bucket = np.where(d < half, d, np.minimum(far, N_BUCKETS - 1))
    out = np.zeros((N_BUCKETS, WINDOW), np.float32)
    out[bucket[::-1], d] = 1.0
    return out


def constant_tiles():
    t, s = np.arange(P)[:, None], np.arange(P)[None, :]
    out = np.zeros((NCONST, P, P), np.float32)
    out[IDENT] = t == s
    out[ONES] = 1.0
    out[FLIP] = t + s == P - 1
    out[TRI] = t <= s
    out[CAUSAL] = np.where(s <= t, 0.0, -BIG)
    for lv in range(LEVELS):
        b = 2 ** lv
        out[LEVEL0 + lv] = (t // b % 2 == 1) & (s // b == t // b - 1)
    return np.ascontiguousarray(out.transpose(1, 0, 2))


def slabs(w):
    *lead, k, c = w.shape
    w = w.reshape(*lead, k // P, P, c // P, P)
    n = len(lead)
    w = w.transpose(*range(n), n + 2, n + 1, n, n + 3)
    return np.ascontiguousarray(w.reshape(*lead, c // P, P, k))


def lay_out(x, mem, rel_bias, norm_mix_g, norm_mem_g, w_mem_kv, w_out, w_in_a, sinks_a, w_in_b,
            conv_qkv_b, a_log_b, dt_bias_b, out_norm_g_b, norm_ffn_g, w_gate_up, ffn_conv_w,
            ffn_conv_b, w_down, final_norm_g):
    order = head_order()
    feat = lambda a: np.moveaxis(a.reshape(*a.shape[:-1], a.shape[-1] // P, P), -1, 0).reshape(P, -1)
    rows = lambda a: np.broadcast_to(a.reshape(1, -1), (P, a.size))
    params = np.concatenate([
        feat(norm_mix_g), feat(norm_mem_g), feat(norm_ffn_g), feat(final_norm_g), feat(conv_qkv_b[0]),
        feat(ffn_conv_w), feat(ffn_conv_b), feat(out_norm_g_b[0]), rows(sinks_a[0][order]),
        rows(dt_bias_b[0]), rows(a_log_b[0])], axis=1)
    nq, nkv = A_HEADS * DH, A_KV * DH
    wa = w_in_a[0]
    q_cols = np.concatenate([np.arange(hd * DH, (hd + 1) * DH) for hd in order])
    wa = np.concatenate([wa[:, nq:nq + 2 * nkv], wa[:, q_cols], wa[:, nq + 2 * nkv:]], axis=1)
    w_o = np.stack([np.concatenate([w_out[0][q_cols], w_out[0][nq:]]), w_out[1]])
    nb = (NQKV + VH) * P
    wb = w_in_b[0]
    w_ba = wb[:, nb:nb + 2 * VH].reshape(KD, P, 2 * VH).transpose(1, 0, 2)
    wb = np.concatenate([wb[:, :nb], wb[:, nb + 2 * VH:]], axis=1)
    gu = slabs(w_gate_up)
    gu = np.stack([gu[:, :FT], gu[:, FT:]], axis=2).reshape(2, 2 * FT, P, D_MODEL)
    tiles = lambda a: a.T.reshape(KD, P, a.shape[0]).transpose(1, 0, 2)
    return {
        "xT": tiles(x[0]), "memT": tiles(mem[0]), "params": params, "consts": constant_tiles(),
        "rel_bias": rel_bias[:, order], "onehot": bucket_onehot(), "w_mem": slabs(w_mem_kv),
        "w_in_a": slabs(wa), "w_in_b": slabs(wb), "w_ba": w_ba, "w_out": slabs(w_o), "w_gu": gu,
        "w_dn": slabs(w_down),
    }


def kernel(**inputs):
    import concourse.bacc as bacc
    from concourse.bass_utils import run_bass_kernel_spmd

    nc = bacc.Bacc("TRN2", target_bir_lowering=False, num_devices=1)
    laid = lay_out(**{k: np.asarray(v) for k, v in inputs.items()})
    arrays = {name: np.ascontiguousarray(a) for name, a in laid.items()}
    args = [nc.dram_tensor(name, a.shape, mybir.dt.from_np(a.dtype), kind="ExternalInput").ap()
            for name, a in arrays.items()]
    args.append(nc.dram_tensor("outT", (P, KD, SEQ), F32, kind="ExternalOutput").ap())
    program(nc, *args)
    r = run_bass_kernel_spmd(nc, [arrays], core_ids=[0])
    out = r.results[0]["outT"].reshape(P, KD, SEQ).transpose(2, 1, 0).reshape(1, SEQ, D_MODEL)
    return np.ascontiguousarray(out)
```

```python
import math
from contextlib import ExitStack

import concourse.bass as bass
import concourse.mybir as mybir
import numpy as np

F32 = mybir.dt.float32
F32R = mybir.dt.float32r
ACT = mybir.ActivationFunctionType
ALU = mybir.AluOpType
AX = mybir.AxisListType

P = 128
D_MODEL, SEQ, MEM, D_FF = 1024, 512, 256, 2816
KD = D_MODEL // P
NB = SEQ // P
MT = MEM // P
FT = D_FF // P
EPS = 1e-6
A_HEADS, A_KV, DH = 12, 2, 64
AJ = A_HEADS // A_KV
N_BUCKETS, MAX_DISTANCE, WINDOW = 32, 128, 128
X_HEADS = 4
QKH, VH, DK = 3, 6, 128
B_TAPS, F_TAPS = 4, 3
NQKV = 2 * QKH + VH
LEVELS = 7
BIG = 1e30

RAW = 4
CUT = 2
DOWN_K = [6, 6, 5, 5]
DOWN_AT = [sum(DOWN_K[:i]) for i in range(4)]

_widths = [("mix_g", 2 * KD), ("mem_g", 2 * KD), ("ffn_g", 2 * KD), ("fin_g", KD),
           ("conv_b", B_TAPS * NQKV), ("conv_f", 2 * F_TAPS * FT), ("bias_f", 2 * FT), ("out_g", 1),
           ("sinks", A_HEADS), ("dt_bias", VH), ("a_log", VH)]
COL = {}
_at = 0
for _name, _w in _widths:
    COL[_name] = _at
    _at += _w
NPAR = _at

IDENT, ONES, TRI, CAUSAL, FLIP, LEVEL0 = range(6)
ABOVE = LEVEL0 + 1
NCONST = ABOVE + LEVELS // 2
BIAS_PAD = 384

STREAM = [("mem0", 4), ("mem1", 4), ("in0", 10), ("out0", KD), ("gu0", 2 * FT), ("dn0", 4 * KD),
          ("in1", 20), ("out1", KD), ("gu1", 2 * FT), ("dn1", 4 * KD)]
SLAB0, TILE0 = {}, {}
_n = _g = 0
for _name, _c in STREAM:
    SLAB0[_name], TILE0[_name] = _n, _g
    _n += _c
    _g += _c // 4 if _name[:2] == "dn" else _c
SLABS = _n


def slab_k(n):
    for name, count in STREAM:
        if SLAB0[name] <= n < SLAB0[name] + count:
            return DOWN_K[(n - SLAB0[name]) % 4] if name[:2] == "dn" else KD
    raise ValueError(n)


def program(nc, xT, memT, params, consts, rel_bias, onehot, w_mem, w_in_a, w_in_b, w_ba, w_out, w_gu,
            w_dn, outT):
    ctx = ExitStack()
    with ctx:
        def sb(name, shape, dt=F32, at=None):
            return (at or ctx).enter_context(nc.sbuf_tensor(name, shape, dt))

        def psum(name):
            return ctx.enter_context(nc.psum_tensor(name, [P, 512], F32))

        def sem(name):
            return ctx.enter_context(nc.semaphore(name))

        h = sb("h", [P, KD, SEQ])
        with ExitStack() as at:
            decay, amat, tmat, attn = (sb(x, [P, VH, P], at=at) for x in ("decay", "amat", "tmat", "attn"))
            zneg, umat, attn_t = (sb(x, [P, 2, VH, P], at=at) for x in ("zneg", "umat", "attn_t"))
        with ExitStack() as at:
            s1 = sb("s1", [P, 3, 4, 2 * P], at=at)
            pt1 = sb("pt1", [P, 2, 2, 4, P], at=at)
            small1 = sb("small1", [P, 3, 6, 4], at=at)
        xh = sb("xh", [P, KD, SEQ], F32R)
        xl = sb("xl", [P, KD, SEQ], F32R)
        with ExitStack() as at:
            osq, og = sb("osq", [P, VH, P], at=at), sb("og", [P, VH, P], at=at)
        sq = sb("sq", [P, SEQ])
        rms = sq
        ssq = sb("ssq", [P, SEQ])
        rinv = sb("rinv", [P, SEQ])
        raw = sb("raw", [P, RAW, KD * P])
        wh = sb("wh", [P, CUT, KD * P], F32R)
        wl = sb("wl", [P, CUT, KD * P], F32R)
        wba = sb("wba", [P, KD, 2 * VH])
        wbah = sb("wbah", [P, KD, 2 * VH], F32R)
        wbal = sb("wbal", [P, KD, 2 * VH], F32R)
        par = sb("par", [P, NPAR])
        con = sb("con", [P, NCONST, P])
        eps = sb("eps", [P, 1])
        mem_k = sb("mem_k", [P, 2, MT, MEM])
        mem_v = sb("mem_v", [P, 2, MT, 2 * P])
        ident, ones = con[:, IDENT, :], con[:, ONES, :]

        def col(name, i=0, n=1):
            a = COL[name] + i
            return par[:, a:a + n] if isinstance(a, int) else par[:, bass.ts(a, 1)]

        with ExitStack() as at:
            mT = sb("mT", [P, KD, MEM], at=at)
            m_sq = sb("m_sq", [P, KD, MEM], at=at)
            m_ss = sb("m_ss", [P, MEM], at=at)
            m_rms = sb("m_rms", [P, MEM], at=at)
            mn = sb("mn", [P, 2, KD, MEM], at=at)
            mh = sb("mh", [P, 2, KD, MEM], F32R, at=at)
            ml = sb("ml", [P, 2, KD, MEM], F32R, at=at)
            relb = sb("relb", [N_BUCKETS, A_HEADS], at=at)
            oneh = sb("oneh", [N_BUCKETS, WINDOW], at=at)
            brow = sb("brow", [A_HEADS, BIAS_PAD], at=at)
            bias_rev = sb("bias_rev", [P, A_HEADS, 2 * P], at=at)
        with ExitStack() as at:
            ch0 = sb("ch0", [P, KD, SEQ], F32R, at=at)
            cl0 = sb("cl0", [P, KD, SEQ], F32R, at=at)
            pa = sb("pa", [P, 10, SEQ], at=at)
            vtok = sb("vtok", [P, NB, P], at=at)
            s0 = sb("s0", [P, 3, 4, 2 * P], at=at)
            pt0 = sb("pt0", [P, 2, 2, 4, P], at=at)
            small0 = sb("small0", [P, 3, 6, 4], at=at)
            sb("under_bias_rev", [P, 3 * P * 2 * 3 + 1024], at=at)
            bias = sb("bias", [P, A_HEADS, 2 * P], at=at)
        with ExitStack() as at:
            ah = sb("ah", [P, FT, SEQ], F32R, at=at)
            al = sb("al", [P, FT, SEQ], F32R, at=at)
            graw = sb("graw", [P, 2, SEQ + 2], at=at)
            gacc = sb("gacc", [P, 2, SEQ], at=at)
            gsil = sb("gsil", [P, 2, SEQ], at=at)
            gup = sb("gup", [P, 2, SEQ], at=at)
        with ExitStack() as at:
            ch1 = sb("ch1", [P, KD, SEQ], F32R, at=at)
            cl1 = sb("cl1", [P, KD, SEQ], F32R, at=at)
            zt = sb("zt", [P, 8, SEQ], at=at)
            qkv = sb("qkv", [P, NQKV, SEQ], at=at)
            with ExitStack() as early:
                craw = sb("craw", [P, 2, SEQ + 3], at=early)
                cacc = sb("cacc", [P, 2, SEQ], at=early)
            gate = sb("gate", [P, 12, NB, VH], at=at)
            tail = sb("tail", [P, 2, VH], at=at)
            ba = sb("ba", [P, NB, 2 * VH], at=at)
            rtok = sb("rtok", [P, 2, NB], at=at)
            last = sb("last", [P, 2, VH], at=at)
            state, delta = (sb(x, [P, VH, P], at=at) for x in ("state", "delta"))
            qdec, vbeta, ktail = (sb(x, [P, 2, VH, P], at=at) for x in ("qdec", "vbeta", "ktail"))
        concat = {0: (ch0, cl0), 1: (ch1, cl1)}
        softmax_bufs = {0: (s0, pt0, small0), 1: (s1, pt1, small1)}
        MAXI, NEG, TOTAL, INV, SINK_D, SINK_E = range(6)
        LOGIT, ABS, EXP_ABS, EXP_B, EXP_A, LN, BETA, SOFT, NEG_G, GC, EXP_GC, NBE = range(12)

        banks = [psum(f"bank{i}") for i in range(8)]
        gemm_out = banks[0:2]
        score_banks = [banks[2:4], banks[0:2]]
        turned = banks[4:6]
        mixed = banks[6:8]
        stats = banks[7]

        par_in, x_in, mem_in, rel_in, ba_in = (sem(x) for x in ("par_in", "x_in", "mem_in", "rel_in", "ba_in"))
        w_in = [sem(f"w_in{i}") for i in range(RAW)]
        hi_cut, lo_cut = sem("hi_cut"), sem("lo_cut")
        slab_done = sem("slab_done")
        tile_out = sem("tile_out")
        sq_ready, sq_summed = sem("sq_ready"), sem("sq_summed")
        x_hi, x_lo = sem("x_hi"), sem("x_lo")
        stat_sum, stat_root, r_ready = sem("stat_sum"), sem("stat_root"), sem("r_ready")
        mem_sq, mem_sum, mem_stat, mem_root = (sem(x) for x in ("mem_sq", "mem_sum", "mem_stat", "mem_root"))
        mem_norm, mem_hi, mem_lo = sem("mem_norm"), sem("mem_hi"), sem("mem_lo")
        bias_mm, bias_row, bias_out, bias_in = (sem(x) for x in ("bias_mm", "bias_row", "bias_out", "bias_in"))
        bias_set = sem("bias_set")
        eps_set, v_turned, v_tok = sem("eps_set"), sem("v_turned"), sem("v_tok")
        sc_ready, max_ready, p_ready, pn_ready = (sem(x) for x in ("sc_ready", "max_ready", "p_ready", "pn_ready"))
        tp_ready, pt_ready, ov_ready = sem("tp_ready"), sem("pt_ready"), sem("ov_ready")
        c_hi, c_lo = sem("c_hi"), sem("c_lo")
        tap0, conv_ready, silu_ready = sem("tap0"), sem("conv_ready"), sem("silu_ready")
        a_ready, a_hi, a_lo = sem("a_ready"), sem("a_hi"), sem("a_lo")
        ba_hi, ba_lo = sem("ba_hi"), sem("ba_lo")
        d_pe, d_act, d_dve, d_pool = sem("d_pe"), sem("d_act"), sem("d_dve"), sem("d_pool")
        v_step, tap_step = sem("v_step"), sem("tap_step")
        out_ready, out_sent = sem("out_ready"), sem("out_sent")
        bias_rows = nc.dram_tensor("bias_rows", [A_HEADS, BIAS_PAD], F32, kind="Internal").ap()

        def gain(e, m):
            name = ("mix_g", "ffn_g", "mix_g", "ffn_g", "fin_g")[e]
            return col(name, m + (0 if e == 4 else (e // 2) * KD))

        def row(t, m):
            return t[:, m, :] if isinstance(m, int) else t[:, bass.ts(m, 1), :].rearrange("p a t -> p (a t)")

        groups = {0: [("self", b, jp) for b in range(NB) for jp in range(AJ // 2)]
                  + [("cross", b, None) for b in range(NB)],
                  1: [("cross", b, None) for b in range(NB)]}
        GROUP0 = {0: 0, 1: len(groups[0])}
        CONV0 = {"gu0": 0, "in1": FT, "gu1": FT + NQKV}

        L2 = range(2 * QKH)
        LV = range(1, LEVELS)
        HALF = range(2)
        ENGINE_STEP = {"pe": d_pe, "act": d_act, "dve": d_dve, "pool": d_pool}
        BEFORE = {
            "pe": ["ba"] + [f"l2 {j}" for j in L2] + ["cumsum"],
            "act": (["silu z", "ba root"] + [f"l2 {x} {j}" for x in ("square", "ln", "inverse") for j in L2]
                    + ["gate abs", "gate exp", "gate ln", "exp cumsum"]),
            "dve": ["ba scaled"] + [f"l2 {j}" for j in L2] + ["gate in", "beta", "g", "cumsum", "nbe"],
            "pool": []}
        PREPARE = {
            "pe": ["negcum", "kk", "qk", "k turned", "v turned", "attn turned", "T turned"],
            "act": ["decay", "grow", "last", "tail", "ktail", "attnT", "U0"],
            "dve": ["NG", "log decay", "tail", "A", "attn", "vbeta", "T0"],
            "pool": ["qdec"]}
        LEVEL = {"pe": ["Z", "UZ", "ZT"], "act": [], "dve": ["z", "U", "T"], "pool": ["clear"]}
        RECUR = {
            "pe": {1: ["kS"], 2: ["delta"], 3: ["out"], 4: ["state"], 5: ["norm"]},
            "act": {2: ["delta"], 3: ["square"], 5: ["norm ln", "norm inverse"], 6: ["hi"]},
            "dve": {1: ["R"], 4: ["state"], 6: ["out", "gated", "lo"]},
            "pool": {}}
        AFTER_FIRST = {"pe": 1, "act": 0, "dve": 3, "pool": 1}

        def exists(name, lv, c):
            return not (name in ("kS", "R") and c == 0 or name == "state" and c == NB - 1
                        or name in ("ZT", "T") and lv == LEVELS - 1)

        NUMBER = {}
        for who in ENGINE_STEP:
            names = [(x, None) for x in BEFORE[who]]
            for c in range(NB + 1):
                names += [(x, c) for x in PREPARE[who] if c < NB]
                for lv in LV:
                    level = [(f"{x} {lv}", c) for x in LEVEL[who] if c < NB and exists(x, lv, c)]
                    cut_at = AFTER_FIRST[who]
                    names += level[:cut_at]
                    names += [(x, c - 1) for x in RECUR[who].get(lv, []) if c and exists(x, None, c - 1)]
                    names += level[cut_at:]
            for n, x in enumerate(names):
                NUMBER[who, x] = n + 1
        told = dict.fromkeys(ENGINE_STEP, 0)

        def step(who, name, c, ins):
            told[who] += 1
            assert told[who] == NUMBER[who, (name, c)], (who, name, c)
            ins.then_inc(ENGINE_STEP[who], 1)

        def after(eng, who, name, c=None):
            eng.wait_ge(ENGINE_STEP[who], NUMBER[who, (name, c)])

        def flat(t):
            return t.rearrange("p a t -> p (a t)")

        def third(bank):
            return bank[:, 0:3 * P].rearrange("p (a t) -> p a t", a=3)

        def heads(hf):
            return slice(3 * hf, 3 * hf + 3)

        def blocks(t, lv, odd):
            b = 2 ** lv
            if len(t.shape) == 3:
                return t.rearrange("p h (n two b) -> p h n two b", two=2, b=b)[:, :, :, odd, :]
            return t.rearrange("p (n two b) -> p n two b", two=2, b=b)[:, :, odd, :]

        def packed(bank, lv):
            return bank[:, 0:3 * P].rearrange("p (h n b) -> p h n b", h=VH, b=2 ** lv)

        def slab_steps(eng, name, cut, post, take=lambda j, i: None):
            n0, count = SLAB0[name], dict(STREAM)[name]
            per = 8 if name[:2] == "dn" else 4
            trips = count // per

            def trip(i, last):
                for j in range(per):
                    take(j, i)
                    if not last:
                        cut(n0 + j + CUT, per * i)
                    elif n0 + per * i + j + CUT < SLABS:
                        cut(n0 + per * i + j + CUT)
                    post(j, i)
            if count % per == 0:
                with eng.Fori(0, trips - 1) as i:
                    trip(i, False)
                trip(trips - 1, True)
            else:
                with eng.Fori(0, trips) as i:
                    trip(i, False)
                for k in range(per * trips, count):
                    take(k, 0)
                    cut(n0 + k + CUT)
                    post(k, 0)

        block = ctx.enter_context(nc.Block())

        @block.sync
        def _(sp):
            def load_slab(n, src, it=0):
                if n >= RAW:
                    sp.wait_ge(lo_cut, n - RAW + 1 + 4 * it)
                sp.dma_start(raw[:, n % RAW, :slab_k(n) * P], src).then_inc(w_in[n % RAW], 16)

            def stream(name, src):
                count = dict(STREAM)[name]
                if count > 4:
                    with sp.Fori(0, count // 4) as i:
                        at = [sp.snap(4 * i + j) for j in range(4)]
                        for j in range(4):
                            load_slab(SLAB0[name] + j, src(at[j]), i)
                for k in range(count - count % 4 if count > 4 else 0, count):
                    load_slab(SLAB0[name] + k, src(k))

            def stream_down(layer):
                with sp.Fori(0, KD) as i:
                    for j in range(4):
                        a = DOWN_AT[j] * P
                        load_slab(SLAB0[f"dn{layer}"] + j, w_dn[layer, i, :, a:a + DOWN_K[j] * P], i)

            sp.dma_start(mT[:], memT).then_inc(mem_in, 16)
            sp.dma_start(con[:], consts).then_inc(par_in, 16)
            sp.dma_start(par[:], params).then_inc(par_in, 16)
            stream("mem0", lambda k: w_mem[0, k])
            sp.dma_start(h[:], xT).then_inc(x_in, 16)
            sp.dma_start(relb[:], rel_bias).then_inc(rel_in, 16)
            sp.dma_start(oneh[:], onehot).then_inc(rel_in, 16)
            sp.dma_start(wba[:], w_ba).then_inc(ba_in, 16)
            stream("mem1", lambda k: w_mem[1, k])
            stream("in0", lambda k: w_in_a[k])
            stream("out0", lambda k: w_out[0, k])
            stream("gu0", lambda k: w_gu[0, k])
            stream_down(0)
            stream("in1", lambda k: w_in_b[k])
            stream("out1", lambda k: w_out[1, k])
            stream("gu1", lambda k: w_gu[1, k])
            stream_down(1)
            for m in range(KD):
                sp.wait_ge(out_ready, m + 1)
                sp.dma_start(outT[:, m, :], h[:, m, :]).then_inc(out_sent, 16)
            sp.wait_ge(out_sent, 16 * KD)

        @block.gpsimd
        def _(pool):
            pool.wait_ge(bias_row, 1)
            pool.dma_start(bias_rows, brow[:]).then_inc(bias_out, 16)
            pool.wait_ge(bias_out, 16)
            for s in range(A_HEADS):
                rows = bass.AP(bias_rows.tensor, s * BIAS_PAD, [[1, P], [1, 2 * P]])
                pool.dma_start(bias_rev[:, s, :], rows).then_inc(bias_in, 16)

            for c in range(NB):
                t = slice(c * P, (c + 1) * P)
                after(pool, "act", "grow", c)
                if c == 0:
                    after(pool, "dve", f"l2 {QKH - 1}")
                for j in range(QKH):
                    q = qkv[:, j, t].unsqueeze(1).to_broadcast([P, 2, P])
                    two = qdec[:, c % 2, 2 * j:2 * j + 2, :]
                    ins = pool.tensor_tensor(two, q, two, ALU.mult)
                step("pool", "qdec", c, ins)
                for lv in LV:
                    if lv > 2:
                        after(pool, "pe", f"ZT {lv - 2}", c)
                    elif c:
                        after(pool, "pe", f"UZ {LEVELS - 1}" if lv == 2 else f"ZT {LEVELS - 2}", c - 1)
                    step("pool", f"clear {lv}", c, pool.memset(zneg[:, lv % 2], 0.0))

        @block.scalar
        def _(act):
            def cut_hi(n, more=0):
                act.wait_ge(w_in[n % RAW], 16 * (n // RAW + 1) + (16 // RAW) * more)
                if n >= CUT:
                    act.wait_ge(slab_done, n - CUT + 1 + more)
                w = slab_k(n) * P
                act.activation(wh[:, n % CUT, :w], raw[:, n % RAW, :w], ACT.Copy).then_inc(hi_cut, 1)

            def square_and_hi(e, m):
                if not (e == 0 and isinstance(m, int) and m == 0):
                    act.wait_ge(sq_summed, KD * e + m)
                act.activation(sq[:], row(h, m), ACT.Square).then_inc(sq_ready, 1)
                if e < 4:
                    act.activation(row(xh, m), row(h, m), ACT.Copy, scale=gain(e, m)).then_inc(x_hi, 1)

            def root(e):
                act.wait_ge(stat_sum, e + 1)
                act.activation(rms[:], stats[:], ACT.Sqrt, bias=eps[:], scale=1.0 / D_MODEL)\
                   .then_inc(stat_root, 1)

            def residual(name, e):
                g0 = TILE0[name]

                def post(j, i):
                    if name[:2] == "dn":
                        if j % 4 == 3:
                            act.wait_ge(tile_out, g0 + j // 4 + 1 + 2 * i)
                            square_and_hi(e, 2 * i + j // 4)
                    else:
                        act.wait_ge(tile_out, g0 + j + 1 + 4 * i)
                        square_and_hi(e, 4 * i + j)
                slab_steps(act, name, cut_hi, post)

            def attention(layer):
                s, pt, small = softmax_bufs[layer]
                ch = concat[layer][0]
                n, g0 = len(groups[layer]), GROUP0[layer]
                for t in range(n + 3):
                    if 2 <= t < n + 2:
                        u = t - 2
                        kind, b, _ = groups[layer][u]
                        act.wait_ge(tp_ready, g0 + u + 1)
                        if u >= 2:
                            act.wait_ge(ov_ready, g0 + u - 1)
                        for kc in range(1 if kind == "self" and b == 0 else 0, 2):
                            ins = act.activation(pt[:, u % 2, kc].rearrange("p a q -> p (a q)"),
                                                 turned[kc][:], ACT.Copy)
                        ins.then_inc(pt_ready, 1)
                    if t < n:
                        kind, b, jp = groups[layer][t]
                        lo = P if kind == "self" and b == 0 else 0
                        sm = small[:, t % 3]
                        act.wait_ge(max_ready, g0 + t + 1)
                        if kind == "self":
                            act.activation(sm[:, SINK_E, :], sm[:, SINK_D, :], ACT.Exp)
                        for i in range(4):
                            src = s[:, t % 3, i, lo:] if kind == "self" else \
                                score_banks[t % 2][i // 2][:, (i % 2) * 256:(i % 2) * 256 + 256]
                            ins = act.activation(s[:, t % 3, i, lo:], src, ACT.Exp, bias=sm[:, NEG, i:i + 1],
                                                 accum_out=sm[:, TOTAL, i:i + 1])
                        ins.then_inc(p_ready, 1)
                    if t >= 3:
                        u = t - 3
                        kind, b, jp = groups[layer][u]
                        first = 2 * jp if kind == "self" else 6
                        act.wait_ge(ov_ready, g0 + u + 1)
                        act.activation(ch[:, first:first + 2, b * P:(b + 1) * P],
                                       mixed[u % 2][:, 0:2 * P].rearrange("p (a q) -> p a q", a=2),
                                       ACT.Copy).then_inc(c_hi, 1)

            def mixer(layer):
                name = f"gu{layer}"
                g0, f0 = TILE0[name], layer * FT

                def post(j, i):
                    q, f = j // 2, 2 * i + j // 2
                    if j % 2 == 0:
                        act.wait_ge(tile_out, g0 + j + 1 + 4 * i)
                        act.activation(gacc[:, q, :], graw[:, q, 0:SEQ], ACT.Identity,
                                       bias=col("bias_f", f + f0),
                                       scale=col("conv_f", f + layer * F_TAPS * FT)).then_inc(tap0, 1)
                        act.wait_ge(conv_ready, CONV0[name] + q + 1 + 2 * i)
                        act.activation(gsil[:, q, :], gacc[:, q, :], ACT.Silu).then_inc(silu_ready, 1)
                    else:
                        act.wait_ge(a_ready, f0 + q + 1 + 2 * i)
                        act.activation(row(ah, f), gup[:, q, :], ACT.Copy).then_inc(a_hi, 1)
                slab_steps(act, name, cut_hi, post)

            def deltanet():
                squares = [decay, amat, tmat, attn, umat[:, 0], umat[:, 1]]
                sq_of = lambda j: flat(squares[j][:] if j < 4 else squares[j])[:, 0:SEQ]
                for j in L2:
                    step("act", f"l2 square {j}", None, act.activation(sq_of(j), qkv[:, j, :], ACT.Square))
                for j in L2:
                    after(act, "pe", f"l2 {j}")
                    step("act", f"l2 ln {j}", None, act.activation(sq_of(j), banks[j][:], ACT.Ln, bias=eps[:]))
                for j in L2:
                    after(act, "act", f"l2 ln {j}")
                    step("act", f"l2 inverse {j}", None, act.activation(sq_of(j), sq_of(j), ACT.Exp, scale=-0.5))
                after(act, "dve", "gate in")
                step("act", "gate abs", None, act.activation(gate[:, ABS], gate[:, LOGIT], ACT.Abs))
                after(act, "act", "gate abs")
                act.activation(gate[:, EXP_ABS], gate[:, ABS], ACT.Exp, scale=-1.0)
                act.activation(gate[:, EXP_A, 0, :], col("a_log", 0, VH), ACT.Exp)
                step("act", "gate exp", None, act.activation(gate[:, EXP_B], ba[:, :, 0:VH], ACT.Exp, scale=-1.0))
                after(act, "act", "gate exp")
                step("act", "gate ln", None, act.activation(gate[:, LN], gate[:, EXP_ABS], ACT.Ln, bias=ones[:, 0:1]))
                after(act, "dve", "cumsum")
                step("act", "exp cumsum", None, act.activation(gate[:, EXP_GC], gate[:, GC], ACT.Exp))

                def prepare(c):
                    s2 = c % 2
                    after(act, "dve", "log decay", c)
                    step("act", "decay", c, act.activation(decay[:], decay[:], ACT.Exp))
                    after(act, "dve", "tail", c)
                    for hf in HALF:
                        ins = act.activation(flat(qdec[:, s2, heads(hf), :]), banks[hf][:, 0:3 * P], ACT.Exp, scale=-1.0)
                    step("act", "grow", c, ins)
                    for hf in HALF:
                        ins = act.activation(last[:, s2, heads(hf)], third(banks[hf])[:, :, P - 1], ACT.Exp, scale=-1.0)
                    step("act", "last", c, ins)
                    step("act", "tail", c, act.activation(tail[:, 1, :], tail[:, 0, :], ACT.Exp, scale=-1.0))
                    after(act, "act", "tail", c)
                    after(act, "pe", "k turned", c)
                    for v in range(VH):
                        ins = act.activation(ktail[:, s2, v, :], banks[5][:, (v // 2) * P:(v // 2 + 1) * P],
                                             ACT.Copy, scale=tail[:, 1, v:v + 1])
                    step("act", "ktail", c, ins)
                    after(act, "pe", "attn turned", c)
                    for hf in HALF:
                        ins = act.activation(flat(attn_t[:, s2, heads(hf), :]), banks[hf][:, 0:3 * P], ACT.Copy)
                    step("act", "attnT", c, ins)
                    after(act, "pe", "T turned", c)
                    for hf, bank in enumerate((banks[2], banks[7])):
                        ins = act.activation(flat(umat[:, s2, heads(hf), :]), bank[:, 0:3 * P], ACT.Copy)
                    step("act", "U0", c, ins)

                def recur(lv, c):
                    t = slice(c * P, (c + 1) * P)
                    if lv == 2:
                        after(act, "pe", "delta", c)
                        for hf in HALF:
                            ins = act.activation(flat(delta[:, heads(hf), :]), banks[5 + hf][:, 0:3 * P], ACT.Copy)
                        step("act", "delta", c, ins)
                    elif lv == 3:
                        after(act, "pe", "out", c)
                        for hf in HALF:
                            ins = act.activation(flat(osq[:, heads(hf), :]), banks[3 + hf][:, 0:3 * P], ACT.Square)
                        step("act", "square", c, ins)
                    elif lv == 5:
                        after(act, "pe", "norm", c)
                        for hf in HALF:
                            ins = act.activation(flat(osq[:, heads(hf), :]), banks[5 + hf][:, 0:3 * P], ACT.Ln,
                                                 bias=eps[:], scale=1.0 / DK)
                        step("act", "norm ln", c, ins)
                        after(act, "act", "norm ln", c)
                        step("act", "norm inverse", c, act.activation(osq[:], osq[:], ACT.Exp, scale=-0.5))
                    elif lv == 6:
                        after(act, "dve", "gated", c)
                        step("act", "hi", c, act.activation(ch1[:, 0:VH, t], og[:], ACT.Copy))

                for c in range(NB + 1):
                    if c < NB:
                        prepare(c)
                    for lv in LV:
                        if c:
                            recur(lv, c - 1)

            act.wait_ge(mem_in, 16)
            act.activation(m_sq[:], mT[:], ACT.Square).then_inc(mem_sq, 1)
            cut_hi(0)
            cut_hi(1)
            act.wait_ge(mem_stat, 1)
            act.wait_ge(eps_set, 1)
            act.activation(m_rms[:], stats[:, 0:MEM], ACT.Sqrt, bias=eps[:], scale=1.0 / D_MODEL)\
               .then_inc(mem_root, 1)
            for layer in range(2):
                act.wait_ge(mem_norm, layer + 1)
                act.activation(mh[:, layer], mn[:, layer], ACT.Copy).then_inc(mem_hi, 1)
            act.wait_ge(x_in, 16)
            act.wait_ge(par_in, 32)
            for k in range(KD):
                cut_hi(k + CUT)
                square_and_hi(0, k)
            root(0)
            slab_steps(act, "in0", cut_hi, lambda j, i: None)
            attention(0)
            residual("out0", 1)
            root(1)
            mixer(0)
            residual("dn0", 2)
            root(2)

            def conv_post(k, i):
                act.wait_ge(tile_out, TILE0["in1"] + k + 1 + 4 * i)
                act.activation(cacc[:, k % 2, :], craw[:, k % 2, 0:SEQ], ACT.Copy,
                               scale=col("conv_b", 4 * i + k)).then_inc(tap0, 1)
                act.wait_ge(conv_ready, CONV0["in1"] + k + 1 + 4 * i)
                act.activation(row(qkv, 4 * i + k), cacc[:, k % 2, :], ACT.Silu).then_inc(silu_ready, 1)
            n0 = SLAB0["in1"]
            with act.Fori(0, NQKV // 4) as i:
                for j in range(4):
                    cut_hi(n0 + j + CUT, 4 * i)
                    conv_post(j, i)
            for k in range(NQKV, 20):
                cut_hi(n0 + k + CUT)
            act.wait_ge(ba_in, 16)
            act.activation(wbah[:], wba[:], ACT.Copy).then_inc(ba_hi, 1)
            act.wait_ge(tile_out, TILE0["out1"])
            step("act", "silu z", None, act.activation(zt[:, 0:VH, :], zt[:, 0:VH, :], ACT.Silu))
            after(act, "pe", "ba")
            step("act", "ba root", None, act.activation(rtok[:, 0, :], stats[:, 64:64 + NB], ACT.Sqrt,
                                                        bias=eps[:], scale=1.0 / D_MODEL))
            attention(1)
            deltanet()
            residual("out1", 3)
            root(3)
            mixer(1)
            residual("dn1", 4)
            root(4)

        @block.vector
        def _(dve):
            steps = [0]

            def then_wait(ins):
                steps[0] += 1
                ins.then_inc(v_step, 1)
                dve.wait_ge(v_step, steps[0])

            def cut_lo(n, more=0):
                dve.wait_ge(hi_cut, n + 1 + more)
                w = slab_k(n) * P
                dve.tensor_tensor(wl[:, n % CUT, :w], raw[:, n % RAW, :w], wh[:, n % CUT, :w].bitcast(F32),
                                  ALU.subtract).then_inc(lo_cut, 1)

            def sum_and_lo(e, m):
                dve.wait_ge(sq_ready, KD * e + 1 + m)
                dve.tensor_tensor(ssq[:], ssq[:], sq[:], ALU.add).then_inc(sq_summed, 1)
                if e < 4:
                    dve.wait_ge(x_hi, KD * e + 1 + m)
                    dve.scalar_tensor_tensor(out=row(xl, m), in0=row(h, m), scalar=gain(e, m),
                                             in1=row(xh, m).bitcast(F32), op0=ALU.mult, op1=ALU.subtract)\
                       .then_inc(x_lo, 1)

            def inverse_rms(e):
                dve.wait_ge(stat_root, e + 1)
                dve.reciprocal(rinv[:], rms[:]).then_inc(r_ready, 1)
                dve.wait_ge(r_ready, e + 1)

            def residual(name, e):
                n0, g0 = SLAB0[name], TILE0[name]
                then_wait(dve.memset(ssq[:], 0.0))

                down = name[:2] == "dn"

                def which(j, i):
                    return (2 * i + j // 4, j // 4) if down else (4 * i + j, j)

                def add(j, i):
                    if down and j % 4 < 3:
                        return
                    m, tile = which(j, i)
                    dve.wait_ge(slab_done, n0 + j + 1 + (8 if down else 4) * i)
                    dve.tensor_tensor(row(h, m), gemm_out[(g0 + tile) % 2][:], row(h, m), ALU.add)\
                       .then_inc(tile_out, 1)

                def post(j, i):
                    if down and j % 4 < 3:
                        return
                    m, tile = which(j, i)
                    dve.wait_ge(tile_out, g0 + tile + 1 + (2 if down else 4) * i)
                    dve.wait_ge(sq_summed, KD * e + m)
                    sum_and_lo(e, m)
                slab_steps(dve, name, cut_lo, post, add)

            def take(name, k, i, out):
                dve.wait_ge(slab_done, SLAB0[name] + k + 1 + 4 * i)
                dve.tensor_tensor(out, gemm_out[(TILE0[name] + k) % 2][:], rinv[:], ALU.mult)\
                   .then_inc(tile_out, 1)

            def taps(name, raw_tile, acc, k, i, weight, count):
                c0 = CONV0[name]
                per = 2 if name[:2] == "gu" else 4
                dve.wait_ge(tap0, c0 + k + 1 + per * i)
                for tap in range(1, count):
                    ins = dve.scalar_tensor_tensor(out=acc, in0=raw_tile[:, tap:tap + SEQ], scalar=weight(tap),
                                                   in1=acc, op0=ALU.mult, op1=ALU.add)
                    if tap < count - 1:
                        ins.then_inc(tap_step, 1)
                        dve.wait_ge(tap_step, tap_steps[name] + (count - 2) * k + tap + (count - 2) * per * i)
                ins.then_inc(conv_ready, 1)

            tap_steps = {"gu0": 0, "in1": FT, "gu1": FT + 2 * NQKV}

            def attention(layer):
                s, pt, small = softmax_bufs[layer]
                ch, cl = concat[layer]
                n, g0 = len(groups[layer]), GROUP0[layer]
                for t in range(n + 3):
                    if t < n:
                        kind, b, jp = groups[layer][t]
                        lo = P if kind == "self" and b == 0 else 0
                        sm = small[:, t % 3]
                        dve.wait_ge(sc_ready, g0 + t + 1)
                        if t >= 3:
                            dve.wait_ge(tp_ready, g0 + t - 2)
                        if kind == "self":
                            for i in range(4):
                                slot = 2 * (2 * jp + i % 2) + i // 2
                                src = score_banks[t % 2][i // 2][:, (i % 2) * 256 + lo:(i % 2) * 256 + 256]
                                ins = dve.tensor_tensor_reduce(
                                    s[:, t % 3, i, lo:], src, bias[:, slot, lo:], 1.0, col("sinks", slot),
                                    ALU.add, ALU.max, sm[:, MAXI, i:i + 1])
                            then_wait(ins)
                            then_wait(dve.tensor_scalar(sm[:, NEG, :], sm[:, MAXI, :], -1.0, None, ALU.mult))
                            sinks = col("sinks", 4 * jp, 4).rearrange("p (j kv) -> p kv j", kv=2)
                            dve.tensor_tensor(sm[:, SINK_D, :].rearrange("p (kv j) -> p kv j", kv=2), sinks,
                                              sm[:, NEG, :].rearrange("p (kv j) -> p kv j", kv=2), ALU.add)\
                               .then_inc(max_ready, 1)
                        else:
                            for half in range(2):
                                ins = dve.tensor_reduce(
                                    sm[:, MAXI, 2 * half:2 * half + 2],
                                    score_banks[t % 2][half][:].rearrange("p (a k) -> p a k", a=2), AX.X, ALU.max)
                            then_wait(ins)
                            dve.tensor_scalar(sm[:, NEG, :], sm[:, MAXI, :], -1.0, None, ALU.mult)\
                               .then_inc(max_ready, 1)
                    if 1 <= t <= n:
                        kind, b, jp = groups[layer][t - 1]
                        lo = P if kind == "self" and b == 0 else 0
                        sm = small[:, (t - 1) % 3]
                        dve.wait_ge(p_ready, g0 + t)
                        total = TOTAL
                        if kind == "self":
                            then_wait(dve.tensor_tensor(sm[:, SINK_D, :], sm[:, TOTAL, :], sm[:, SINK_E, :], ALU.add))
                            total = SINK_D
                        then_wait(dve.reciprocal(sm[:, INV, :], sm[:, total, :]))
                        for i in range(4):
                            p = s[:, (t - 1) % 3, i, lo:]
                            ins = dve.tensor_scalar(p, p, sm[:, INV, i:i + 1], None, ALU.mult)
                        ins.then_inc(pn_ready, 1)
                    if t >= 3:
                        kind, b, jp = groups[layer][t - 3]
                        first = 2 * jp if kind == "self" else 6
                        q = slice(b * P, (b + 1) * P)
                        dve.wait_ge(c_hi, g0 + t - 2)
                        dve.tensor_tensor(cl[:, first:first + 2, q],
                                          mixed[(t - 3) % 2][:, 0:2 * P].rearrange("p (a q) -> p a q", a=2),
                                          ch[:, first:first + 2, q].bitcast(F32), ALU.subtract).then_inc(c_lo, 1)

            def mixer(layer):
                name = f"gu{layer}"
                f0 = layer * FT
                then_wait(dve.memset(graw[:, :, 0:F_TAPS - 1], 0.0))

                def take_tile(j, i):
                    take(name, j, i, graw[:, j // 2, F_TAPS - 1:] if j % 2 == 0 else gup[:, j // 2, :])

                def post(j, i):
                    q, f = j // 2, 2 * i + j // 2
                    if j % 2 == 0:
                        dve.wait_ge(tile_out, TILE0[name] + j + 1 + 4 * i)
                        taps(name, graw[:, q], gacc[:, q, :], q, i,
                             lambda tap: col("conv_f", f + (layer * F_TAPS + tap) * FT), F_TAPS)
                    else:
                        dve.wait_ge(tile_out, TILE0[name] + j + 1 + 4 * i)
                        dve.wait_ge(silu_ready, CONV0[name] + q + 1 + 2 * i)
                        dve.tensor_tensor(gup[:, q, :], gsil[:, q, :], gup[:, q, :], ALU.mult).then_inc(a_ready, 1)
                        dve.wait_ge(a_ready, f0 + q + 1 + 2 * i)
                        dve.wait_ge(a_hi, f0 + q + 1 + 2 * i)
                        dve.tensor_tensor(row(al, f), gup[:, q, :], row(ah, f).bitcast(F32), ALU.subtract)\
                           .then_inc(a_lo, 1)
                slab_steps(dve, name, cut_lo, post, take_tile)

            def deltanet():
                tokens = lambda t: t.unsqueeze(2).to_broadcast([P, NB, VH])
                inverses = [decay, amat, tmat, attn, umat[:, 0], umat[:, 1]]
                for j in L2:
                    r = flat(inverses[j][:] if j < 4 else inverses[j])[:, 0:SEQ]
                    after(dve, "act", f"l2 inverse {j}")
                    if j < QKH:
                        ins = dve.scalar_tensor_tensor(out=qkv[:, j, :], in0=qkv[:, j, :], scalar=DK ** -0.5,
                                                       in1=r, op0=ALU.mult, op1=ALU.mult)
                    else:
                        ins = dve.tensor_tensor(qkv[:, j, :], qkv[:, j, :], r, ALU.mult)
                    step("dve", f"l2 {j}", None, ins)
                dt = col("dt_bias", 0, VH).unsqueeze(1).to_broadcast([P, NB, VH])
                step("dve", "gate in", None, dve.tensor_tensor(gate[:, LOGIT], ba[:, :, VH:], dt, ALU.add))
                after(dve, "act", "gate exp")
                then_wait(dve.tensor_scalar(gate[:, BETA], gate[:, EXP_B], 1.0, None, ALU.add))
                step("dve", "beta", None, dve.reciprocal(gate[:, BETA], gate[:, BETA]))
                after(dve, "act", "gate ln")
                then_wait(dve.scalar_tensor_tensor(out=gate[:, SOFT], in0=gate[:, LOGIT], scalar=0.0,
                                                   in1=gate[:, LN], op0=ALU.max, op1=ALU.add))
                ea = gate[:, EXP_A, 0, :].unsqueeze(1).to_broadcast([P, NB, VH])
                step("dve", "g", None, dve.tensor_tensor(gate[:, NEG_G], gate[:, SOFT], ea, ALU.mult))
                after(dve, "pe", "cumsum")
                step("dve", "cumsum", None, dve.tensor_scalar(
                    gate[:, GC].rearrange("p c v -> p (c v)"), stats[:, 128:128 + NB * VH], -1.0, None, ALU.mult))
                after(dve, "act", "exp cumsum")
                step("dve", "nbe", None, dve.scalar_tensor_tensor(
                    out=gate[:, NBE], in0=gate[:, BETA], scalar=-1.0, in1=gate[:, EXP_GC], op0=ALU.mult, op1=ALU.mult))
                after(dve, "dve", "nbe")

                def prepare(c):
                    s2 = c % 2
                    beta = gate[:, BETA, c, :].unsqueeze(2)
                    for v in range(VH):
                        ins = dve.tensor_scalar(attn[:, v, :], con[:, TRI, :], gate[:, NEG_G, c, v:v + 1], None, ALU.mult)
                    step("dve", "NG", c, ins)
                    after(dve, "pe", "negcum", c)
                    for v in range(VH):
                        ins = dve.scalar_tensor_tensor(
                            out=decay[:, v, :], in0=banks[v // 3][:, (v % 3) * P:(v % 3 + 1) * P],
                            scalar=gate[:, GC, c, v:v + 1], in1=con[:, CAUSAL, :], op0=ALU.add, op1=ALU.add)
                    step("dve", "log decay", c, ins)
                    for hf in HALF:
                        ins = dve.tensor_tensor(tail[:, 0, heads(hf)], third(banks[hf])[:, :, P - 1],
                                                gate[:, GC, c, heads(hf)], ALU.add)
                    step("dve", "tail", c, ins)
                    after(dve, "act", "decay", c)
                    then_wait(dve.tensor_tensor(amat[:], decay[:], beta.to_broadcast([P, VH, P]), ALU.mult))
                    after(dve, "pe", "qk", c)
                    pair = lambda x: x[:].rearrange("p (j e) t -> p j e t", e=2)
                    both = lambda bank: third(bank).unsqueeze(2).to_broadcast([P, 3, 2, P])
                    step("dve", "A", c, dve.tensor_tensor(pair(amat), both(banks[2]), pair(amat), ALU.mult))
                    step("dve", "attn", c, dve.tensor_tensor(pair(attn), both(banks[7]), pair(decay), ALU.mult))
                    after(dve, "pe", "v turned", c)
                    for hf in HALF:
                        ins = dve.tensor_tensor(vbeta[:, s2, heads(hf), :], third(banks[3 + hf]),
                                                gate[:, BETA, c, heads(hf)].unsqueeze(2).to_broadcast([P, 3, P]), ALU.mult)
                    step("dve", "vbeta", c, ins)
                    after(dve, "dve", "A", c)
                    m0 = con[:, LEVEL0, :].unsqueeze(1).to_broadcast([P, VH, P])
                    idb = ident.unsqueeze(1).to_broadcast([P, VH, P])
                    then_wait(dve.tensor_tensor(tmat[:], amat[:], m0, ALU.mult))
                    step("dve", "T0", c, dve.tensor_tensor(tmat[:], idb, tmat[:], ALU.subtract))

                def level(lv, c):
                    above = con[:, ABOVE + (lv - 1) // 2, (lv - 1) % 2 * (P // 2):((lv - 1) % 2 + 1) * (P // 2)]
                    above = above.rearrange("p (n b) -> p n b", b=2 ** lv).unsqueeze(1)\
                        .to_broadcast([P, VH, P // 2 // 2 ** lv, 2 ** lv])
                    after(dve, "pe", f"Z {lv}", c)
                    after(dve, "pool", f"clear {lv}", c)
                    step("dve", f"z {lv}", c, dve.tensor_tensor(
                        blocks(zneg[:, lv % 2], lv, 1), packed(banks[0], lv), above, ALU.mult))
                    after(dve, "pe", f"UZ {lv}", c)
                    u = blocks(umat[:, c % 2], lv, 1)
                    step("dve", f"U {lv}", c, dve.tensor_tensor(u, packed(banks[1], lv), u, ALU.add))
                    if lv < LEVELS - 1:
                        after(dve, "pe", f"ZT {lv}", c)
                        tt = blocks(tmat[:], lv, 0)
                        step("dve", f"T {lv}", c, dve.tensor_tensor(tt, packed(banks[2], lv), tt, ALU.add))

                def recur(lv, c):
                    s2, t = c % 2, slice(c * P, (c + 1) * P)
                    if lv == 1 and c:
                        after(dve, "pe", "kS", c)
                        for v in range(VH):
                            ins = dve.scalar_tensor_tensor(
                                out=vbeta[:, s2, v, :], in0=banks[3 + v // 3][:, (v % 3) * P:(v % 3 + 1) * P],
                                scalar=gate[:, NBE, c, v:v + 1], in1=vbeta[:, s2, v, :], op0=ALU.mult, op1=ALU.add)
                        step("dve", "R", c, ins)
                    elif lv == 4 and c < NB - 1:
                        after(dve, "pe", "state", c)
                        for v in range(VH):
                            ps = banks[5 + v // 3][:, (v % 3) * P:(v % 3 + 1) * P]
                            if c:
                                ins = dve.scalar_tensor_tensor(out=state[:, v, :], in0=state[:, v, :],
                                                               scalar=last[:, s2, v:v + 1], in1=ps,
                                                               op0=ALU.mult, op1=ALU.add)
                            else:
                                ins = dve.tensor_copy(state[:, v, :], ps)
                        step("dve", "state", c, ins)
                    elif lv == 6:
                        after(dve, "act", "norm inverse", c)
                        for hf in HALF:
                            ins = dve.scalar_tensor_tensor(out=og[:, heads(hf), :], in0=third(banks[3 + hf]),
                                                           scalar=col("out_g"), in1=osq[:, heads(hf), :],
                                                           op0=ALU.mult, op1=ALU.mult)
                        step("dve", "out", c, ins)
                        after(dve, "dve", "out", c)
                        step("dve", "gated", c, dve.tensor_tensor(og[:], og[:], zt[:, 0:VH, t], ALU.mult))
                        after(dve, "act", "hi", c)
                        step("dve", "lo", c, dve.tensor_tensor(cl1[:, 0:VH, t], og[:], ch1[:, 0:VH, t].bitcast(F32),
                                                               ALU.subtract))

                for c in range(NB + 1):
                    if c < NB:
                        prepare(c)
                    for lv in LV:
                        if c < NB:
                            level(lv, c)
                        if c:
                            recur(lv, c - 1)

            dve.memset(eps[:], EPS).then_inc(eps_set, 1)
            then_wait(dve.memset(brow[:], -BIG))
            dve.wait_ge(mem_sq, 1)
            then_wait(dve.tensor_tensor(m_ss[:], m_sq[:, 0, :], m_sq[:, 1, :], ALU.add))
            for k in range(2, KD):
                ins = dve.tensor_tensor(m_ss[:], m_ss[:], m_sq[:, k, :], ALU.add)
                then_wait(ins) if k < KD - 1 else ins.then_inc(mem_sum, 1)
            cut_lo(0)
            cut_lo(1)
            dve.wait_ge(mem_root, 1)
            dve.wait_ge(par_in, 32)
            then_wait(dve.reciprocal(m_rms[:], m_rms[:]))
            for layer in range(2):
                for k in range(KD):
                    ins = dve.scalar_tensor_tensor(out=mn[:, layer, k, :], in0=mT[:, k, :],
                                                   scalar=col("mem_g", layer * KD + k), in1=m_rms[:],
                                                   op0=ALU.mult, op1=ALU.mult)
                ins.then_inc(mem_norm, 1)
                dve.wait_ge(mem_norm, layer + 1)
                dve.wait_ge(mem_hi, layer + 1)
                dve.tensor_tensor(ml[:, layer], mn[:, layer], mh[:, layer].bitcast(F32), ALU.subtract)\
                   .then_inc(mem_lo, 1)
            dve.wait_ge(bias_mm, 1)
            dve.tensor_copy(brow[:, P:2 * P], mixed[0][0:A_HEADS, 0:WINDOW]).then_inc(bias_row, 1)
            then_wait(dve.memset(ssq[:], 0.0))
            dve.wait_ge(x_in, 16)
            for k in range(8):
                layer, part = k // 4, k % 4
                dve.wait_ge(slab_done, k + 1)
                bank = gemm_out[k % 2]
                if part < 2:
                    dve.tensor_scalar(mem_k[:, layer, part, :], bank[:, 0:MEM], DH ** -0.5, None, ALU.mult)\
                       .then_inc(tile_out, 1)
                else:
                    dve.tensor_copy(mem_v[:, layer, :, (part - 2) * P:(part - 1) * P],
                                    bank[:, 0:MT * P].rearrange("p (a d) -> p a d", a=MT)).then_inc(tile_out, 1)
                cut_lo(k + CUT)
                if k:
                    dve.wait_ge(sq_summed, k)
                sum_and_lo(0, k)
            dve.wait_ge(bias_out, 16)
            inverse_rms(0)
            slab_steps(dve, "in0", cut_lo, lambda j, i: None, lambda j, i: take(
                "in0", j, i, row(pa, 4 * i + j if j < 4 else j)))
            dve.wait_ge(tile_out, TILE0["out0"])
            then_wait(dve.tensor_scalar(pa[:, 0, :], pa[:, 0, :], DH ** -0.5, None, ALU.mult))
            dve.wait_ge(v_turned, 1)
            dve.tensor_copy(vtok[:].rearrange("p b d -> p (b d)"), turned[0][:]).then_inc(v_tok, 1)
            for n in range(6):
                dve.wait_ge(bias_mm, n + 2)
                dve.tensor_copy(bias[:, 2 * n:2 * n + 2, :].rearrange("p a k -> p (a k)"), banks[2 + n][:])\
                   .then_inc(bias_set, 1)
            dve.wait_ge(bias_set, 6)
            attention(0)
            residual("out0", 1)
            inverse_rms(1)
            mixer(0)
            residual("dn0", 2)
            inverse_rms(2)
            then_wait(dve.memset(craw[:, :, 0:B_TAPS - 1], 0.0))

            def conv_post(k, i):
                dve.wait_ge(tile_out, TILE0["in1"] + k + 1 + 4 * i)
                taps("in1", craw[:, k % 2], cacc[:, k % 2, :], k, i,
                     lambda tap: col("conv_b", 4 * i + (k + tap * NQKV)), B_TAPS)
            with dve.Fori(0, NQKV // 4) as i:
                for j in range(4):
                    take("in1", j, i, craw[:, j % 2, B_TAPS - 1:])
                    cut_lo(SLAB0["in1"] + j + CUT, 4 * i)
                    conv_post(j, i)
            for k in range(NQKV, 20):
                take("in1", k, 0, zt[:, k - NQKV, :])
                cut_lo(SLAB0["in1"] + k + CUT)
            dve.wait_ge(ba_hi, 1)
            dve.tensor_tensor(wbal[:], wba[:], wbah[:].bitcast(F32), ALU.subtract).then_inc(ba_lo, 1)
            after(dve, "act", "ba root")
            then_wait(dve.reciprocal(rtok[:, 1, :], rtok[:, 0, :]))
            for b in range(NB):
                ins = dve.tensor_scalar(ba[:, b, :], stats[:, 2 * VH * b:2 * VH * (b + 1)],
                                        rtok[:, 1, b:b + 1], None, ALU.mult)
            step("dve", "ba scaled", None, ins)
            attention(1)
            deltanet()
            after(dve, "dve", "lo", NB - 1)
            residual("out1", 3)
            inverse_rms(3)
            mixer(1)
            residual("dn1", 4)
            inverse_rms(4)
            for m in range(KD):
                dve.scalar_tensor_tensor(out=h[:, m, :], in0=h[:, m, :], scalar=gain(4, m), in1=rinv[:],
                                         op0=ALU.mult, op1=ALU.mult).then_inc(out_ready, 1)

        @block.tensor
        def _(pe):
            def slab(n, more, out, moving, first=True, last=True, k0=0):
                pe.wait_ge(lo_cut, n + 1 + more)
                count = slab_k(n)
                for k in range(count):
                    w = slice(k * P, (k + 1) * P)
                    xhi, xlo = moving(k0 + k)
                    pe.matmul(out, wh[:, n % CUT, w], xhi, start=first and k == 0, stop=False)
                    pe.matmul(out, wh[:, n % CUT, w], xlo, start=False, stop=False)
                    ins = pe.matmul(out, wl[:, n % CUT, w], xhi, start=False, stop=last and k == count - 1)
                ins.then_inc(slab_done, 1)

            def of(hi, lo):
                return lambda k: (hi[:, k, :], lo[:, k, :])

            def products(name, moving):
                n0, g0, count = SLAB0[name], TILE0[name], dict(STREAM)[name]

                def one(j, i):
                    pe.wait_ge(tile_out, g0 + j - 1 + 4 * i)
                    slab(n0 + j, 4 * i, gemm_out[(g0 + j) % 2][:], moving)
                with pe.Fori(0, count // 4) as i:
                    for j in range(4):
                        one(j, i)
                for k in range(count - count % 4, count):
                    one(k, 0)

            def down(layer):
                n0, g0 = SLAB0[f"dn{layer}"], TILE0[f"dn{layer}"]
                pe.wait_ge(a_lo, FT * (layer + 1))
                with pe.Fori(0, KD // 2) as i:
                    for j in range(8):
                        if j % 4 == 0:
                            pe.wait_ge(tile_out, g0 + j // 4 - 1 + 2 * i)
                        slab(n0 + j, 8 * i, gemm_out[(g0 + j // 4) % 2][:], of(ah, al), first=j % 4 == 0,
                             last=j % 4 == 3, k0=DOWN_AT[j % 4])

            def norm(e):
                if e < 4:
                    pe.wait_ge(x_lo, KD * (e + 1))
                pe.wait_ge(sq_summed, KD * (e + 1))
                pe.matmul(stats[:], ones, ssq[:], start=True, stop=True).then_inc(stat_sum, 1)

            def attention(layer):
                s, pt, small = softmax_bufs[layer]
                n, g0 = len(groups[layer]), GROUP0[layer]
                queries = pa[:, 8:10] if layer == 0 else zt[:, 6:8]
                for t in range(n + 3):
                    if t < n:
                        kind, b, jp = groups[layer][t]
                        q = slice(b * P, (b + 1) * P)
                        if t >= 2:
                            used = max_ready if groups[layer][t - 2][0] == "self" else p_ready
                            pe.wait_ge(used, g0 + t - 1)
                        for i in range(4):
                            half, side = slice((i // 2) * DH, (i // 2 + 1) * DH), (i % 2) * 256
                            out = score_banks[t % 2][i // 2]
                            if kind == "self":
                                lo = P if b == 0 else 0
                                ins = pe.matmul(out[:, side + lo:side + 256], pa[half, 2 + 2 * jp + i % 2, q],
                                                pa[half, 0, (b - 1) * P + lo:(b + 1) * P], start=True, stop=True)
                            else:
                                ins = pe.matmul(out[:, side:side + 256], queries[half, i % 2, q],
                                                mem_k[half, layer, i % 2, :], start=True, stop=True)
                        ins.then_inc(sc_ready, 1)
                    if 2 <= t < n + 2:
                        u = t - 2
                        kind, b, jp = groups[layer][u]
                        pe.wait_ge(pn_ready, g0 + u + 1)
                        if u:
                            pe.wait_ge(pt_ready, g0 + u)
                        for kc in range(1 if kind == "self" and b == 0 else 0, 2):
                            for i in range(4):
                                ins = pe.transpose(turned[kc][:, i * P:(i + 1) * P],
                                                   s[:, u % 3, i, kc * P:(kc + 1) * P], ident)
                        ins.then_inc(tp_ready, 1)
                    if t >= 3:
                        u = t - 3
                        kind, b, jp = groups[layer][u]
                        pe.wait_ge(pt_ready, g0 + u + 1)
                        if u >= 2:
                            pe.wait_ge(c_lo, g0 + u - 1)
                        out, p = mixed[u % 2], pt[:, u % 2]
                        for half in range(2):
                            if kind == "self":
                                d = slice(half * DH, (half + 1) * DH)
                                parts = range(1 if b == 0 else 0, 2)
                                for kc in parts:
                                    ins = pe.matmul(out[d, 0:2 * P], vtok[:, b - 1 + kc, d],
                                                    p[:, kc, 2 * half:2 * half + 2, :].rearrange("p a q -> p (a q)"),
                                                    start=kc == parts[0], stop=kc == 1)
                                continue
                            for a in range(2):
                                hd = 2 * a + half
                                for kc in range(2):
                                    ins = pe.matmul(out[half * DH:(half + 1) * DH, a * P:(a + 1) * P],
                                                    mem_v[:, layer, kc, hd * DH:(hd + 1) * DH],
                                                    p[:, kc, 2 * half + a, :], start=kc == 0, stop=kc == 1)
                        ins.then_inc(ov_ready, 1)
                pe.wait_ge(c_lo, g0 + n)

            def gates():
                pe.wait_ge(ba_lo, 1)
                for b in range(NB):
                    t, o = slice(b * P, (b + 1) * P), stats[:, 2 * VH * b:2 * VH * (b + 1)]
                    for k in range(KD):
                        pe.matmul(o, xh[:, k, t], wbah[:, k, :], start=k == 0, stop=False)
                        pe.matmul(o, xl[:, k, t], wbah[:, k, :], start=False, stop=False)
                        pe.matmul(o, xh[:, k, t], wbal[:, k, :], start=False, stop=k == KD - 1)
                for b in range(NB):
                    ins = pe.matmul(stats[:, 64 + b:65 + b], ssq[:, b * P:(b + 1) * P], ones[:, 0:1],
                                    start=True, stop=True)
                step("pe", "ba", None, ins)

            def deltanet():
                squares = [decay, amat, tmat, attn, umat[:, 0], umat[:, 1]]
                for j in L2:
                    after(pe, "act", f"l2 square {j}")
                    sq_of = flat(squares[j][:] if j < 4 else squares[j])[:, 0:SEQ]
                    step("pe", f"l2 {j}", None, pe.matmul(banks[j][:], ones, sq_of, start=True, stop=True))
                after(pe, "dve", "g")
                step("pe", "cumsum", None, pe.matmul(stats[:, 128:128 + NB * VH], con[:, TRI, :],
                                                     gate[:, NEG_G].rearrange("p c v -> p (c v)"), start=True, stop=True))

                def tile(bank, v):
                    return bank[:, v * P:(v + 1) * P]

                def prepare(c):
                    t = slice(c * P, (c + 1) * P)
                    after(pe, "dve", "NG", c)
                    for hf in HALF:
                        ins = pe.matmul(banks[hf][:, 0:3 * P], ones, flat(attn[:, heads(hf), :]), start=True, stop=True)
                    step("pe", "negcum", c, ins)
                    after(pe, "dve", f"l2 {2 * QKH - 1}")
                    for j in range(QKH):
                        ins = pe.matmul(tile(banks[2], j), qkv[:, QKH + j, t], qkv[:, QKH + j, t], start=True, stop=True)
                    step("pe", "kk", c, ins)
                    after(pe, "dve", "cumsum")
                    for j in range(QKH):
                        ins = pe.matmul(tile(banks[7], j), qkv[:, j, t], qkv[:, QKH + j, t], start=True, stop=True)
                    step("pe", "qk", c, ins)
                    if c > 1:
                        after(pe, "act", "norm ln", c - 2)
                    for j in range(QKH):
                        ins = pe.transpose(tile(banks[5], j), qkv[:, QKH + j, t], ident)
                    step("pe", "k turned", c, ins)
                    if c > 1:
                        after(pe, "dve", "out", c - 2)
                    for v in range(VH):
                        ins = pe.transpose(tile(banks[3 + v // 3], v % 3), qkv[:, 2 * QKH + v, t], ident)
                    step("pe", "v turned", c, ins)
                    after(pe, "dve", "attn", c)
                    after(pe, "act", "last", c)
                    for v in range(VH):
                        ins = pe.transpose(tile(banks[v // 3], v % 3), attn[:, v, :], ident)
                    step("pe", "attn turned", c, ins)
                    after(pe, "dve", "T0", c)
                    for v in range(VH):
                        ins = pe.transpose(tile((banks[2], banks[7])[v // 3], v % 3), tmat[:, v, :], ident)
                    step("pe", "T turned", c, ins)
                    after(pe, "act", "U0", c)

                def level(lv, c, between):
                    half = slice(0, P // 2)
                    out = lambda bank, v: bank[:, v * P // 2:(v + 1) * P // 2]\
                        .rearrange("p (n b) -> p n b", b=2 ** lv)
                    if lv > 1:
                        after(pe, "dve", f"U {lv - 1}", c)
                    for v in range(VH):
                        ins = pe.matmul(out(banks[0], v), amat[:, v, :], blocks(umat[:, c % 2, v, :], lv, 1),
                                        start=True, stop=True)
                    step("pe", f"Z {lv}", c, ins)
                    between()
                    after(pe, "dve", f"z {lv}", c)
                    if lv > 1:
                        after(pe, "dve", f"T {lv - 1}", c)
                    for v in range(VH):
                        ins = pe.matmul(out(banks[1], v), tmat[:, v, :], blocks(zneg[:, lv % 2, v, :], lv, 1),
                                        start=True, stop=True)
                    step("pe", f"UZ {lv}", c, ins)
                    if lv < LEVELS - 1:
                        for v in range(VH):
                            ins = pe.matmul(out(banks[2], v), zneg[:, lv % 2, v, :], blocks(tmat[:, v, :], lv, 0),
                                            start=True, stop=True)
                        step("pe", f"ZT {lv}", c, ins)

                def recur(lv, c):
                    s2, t = c % 2, slice(c * P, (c + 1) * P)
                    if lv == 1 and c:
                        after(pe, "dve", "state", c - 1)
                        after(pe, "dve", "out", c - 1)
                        for v in range(VH):
                            ins = pe.matmul(tile(banks[3 + v // 3], v % 3), qkv[:, QKH + v // 2, t], state[:, v, :],
                                            start=True, stop=True)
                        step("pe", "kS", c, ins)
                    elif lv == 2:
                        if c:
                            after(pe, "dve", "R", c)
                            after(pe, "act", "norm ln", c - 1)
                        for v in range(VH):
                            ins = pe.matmul(tile(banks[5 + v // 3], v % 3), umat[:, s2, v, :], vbeta[:, s2, v, :],
                                            start=True, stop=True)
                        step("pe", "delta", c, ins)
                    elif lv == 3:
                        after(pe, "pool", "qdec", c)
                        after(pe, "act", "delta", c)
                        for v in range(VH):
                            o = tile(banks[3 + v // 3], v % 3)
                            if c:
                                pe.matmul(o, state[:, v, :], qdec[:, s2, v, :], start=True, stop=False)
                            ins = pe.matmul(o, delta[:, v, :], attn_t[:, s2, v, :], start=c == 0, stop=True)
                        step("pe", "out", c, ins)
                    elif lv == 4 and c < NB - 1:
                        for v in range(VH):
                            ins = pe.matmul(tile(banks[5 + v // 3], v % 3), ktail[:, s2, v, :], delta[:, v, :],
                                            start=True, stop=True)
                        step("pe", "state", c, ins)
                    elif lv == 5:
                        if c < NB - 1:
                            after(pe, "dve", "state", c)
                        after(pe, "act", "square", c)
                        for hf in HALF:
                            ins = pe.matmul(banks[5 + hf][:, 0:3 * P], ones, flat(osq[:, heads(hf), :]),
                                            start=True, stop=True)
                        step("pe", "norm", c, ins)

                for c in range(NB + 1):
                    if c < NB:
                        prepare(c)
                    for lv in LV:
                        between = lambda: recur(lv, c - 1) if c else None
                        if c < NB:
                            level(lv, c, between)
                        else:
                            if lv == 1:
                                after(pe, "dve", f"U {LEVELS - 1}", c - 1)
                            between()
                after(pe, "dve", "lo", NB - 1)

            pe.wait_ge(par_in, 32)
            pe.wait_ge(mem_sum, 1)
            pe.matmul(stats[:, 0:MEM], ones, m_ss[:], start=True, stop=True).then_inc(mem_stat, 1)
            pe.wait_ge(rel_in, 32)
            pe.matmul(mixed[0][0:A_HEADS, 0:WINDOW], relb[:], oneh[:], start=True, stop=True).then_inc(bias_mm, 1)
            for k in range(8):
                layer, part = k // 4, k % 4
                if part == 0:
                    pe.wait_ge(mem_lo, layer + 1)
                if k >= 2:
                    pe.wait_ge(tile_out, k - 1)
                bank = gemm_out[k % 2]
                if part < 2:
                    slab(k, 0, bank[:, 0:MEM], of(mh[:, layer], ml[:, layer]))
                    continue
                pe.wait_ge(lo_cut, k + 1)
                for mt in range(MT):
                    t, o = slice(mt * P, (mt + 1) * P), bank[:, mt * P:(mt + 1) * P]
                    for kk in range(KD):
                        w = slice(kk * P, (kk + 1) * P)
                        hi, lo = wh[:, k % CUT, w], wl[:, k % CUT, w]
                        pe.matmul(o, mh[:, layer, kk, t], hi, start=kk == 0, stop=False)
                        pe.matmul(o, mh[:, layer, kk, t], lo, start=False, stop=False)
                        ins = pe.matmul(o, ml[:, layer, kk, t], hi, start=False, stop=kk == KD - 1)
                ins.then_inc(slab_done, 1)
            norm(0)
            products("in0", of(xh, xl))
            pe.wait_ge(tile_out, TILE0["in0"] + 2)
            for b in range(NB):
                ins = pe.transpose(turned[0][:, b * P:(b + 1) * P], pa[:, 1, b * P:(b + 1) * P], ident)
            ins.then_inc(v_turned, 1)
            pe.wait_ge(tile_out, TILE0["out0"])
            pe.wait_ge(v_tok, 1)
            pe.wait_ge(bias_in, 16 * A_HEADS)
            for n in range(6):
                pe.matmul(banks[2 + n][:], con[:, FLIP, :],
                          bias_rev[:, 2 * n:2 * n + 2, :].rearrange("p a k -> p (a k)"), start=True, stop=True)\
                  .then_inc(bias_mm, 1)
            pe.wait_ge(bias_set, 6)
            attention(0)
            products("out0", of(ch0, cl0))
            norm(1)
            products("gu0", of(xh, xl))
            down(0)
            norm(2)
            products("in1", of(xh, xl))
            pe.wait_ge(tile_out, TILE0["out1"])
            gates()
            after(pe, "dve", "ba scaled")
            attention(1)
            deltanet()
            products("out1", of(ch1, cl1))
            norm(3)
            products("gu1", of(xh, xl))
            down(1)
            norm(4)


def head_order():
    return [kv * AJ + j for j in range(AJ) for kv in range(A_KV)]


def bucket_onehot():
    d = np.arange(WINDOW)
    half = N_BUCKETS // 2
    far = half + (np.log(np.maximum(d, 1).astype(np.float32) / np.float32(half))
                  / np.float32(math.log(MAX_DISTANCE / half)) * np.float32(N_BUCKETS - half)).astype(np.int32)
    bucket = np.where(d < half, d, np.minimum(far, N_BUCKETS - 1))
    out = np.zeros((N_BUCKETS, WINDOW), np.float32)
    out[bucket[::-1], d] = 1.0
    return out


def constant_tiles():
    t, s = np.arange(P)[:, None], np.arange(P)[None, :]
    out = np.zeros((NCONST, P, P), np.float32)
    out[IDENT] = t == s
    out[ONES] = 1.0
    out[FLIP] = t + s == P - 1
    out[TRI] = t <= s
    out[CAUSAL] = np.where(s <= t, 0.0, -BIG)
    out[LEVEL0] = (t % 2 == 1) & (s == t - 1)
    out = np.ascontiguousarray(out.transpose(1, 0, 2))
    for lv in range(1, LEVELS):
        b = 2 ** lv
        column = np.arange(P).reshape(-1, 2, b)[:, 1].reshape(1, -1)
        above = -1.0 * (t // b == column // b - 1)
        out[:, ABOVE + (lv - 1) // 2, (lv - 1) % 2 * (P // 2):][:, :P // 2] = above
    return out


def slabs(w):
    *lead, k, c = w.shape
    w = w.reshape(*lead, k // P, P, c // P, P)
    n = len(lead)
    w = w.transpose(*range(n), n + 2, n + 1, n, n + 3)
    return np.ascontiguousarray(w.reshape(*lead, c // P, P, k))


def lay_out(x, mem, rel_bias, norm_mix_g, norm_mem_g, w_mem_kv, w_out, w_in_a, sinks_a, w_in_b,
            conv_qkv_b, a_log_b, dt_bias_b, out_norm_g_b, norm_ffn_g, w_gate_up, ffn_conv_w,
            ffn_conv_b, w_down, final_norm_g):
    order = head_order()
    feat = lambda a: np.moveaxis(a.reshape(*a.shape[:-1], a.shape[-1] // P, P), -1, 0).reshape(P, -1)
    rows = lambda a: np.broadcast_to(a.reshape(1, -1), (P, a.size))
    params = np.concatenate([
        feat(norm_mix_g), feat(norm_mem_g), feat(norm_ffn_g), feat(final_norm_g), feat(conv_qkv_b[0]),
        feat(ffn_conv_w), feat(ffn_conv_b), feat(out_norm_g_b[0]), rows(sinks_a[0][order]),
        rows(dt_bias_b[0]), rows(a_log_b[0])], axis=1)
    nq, nkv = A_HEADS * DH, A_KV * DH
    wa = w_in_a[0]
    q_cols = np.concatenate([np.arange(hd * DH, (hd + 1) * DH) for hd in order])
    wa = np.concatenate([wa[:, nq:nq + 2 * nkv], wa[:, q_cols], wa[:, nq + 2 * nkv:]], axis=1)
    w_o = np.stack([np.concatenate([w_out[0][q_cols], w_out[0][nq:]]), w_out[1]])
    nb = (NQKV + VH) * P
    wb = w_in_b[0]
    w_ba = wb[:, nb:nb + 2 * VH].reshape(KD, P, 2 * VH).transpose(1, 0, 2)
    wb = np.concatenate([wb[:, :nb], wb[:, nb + 2 * VH:]], axis=1)
    gu = slabs(w_gate_up)
    gu = np.stack([gu[:, :FT], gu[:, FT:]], axis=2).reshape(2, 2 * FT, P, D_MODEL)
    tiles = lambda a: a.T.reshape(KD, P, a.shape[0]).transpose(1, 0, 2)
    return {
        "xT": tiles(x[0]), "memT": tiles(mem[0]), "params": params, "consts": constant_tiles(),
        "rel_bias": rel_bias[:, order], "onehot": bucket_onehot(), "w_mem": slabs(w_mem_kv),
        "w_in_a": slabs(wa), "w_in_b": slabs(wb), "w_ba": w_ba, "w_out": slabs(w_o), "w_gu": gu,
        "w_dn": slabs(w_down),
    }


def kernel(**inputs):
    import concourse.bacc as bacc
    from concourse.bass_utils import run_bass_kernel_spmd

    nc = bacc.Bacc("TRN2", target_bir_lowering=False, num_devices=1)
    laid = lay_out(**{k: np.asarray(v) for k, v in inputs.items()})
    arrays = {name: np.ascontiguousarray(a) for name, a in laid.items()}
    args = [nc.dram_tensor(name, a.shape, mybir.dt.from_np(a.dtype), kind="ExternalInput").ap()
            for name, a in arrays.items()]
    args.append(nc.dram_tensor("outT", (P, KD, SEQ), F32, kind="ExternalOutput").ap())
    program(nc, *args)
    r = run_bass_kernel_spmd(nc, [arrays], core_ids=[0])
    out = r.results[0]["outT"].reshape(P, KD, SEQ).transpose(2, 1, 0).reshape(1, SEQ, D_MODEL)
    return np.ascontiguousarray(out)
```

```python
import math
from contextlib import ExitStack

import concourse.bass as bass
import concourse.mybir as mybir
import numpy as np

F32 = mybir.dt.float32
F32R = mybir.dt.float32r
BF16 = mybir.dt.bfloat16
ACT = mybir.ActivationFunctionType
ALU = mybir.AluOpType
AX = mybir.AxisListType

P = 128
D_MODEL, SEQ, MEM, D_FF = 1024, 512, 256, 2816
KD = D_MODEL // P
NB = SEQ // P
MT = MEM // P
FT = D_FF // P
EPS = 1e-6
A_HEADS, A_KV, DH = 12, 2, 64
AJ = A_HEADS // A_KV
N_BUCKETS, MAX_DISTANCE, WINDOW = 32, 128, 128
X_HEADS = 4
QKH, VH, DK = 3, 6, 128
B_TAPS, F_TAPS = 4, 3
NQKV = 2 * QKH + VH
LEVELS = 7
BIG = 1e30

RAW = 4
CUT = 2
DOWN_K = [6, 6, 5, 5]
DOWN_AT = [sum(DOWN_K[:i]) for i in range(4)]

_widths = [("mix_g", 2 * KD), ("mem_g", 2 * KD), ("ffn_g", 2 * KD), ("fin_g", KD),
           ("conv_b", B_TAPS * NQKV), ("conv_f", 2 * F_TAPS * FT), ("bias_f", 2 * FT), ("out_g", 1),
           ("sinks", A_HEADS), ("dt_bias", VH), ("a_log", VH)]
COL = {}
_at = 0
for _name, _w in _widths:
    COL[_name] = _at
    _at += _w
NPAR = _at

IDENT, ONES, TRI, CAUSAL, FLIP, LEVEL0 = range(6)
ABOVE = LEVEL0 + 1
NCONST = ABOVE + LEVELS // 2
BIAS_PAD = 384

STREAM = [("mem0", 4), ("mem1", 4), ("in0", 10), ("out0", KD), ("gu0", 2 * FT), ("dn0", 4 * KD),
          ("in1", 20), ("out1", KD), ("gu1", 2 * FT), ("dn1", 4 * KD)]
SLAB0, TILE0 = {}, {}
_n = _g = 0
for _name, _c in STREAM:
    SLAB0[_name], TILE0[_name] = _n, _g
    _n += _c
    _g += _c // 4 if _name[:2] == "dn" else _c
SLABS = _n


def slab_k(n):
    for name, count in STREAM:
        if SLAB0[name] <= n < SLAB0[name] + count:
            return DOWN_K[(n - SLAB0[name]) % 4] if name[:2] == "dn" else KD
    raise ValueError(n)


def program(nc, xT, memT, params, consts, rel_bias, onehot, w_mem, w_in_a, w_in_b, w_ba, w_out, w_gu,
            w_dn, outT):
    ctx = ExitStack()
    with ctx:
        def sb(name, shape, dt=F32, at=None):
            return (at or ctx).enter_context(nc.sbuf_tensor(name, shape, dt))

        def psum(name):
            return ctx.enter_context(nc.psum_tensor(name, [P, 512], F32))

        def sem(name):
            return ctx.enter_context(nc.semaphore(name))

        h = sb("h", [P, KD, SEQ])
        with ExitStack() as at:
            decay, amat, tmat, attn = (sb(x, [P, VH, P], at=at) for x in ("decay", "amat", "tmat", "attn"))
            zneg, umat, attn_t = (sb(x, [P, 2, VH, P], at=at) for x in ("zneg", "umat", "attn_t"))
        with ExitStack() as at:
            s1 = sb("s1", [P, 3, 4, 2 * P], at=at)
            pt1 = sb("pt1", [P, 2, 2, 4, P], at=at)
            small1 = sb("small1", [P, 3, 6, 4], at=at)
        xh = sb("xh", [P, KD, SEQ], F32R)
        xl = sb("xl", [P, KD, SEQ], F32R)
        with ExitStack() as at:
            osq, og = sb("osq", [P, VH, P], at=at), sb("og", [P, VH, P], at=at)
        sq = sb("sq", [P, SEQ])
        rms = sq
        ssq = sb("ssq", [P, SEQ])
        rinv = sb("rinv", [P, SEQ])
        raw = sb("raw", [P, RAW, KD * P])
        wh = sb("wh", [P, CUT, KD * P], F32R)
        wl = sb("wl", [P, CUT, KD * P], F32R)
        wba = sb("wba", [P, KD, 2 * VH])
        wbag = sb("wbag", [P, KD, 2 * VH])
        par = sb("par", [P, NPAR])
        con = sb("con", [P, NCONST, P])
        eps = sb("eps", [P, 1])
        table = sb("table", [P, 1])
        mem_k = sb("mem_k", [P, 2, MT, MEM])
        mem_v = sb("mem_v", [P, 2, MT, 2 * P])
        ident, ones = con[:, IDENT, :], con[:, ONES, :]

        def col(name, i=0, n=1):
            a = COL[name] + i
            return par[:, a:a + n] if isinstance(a, int) else par[:, bass.ts(a, 1)]

        with ExitStack() as at:
            mT = sb("mT", [P, KD, MEM], at=at)
            m_sq = sb("m_sq", [P, KD, MEM], at=at)
            m_ss = sb("m_ss", [P, MEM], at=at)
            m_rms = sb("m_rms", [P, MEM], at=at)
            mn = sb("mn", [P, 2, KD, MEM], at=at)
            mh = sb("mh", [P, 2, KD, MEM], F32R, at=at)
            ml = sb("ml", [P, 2, KD, MEM], F32R, at=at)
            relb = sb("relb", [N_BUCKETS, A_HEADS], at=at)
            oneh = sb("oneh", [N_BUCKETS, WINDOW], at=at)
            brow = sb("brow", [A_HEADS, BIAS_PAD], at=at)
            bias_rev = sb("bias_rev", [P, A_HEADS, 2 * P], at=at)
        with ExitStack() as at:
            ch0 = sb("ch0", [P, KD, SEQ], F32R, at=at)
            cl0 = sb("cl0", [P, KD, SEQ], F32R, at=at)
            pa = sb("pa", [P, 10, SEQ], at=at)
            vtok = sb("vtok", [P, NB, P], at=at)
            s0 = sb("s0", [P, 3, 4, 2 * P], at=at)
            pt0 = sb("pt0", [P, 2, 2, 4, P], at=at)
            small0 = sb("small0", [P, 3, 6, 4], at=at)
            sb("under_bias_rev", [P, 3 * P * 2 * 3 + 1024], at=at)
            bias = sb("bias", [P, A_HEADS, 2 * P], at=at)
        with ExitStack() as at:
            ah = sb("ah", [P, FT, SEQ], F32R, at=at)
            al = sb("al", [P, FT, SEQ], F32R, at=at)
            graw = sb("graw", [P, 2, SEQ + 2], at=at)
            gacc = sb("gacc", [P, 2, SEQ], at=at)
            gsil = sb("gsil", [P, 2, SEQ], at=at)
            gup = sb("gup", [P, 2, SEQ], at=at)
        with ExitStack() as at:
            ch1 = sb("ch1", [P, KD, SEQ], F32R, at=at)
            cl1 = sb("cl1", [P, KD, SEQ], F32R, at=at)
            zt = sb("zt", [P, 8, SEQ], at=at)
            qkv = sb("qkv", [P, NQKV, SEQ], at=at)
            with ExitStack() as early:
                craw = sb("craw", [P, 2, SEQ + 3], at=early)
                cacc = sb("cacc", [P, 2, SEQ], at=early)
            gate = sb("gate", [P, 12, NB, VH], at=at)
            tail = sb("tail", [P, 2, VH], at=at)
            ba = sb("ba", [P, NB, 2 * VH], at=at)
            last = sb("last", [P, 2, VH], at=at)
            state, delta = (sb(x, [P, VH, P], at=at) for x in ("state", "delta"))
            qdec, vbeta, ktail = (sb(x, [P, 2, VH, P], at=at) for x in ("qdec", "vbeta", "ktail"))
        concat = {0: (ch0, cl0), 1: (ch1, cl1)}
        softmax_bufs = {0: (s0, pt0, small0), 1: (s1, pt1, small1)}
        MAXI, NEG, TOTAL, INV, SINK_D, SINK_E = range(6)
        LOGIT, ABS, EXP_ABS, EXP_B, EXP_A, LN, BETA, SOFT, NEG_G, GC, EXP_GC, NBE = range(12)

        banks = [psum(f"bank{i}") for i in range(8)]
        SELF_TILES = list(range(A_HEADS // 2))
        gemm_out = banks[0:2]
        score_banks = [banks[2:4], banks[0:2]]
        turned = banks[4:6]
        mixed = banks[6:8]
        stats = banks[7]
        NEGCUM = (banks[7], banks[2])
        TURNED_T = (banks[0], banks[6])
        WAIT_T0, WAIT_U0, WAIT_Z, WAIT_L2, WAIT_LAST = 14, 4, 3, 20, 5

        par_in, x_in, mem_in, rel_in, ba_in = (sem(x) for x in ("par_in", "x_in", "mem_in", "rel_in", "ba_in"))
        w_in = [sem(f"w_in{i}") for i in range(RAW)]
        hi_cut, lo_cut = sem("hi_cut"), sem("lo_cut")
        slab_done = sem("slab_done")
        tile_out = sem("tile_out")
        sq_ready, sq_summed = sem("sq_ready"), sem("sq_summed")
        x_hi, x_lo = sem("x_hi"), sem("x_lo")
        stat_sum, stat_root, r_ready = sem("stat_sum"), sem("stat_root"), sem("r_ready")
        mem_sq, mem_sum, mem_stat, mem_root = (sem(x) for x in ("mem_sq", "mem_sum", "mem_stat", "mem_root"))
        mem_norm, mem_hi, mem_lo = sem("mem_norm"), sem("mem_hi"), sem("mem_lo")
        bias_mm, bias_row, bias_out, bias_in = (sem(x) for x in ("bias_mm", "bias_row", "bias_out", "bias_in"))
        bias_set = sem("bias_set")
        eps_set, v_turned, v_tok = sem("eps_set"), sem("v_turned"), sem("v_tok")
        sc_ready, max_ready, p_ready, pn_ready = (sem(x) for x in ("sc_ready", "max_ready", "p_ready", "pn_ready"))
        tp_ready, pt_ready, ov_ready = sem("tp_ready"), sem("pt_ready"), sem("ov_ready")
        c_hi, c_lo = sem("c_hi"), sem("c_lo")
        tap0, conv_ready, silu_ready = sem("tap0"), sem("conv_ready"), sem("silu_ready")
        a_ready, a_hi, a_lo = sem("a_ready"), sem("a_hi"), sem("a_lo")
        ba_gain = sem("ba_gain")
        d_pe, d_act, d_dve, d_pool = sem("d_pe"), sem("d_act"), sem("d_dve"), sem("d_pool")
        v_step, tap_step = sem("v_step"), sem("tap_step")
        out_ready, out_sent = sem("out_ready"), sem("out_sent")
        bias_rows = nc.dram_tensor("bias_rows", [A_HEADS, BIAS_PAD], F32, kind="Internal").ap()

        def gain(e, m):
            name = ("mix_g", "ffn_g", "mix_g", "ffn_g", "fin_g")[e]
            return col(name, m + (0 if e == 4 else (e // 2) * KD))

        def row(t, m):
            return t[:, m, :] if isinstance(m, int) else t[:, bass.ts(m, 1), :].rearrange("p a t -> p (a t)")

        groups = {0: [("self", b, jp) for b in range(NB) for jp in range(AJ // 2)]
                  + [("cross", b, None) for b in range(NB)],
                  1: [("cross", b, None) for b in range(NB)]}
        GROUP0 = {0: 0, 1: len(groups[0])}
        CONV0 = {"gu0": 0, "in1": FT, "gu1": FT + NQKV}

        L2 = range(2 * QKH)
        LV = range(1, LEVELS)
        HALF = range(2)
        ENGINE_STEP = {"pe": d_pe, "act": d_act, "dve": d_dve, "pool": d_pool}
        BEFORE = {
            "pe": ["ba", "ba turned", "l2 0", "l2 1", "l2 2", "cumsum", "l2 3", "l2 4", "l2 5", "negcum"],
            "act": (["gate abs", "gate exp", "gate ln"]
                    + [f"l2 {x} {j}" for x in ("ln", "inverse") for j in L2]
                    + ["exp cumsum", "decay", "grow", "last", "tail"]),
            "dve": (["ba scaled", "ba", "gate in", "beta", "g", "cumsum", "NG", "log decay", "tail"]
                    + [f"l2 {j}" for j in L2] + ["nbe"]),
            "pool": [f"l2 square {j}" for j in L2]}
        FINISH = "finish"
        PREPARE = {
            "pe": ["kk", "k turned", "qk", "T turned", "attn turned", "v turned"],
            "act": ["ktail", "U0", "attnT"],
            "dve": ["A", "T0", "attn", FINISH, "vbeta"],
            "pool": ["qdec"]}
        FINISHED = {"pe": [], "act": [], "dve": ["out"], "pool": []}
        LATER = {"pe": {}, "act": {3: ["hi"]}, "dve": {2: ["gated"], 3: ["lo"]}, "pool": {}}
        AHEAD = {"pe": {6: ["negcum"]}, "act": {6: ["decay", "grow", "last", "tail"]},
                 "dve": {5: ["NG"], 6: ["log decay", "tail"]}, "pool": {}}
        LEVEL = {"pe": ["Z", "UZ", "ZT"], "act": [], "dve": ["z", "U", "T"], "pool": ["clear"]}
        RECUR = {
            "pe": {1: ["kS"], 2: ["delta"], 3: ["out"], 4: ["state"], 5: ["norm"]},
            "act": {2: ["delta"], 3: ["square"], 5: ["norm ln", "norm inverse"]},
            "dve": {1: ["R"], 4: ["state"]},
            "pool": {}}
        AFTER_FIRST = {"pe": 1, "act": 0, "dve": 3, "pool": 1}

        def exists(name, lv, c):
            return not (name in ("kS", "R") and c == 0 or name == "state" and c == NB - 1
                        or name in ("ZT", "T") and lv == LEVELS - 1)

        NUMBER = {}
        for who in ENGINE_STEP:
            names = [(x, None) for x in BEFORE[who]]
            names = [(x, 0 if x in sum(AHEAD[who].values(), []) else None) for x, _ in names]
            for c in range(NB + 1):
                finish = [(x, c - 2) for x in FINISHED[who] if c > 1]
                for x in PREPARE[who]:
                    names += (finish if x == FINISH else [(x, c)]) if c < NB else []
                names += finish if c == NB else []
                names += [("silu z", 0)] if c == 0 and who == "act" else []
                for lv in LV:
                    level = [(f"{x} {lv}", c) for x in LEVEL[who] if c < NB and exists(x, lv, c)]
                    cut_at = 1 if lv == LEVELS - 1 and level else AFTER_FIRST[who]
                    names += level[:cut_at]
                    names += [(x, c + 1) for x in AHEAD[who].get(lv, []) if c + 1 < NB]
                    names += [(x, c - 1) for x in RECUR[who].get(lv, []) if c and exists(x, None, c - 1)]
                    names += level[cut_at:]
                    names += [(x, c - 2) for x in LATER[who].get(lv, []) if c > 1]
            names += [(x, NB - 1) for x in FINISHED[who] + sum(LATER[who].values(), [])]
            for n, x in enumerate(names):
                NUMBER[who, x] = n + 1
        told = dict.fromkeys(ENGINE_STEP, 0)

        def step(who, name, c, ins):
            told[who] += 1
            assert told[who] == NUMBER[who, (name, c)], (who, name, c)
            ins.then_inc(ENGINE_STEP[who], 1)

        def after(eng, who, name, c=None):
            eng.wait_ge(ENGINE_STEP[who], NUMBER[who, (name, c)])

        def flat(t):
            return t.rearrange("p a t -> p (a t)")

        def l2_tile(j):
            return (qdec, vbeta)[j // QKH][:].rearrange("p a v t -> p (a v t)")[:, (j % QKH) * SEQ:(j % QKH + 1) * SEQ]

        def third(bank):
            return bank[:, 0:3 * P].rearrange("p (a t) -> p a t", a=3)

        def heads(hf):
            return slice(3 * hf, 3 * hf + 3)

        def blocks(t, lv, odd):
            b = 2 ** lv
            if len(t.shape) == 3:
                return t.rearrange("p h (n two b) -> p h n two b", two=2, b=b)[:, :, :, odd, :]
            return t.rearrange("p (n two b) -> p n two b", two=2, b=b)[:, :, odd, :]

        def packed(bank, lv):
            return bank[:, 0:3 * P].rearrange("p (h n b) -> p h n b", h=VH, b=2 ** lv)

        def slab_steps(eng, name, cut, post, take=lambda j, i: None):
            n0, count = SLAB0[name], dict(STREAM)[name]
            per = 8 if name[:2] == "dn" else 4
            trips = count // per

            def trip(i, last):
                for j in range(per):
                    take(j, i)
                    if not last:
                        cut(n0 + j + CUT, per * i)
                    elif n0 + per * i + j + CUT < SLABS:
                        cut(n0 + per * i + j + CUT)
                    post(j, i)
            if count % per == 0:
                with eng.Fori(0, trips - 1) as i:
                    trip(i, False)
                trip(trips - 1, True)
            else:
                with eng.Fori(0, trips) as i:
                    trip(i, False)
                for k in range(per * trips, count):
                    take(k, 0)
                    cut(n0 + k + CUT)
                    post(k, 0)

        block = ctx.enter_context(nc.Block())

        @block.sync
        def _(sp):
            def load_slab(n, src, it=0):
                if n >= RAW:
                    sp.wait_ge(lo_cut, n - RAW + 1 + 4 * it)
                sp.dma_start(raw[:, n % RAW, :slab_k(n) * P], src).then_inc(w_in[n % RAW], 16)

            def stream(name, src):
                count = dict(STREAM)[name]
                if count > 4:
                    with sp.Fori(0, count // 4) as i:
                        at = [sp.snap(4 * i + j) for j in range(4)]
                        for j in range(4):
                            load_slab(SLAB0[name] + j, src(at[j]), i)
                for k in range(count - count % 4 if count > 4 else 0, count):
                    load_slab(SLAB0[name] + k, src(k))

            def stream_down(layer):
                with sp.Fori(0, KD) as i:
                    for j in range(4):
                        a = DOWN_AT[j] * P
                        load_slab(SLAB0[f"dn{layer}"] + j, w_dn[layer, i, :, a:a + DOWN_K[j] * P], i)

            sp.dma_start(mT[:], memT).then_inc(mem_in, 16)
            sp.dma_start(con[:], consts).then_inc(par_in, 16)
            sp.dma_start(par[:], params).then_inc(par_in, 16)
            stream("mem0", lambda k: w_mem[0, k])
            sp.dma_start(h[:], xT).then_inc(x_in, 16)
            sp.dma_start(relb[:], rel_bias).then_inc(rel_in, 16)
            sp.dma_start(oneh[:], onehot).then_inc(rel_in, 16)
            sp.dma_start(wba[:], w_ba).then_inc(ba_in, 16)
            stream("mem1", lambda k: w_mem[1, k])
            stream("in0", lambda k: w_in_a[k])
            stream("out0", lambda k: w_out[0, k])
            stream("gu0", lambda k: w_gu[0, k])
            stream_down(0)
            stream("in1", lambda k: w_in_b[k])
            stream("out1", lambda k: w_out[1, k])
            stream("gu1", lambda k: w_gu[1, k])
            stream_down(1)
            for m in range(KD):
                sp.wait_ge(out_ready, m + 1)
                sp.dma_start(outT[:, m, :], h[:, m, :]).then_inc(out_sent, 16)
            sp.wait_ge(out_sent, 16 * KD)

        @block.gpsimd
        def _(pool):
            pool.wait_ge(bias_row, 1)
            pool.dma_start(bias_rows, brow[:]).then_inc(bias_out, 16)
            pool.wait_ge(bias_out, 16)
            for s in range(A_HEADS):
                rows = bass.AP(bias_rows.tensor, s * BIAS_PAD, [[1, P], [1, 2 * P]])
                pool.dma_start(bias_rev[:, s, :], rows).then_inc(bias_in, 16)

            pool.wait_ge(silu_ready, CONV0["in1"] + NQKV)
            for j in L2:
                step("pool", f"l2 square {j}", None, pool.tensor_tensor(l2_tile(j), qkv[:, j, :], qkv[:, j, :], ALU.mult))
            for c in range(NB):
                t = slice(c * P, (c + 1) * P)
                after(pool, "act", "grow", c)
                if c == 0:
                    after(pool, "dve", f"l2 {QKH - 1}")
                for j in range(QKH):
                    q = qkv[:, j, t].unsqueeze(1).to_broadcast([P, 2, P])
                    two = qdec[:, c % 2, 2 * j:2 * j + 2, :]
                    ins = pool.tensor_tensor(two, q, two, ALU.mult)
                step("pool", "qdec", c, ins)
                for lv in LV:
                    if lv > 2:
                        after(pool, "pe", f"ZT {lv - 2}", c)
                    elif c:
                        after(pool, "pe", f"UZ {LEVELS - 1}" if lv == 2 else f"ZT {LEVELS - 2}", c - 1)
                    step("pool", f"clear {lv}", c, pool.memset(zneg[:, lv % 2], 0.0))

        @block.scalar
        def _(act):
            def cut_hi(n, more=0):
                act.wait_ge(w_in[n % RAW], 16 * (n // RAW + 1) + (16 // RAW) * more)
                if n >= CUT:
                    act.wait_ge(slab_done, n - CUT + 1 + more)
                w = slab_k(n) * P
                act.activation(wh[:, n % CUT, :w], raw[:, n % RAW, :w], ACT.Copy).then_inc(hi_cut, 1)

            def square_and_hi(e, m):
                if not (e == 0 and isinstance(m, int) and m == 0):
                    act.wait_ge(sq_summed, KD * e + m)
                act.activation(sq[:], row(h, m), ACT.Square).then_inc(sq_ready, 1)
                if e < 4:
                    act.activation(row(xh, m), row(h, m), ACT.Copy, scale=gain(e, m)).then_inc(x_hi, 1)

            def root(e):
                act.wait_ge(stat_sum, e + 1)
                act.activation(rms[:], stats[:], ACT.Sqrt, bias=eps[:], scale=1.0 / D_MODEL)\
                   .then_inc(stat_root, 1)

            def residual(name, e):
                g0 = TILE0[name]

                def post(j, i):
                    if name[:2] == "dn":
                        if j % 4 == 3:
                            act.wait_ge(tile_out, g0 + j // 4 + 1 + 2 * i)
                            square_and_hi(e, 2 * i + j // 4)
                    else:
                        act.wait_ge(tile_out, g0 + j + 1 + 4 * i)
                        square_and_hi(e, 4 * i + j)
                slab_steps(act, name, cut_hi, post)

            def attention(layer):
                s, pt, small = softmax_bufs[layer]
                ch = concat[layer][0]
                n, g0 = len(groups[layer]), GROUP0[layer]
                for t in range(n + 3):
                    if 2 <= t < n + 2:
                        u = t - 2
                        kind, b, _ = groups[layer][u]
                        act.wait_ge(tp_ready, g0 + u + 1)
                        if u >= 2:
                            act.wait_ge(ov_ready, g0 + u - 1)
                        for kc in range(1 if kind == "self" and b == 0 else 0, 2):
                            ins = act.activation(pt[:, u % 2, kc].rearrange("p a q -> p (a q)"),
                                                 turned[kc][:], ACT.Copy)
                        ins.then_inc(pt_ready, 1)
                    if t < n:
                        kind, b, jp = groups[layer][t]
                        lo = P if kind == "self" and b == 0 else 0
                        sm = small[:, t % 3]
                        act.wait_ge(max_ready, g0 + t + 1)
                        if kind == "self":
                            act.activation(sm[:, SINK_E, :], sm[:, SINK_D, :], ACT.Exp)
                        for i in range(4):
                            src = s[:, t % 3, i, lo:] if kind == "self" else \
                                score_banks[t % 2][i // 2][:, (i % 2) * 256:(i % 2) * 256 + 256]
                            ins = act.activation(s[:, t % 3, i, lo:], src, ACT.Exp, bias=sm[:, NEG, i:i + 1],
                                                 accum_out=sm[:, TOTAL, i:i + 1])
                        ins.then_inc(p_ready, 1)
                    if t >= 3:
                        u = t - 3
                        kind, b, jp = groups[layer][u]
                        first = 2 * jp if kind == "self" else 6
                        act.wait_ge(ov_ready, g0 + u + 1)
                        act.activation(ch[:, first:first + 2, b * P:(b + 1) * P],
                                       mixed[u % 2][:, 0:2 * P].rearrange("p (a q) -> p a q", a=2),
                                       ACT.Copy).then_inc(c_hi, 1)

            def mixer(layer):
                name = f"gu{layer}"
                g0, f0 = TILE0[name], layer * FT

                def post(j, i):
                    q, f = j // 2, 2 * i + j // 2
                    if j % 2 == 0:
                        act.wait_ge(tile_out, g0 + j + 1 + 4 * i)
                        act.activation(gacc[:, q, :], graw[:, q, 0:SEQ], ACT.Identity,
                                       bias=col("bias_f", f + f0),
                                       scale=col("conv_f", f + layer * F_TAPS * FT)).then_inc(tap0, 1)
                        act.wait_ge(conv_ready, CONV0[name] + q + 1 + 2 * i)
                        act.activation(gsil[:, q, :], gacc[:, q, :], ACT.Silu).then_inc(silu_ready, 1)
                    else:
                        act.wait_ge(a_ready, f0 + q + 1 + 2 * i)
                        act.activation(row(ah, f), gup[:, q, :], ACT.Copy).then_inc(a_hi, 1)
                slab_steps(act, name, cut_hi, post)

            def deltanet():
                step("act", "gate ln", None, act.activation(gate[:, LN], gate[:, EXP_ABS], ACT.Ln, bias=ones[:, 0:1]))
                for j in L2:
                    after(act, "pe", f"l2 {j}")
                    step("act", f"l2 ln {j}", None, act.activation(l2_tile(j), banks[j][:], ACT.Ln, bias=eps[:]))
                for j in L2:
                    after(act, "act", f"l2 ln {j}")
                    step("act", f"l2 inverse {j}", None, act.activation(l2_tile(j), l2_tile(j), ACT.Exp, scale=-0.5))
                after(act, "dve", "cumsum")
                step("act", "exp cumsum", None, act.activation(gate[:, EXP_GC], gate[:, GC], ACT.Exp))

                def ahead(lv, c):
                    if lv < LEVELS - 1:
                        return
                    s2 = c % 2
                    after(act, "dve", "log decay", c)
                    step("act", "decay", c, act.activation(decay[:], decay[:], ACT.Exp))
                    after(act, "dve", "tail", c)
                    if c == 0:
                        after(act, "dve", f"l2 {QKH - 1}")
                    for hf, bank in enumerate(NEGCUM):
                        ins = act.activation(flat(qdec[:, s2, heads(hf), :]), bank[:, 0:3 * P], ACT.Exp, scale=-1.0)
                    step("act", "grow", c, ins)
                    for hf, bank in enumerate(NEGCUM):
                        ins = act.activation(last[:, s2, heads(hf)], third(bank)[:, :, P - 1], ACT.Exp, scale=-1.0)
                    step("act", "last", c, ins)
                    step("act", "tail", c, act.activation(tail[:, 1, :], tail[:, 0, :], ACT.Exp, scale=-1.0))

                def prepare(c):
                    s2 = c % 2
                    after(act, "act", "tail", c)
                    after(act, "pe", "k turned", c)
                    for v in range(VH):
                        ins = act.activation(ktail[:, s2, v, :], banks[5][:, (v // 2) * P:(v // 2 + 1) * P],
                                             ACT.Copy, scale=tail[:, 1, v:v + 1])
                    step("act", "ktail", c, ins)
                    after(act, "pe", "T turned", c)
                    for hf, bank in enumerate(TURNED_T):
                        ins = act.activation(flat(umat[:, s2, heads(hf), :]), bank[:, 0:3 * P], ACT.Copy)
                    step("act", "U0", c, ins)
                    after(act, "pe", "attn turned", c)
                    for hf, bank in enumerate(NEGCUM):
                        ins = act.activation(flat(attn_t[:, s2, heads(hf), :]), bank[:, 0:3 * P], ACT.Copy)
                    step("act", "attnT", c, ins)
                    if c == 0:
                        act.wait_ge(tile_out, TILE0["out1"])
                        step("act", "silu z", c, act.activation(zt[:, 0:VH, :], zt[:, 0:VH, :], ACT.Silu))

                def finish(c):
                    after(act, "dve", "gated", c)
                    step("act", "hi", c, act.activation(ch1[:, 0:VH, c * P:(c + 1) * P], og[:], ACT.Copy))

                def recur(lv, c):
                    if lv == 2:
                        after(act, "pe", "delta", c)
                        for hf in HALF:
                            ins = act.activation(flat(delta[:, heads(hf), :]), banks[5 + hf][:, 0:3 * P], ACT.Copy)
                        step("act", "delta", c, ins)
                        if c == NB - 1:
                            act.activation(table[:], ones[:, 0:1], ACT.Ln)
                    elif lv == 3:
                        after(act, "pe", "out", c)
                        for hf in HALF:
                            ins = act.activation(flat(osq[:, heads(hf), :]), banks[3 + hf][:, 0:3 * P], ACT.Square)
                        step("act", "square", c, ins)
                    elif lv == 5:
                        after(act, "pe", "norm", c)
                        for hf in HALF:
                            ins = act.activation(flat(osq[:, heads(hf), :]), banks[5 + hf][:, 0:3 * P], ACT.Ln,
                                                 bias=eps[:], scale=1.0 / DK)
                        step("act", "norm ln", c, ins)
                        after(act, "act", "norm ln", c)
                        step("act", "norm inverse", c, act.activation(osq[:], osq[:], ACT.Exp, scale=-0.5))

                ahead(LEVELS - 1, 0)
                for c in range(NB + 1):
                    if c < NB:
                        prepare(c)
                    for lv in LV:
                        if c + 1 < NB:
                            ahead(lv, c + 1)
                        if c:
                            recur(lv, c - 1)
                        if c > 1 and lv == 3:
                            finish(c - 2)
                finish(NB - 1)

            act.wait_ge(mem_in, 16)
            act.activation(m_sq[:], mT[:], ACT.Square).then_inc(mem_sq, 1)
            cut_hi(0)
            cut_hi(1)
            act.wait_ge(mem_stat, 1)
            act.wait_ge(eps_set, 1)
            act.activation(m_rms[:], stats[:, 0:MEM], ACT.Sqrt, bias=eps[:], scale=1.0 / D_MODEL)\
               .then_inc(mem_root, 1)
            for i in range(4):
                layer, ks = i // 2, slice(i % 2 * (KD // 2), (i % 2 + 1) * (KD // 2))
                act.wait_ge(mem_norm, i + 1)
                act.activation(mh[:, layer, ks], mn[:, layer, ks], ACT.Copy).then_inc(mem_hi, 1)
            act.wait_ge(x_in, 16)
            act.wait_ge(par_in, 32)
            for k in range(KD):
                cut_hi(k + CUT)
                square_and_hi(0, k)
            root(0)
            slab_steps(act, "in0", cut_hi, lambda j, i: None)
            attention(0)
            residual("out0", 1)
            root(1)
            mixer(0)
            residual("dn0", 2)
            root(2)

            def conv_post(k, i):
                act.wait_ge(tile_out, TILE0["in1"] + k + 1 + 4 * i)
                act.activation(cacc[:, k % 2, :], craw[:, k % 2, 0:SEQ], ACT.Copy,
                               scale=col("conv_b", 4 * i + k)).then_inc(tap0, 1)
                act.wait_ge(conv_ready, CONV0["in1"] + k + 1 + 4 * i)
                act.activation(row(qkv, 4 * i + k), cacc[:, k % 2, :], ACT.Silu).then_inc(silu_ready, 1)
            n0 = SLAB0["in1"]
            with act.Fori(0, NQKV // 4) as i:
                act.activation(table[:], ones[:, 0:1], ACT.Silu)
                for j in range(4):
                    cut_hi(n0 + j + CUT, 4 * i)
                    conv_post(j, i)
            for k in range(NQKV, 20):
                cut_hi(n0 + k + CUT)
            after(act, "dve", "gate in")
            step("act", "gate abs", None, act.activation(gate[:, ABS], gate[:, LOGIT], ACT.Abs))
            after(act, "act", "gate abs")
            act.activation(gate[:, EXP_ABS], gate[:, ABS], ACT.Exp, scale=-1.0)
            act.activation(gate[:, EXP_A, 0, :], col("a_log", 0, VH), ACT.Exp)
            step("act", "gate exp", None, act.activation(gate[:, EXP_B], ba[:, :, 0:VH], ACT.Exp, scale=-1.0))
            attention(1)
            deltanet()
            residual("out1", 3)
            root(3)
            mixer(1)
            residual("dn1", 4)
            root(4)

        @block.vector
        def _(dve):
            steps = [0]

            def then_wait(ins):
                steps[0] += 1
                ins.then_inc(v_step, 1)
                dve.wait_ge(v_step, steps[0])

            def cut_lo(n, more=0):
                dve.wait_ge(hi_cut, n + 1 + more)
                w = slab_k(n) * P
                dve.tensor_tensor(wl[:, n % CUT, :w], raw[:, n % RAW, :w], wh[:, n % CUT, :w].bitcast(F32),
                                  ALU.subtract).then_inc(lo_cut, 1)

            def sum_and_lo(e, m):
                dve.wait_ge(sq_ready, KD * e + 1 + m)
                dve.tensor_tensor(ssq[:], ssq[:], sq[:], ALU.add).then_inc(sq_summed, 1)
                if e < 4:
                    dve.wait_ge(x_hi, KD * e + 1 + m)
                    dve.scalar_tensor_tensor(out=row(xl, m), in0=row(h, m), scalar=gain(e, m),
                                             in1=row(xh, m).bitcast(F32), op0=ALU.mult, op1=ALU.subtract)\
                       .then_inc(x_lo, 1)

            def inverse_rms(e):
                dve.wait_ge(stat_root, e + 1)
                dve.reciprocal(rinv[:], rms[:]).then_inc(r_ready, 1)
                dve.wait_ge(r_ready, e + 1)

            def residual(name, e):
                n0, g0 = SLAB0[name], TILE0[name]
                then_wait(dve.memset(ssq[:], 0.0))

                down = name[:2] == "dn"

                def which(j, i):
                    return (2 * i + j // 4, j // 4) if down else (4 * i + j, j)

                def add(j, i):
                    if down and j % 4 < 3:
                        return
                    m, tile = which(j, i)
                    dve.wait_ge(slab_done, n0 + j + 1 + (8 if down else 4) * i)
                    dve.tensor_tensor(row(h, m), gemm_out[(g0 + tile) % 2][:], row(h, m), ALU.add)\
                       .then_inc(tile_out, 1)

                def post(j, i):
                    if down and j % 4 < 3:
                        return
                    m, tile = which(j, i)
                    dve.wait_ge(tile_out, g0 + tile + 1 + (2 if down else 4) * i)
                    dve.wait_ge(sq_summed, KD * e + m)
                    sum_and_lo(e, m)
                slab_steps(dve, name, cut_lo, post, add)

            def take(name, k, i, out):
                dve.wait_ge(slab_done, SLAB0[name] + k + 1 + 4 * i)
                dve.tensor_tensor(out, gemm_out[(TILE0[name] + k) % 2][:], rinv[:], ALU.mult)\
                   .then_inc(tile_out, 1)

            def taps(name, raw_tile, acc, k, i, weight, count):
                c0 = CONV0[name]
                per = 2 if name[:2] == "gu" else 4
                dve.wait_ge(tap0, c0 + k + 1 + per * i)
                for tap in range(1, count):
                    ins = dve.scalar_tensor_tensor(out=acc, in0=raw_tile[:, tap:tap + SEQ], scalar=weight(tap),
                                                   in1=acc, op0=ALU.mult, op1=ALU.add)
                    if tap < count - 1:
                        ins.then_inc(tap_step, 1)
                        dve.wait_ge(tap_step, tap_steps[name] + (count - 2) * k + tap + (count - 2) * per * i)
                ins.then_inc(conv_ready, 1)

            tap_steps = {"gu0": 0, "in1": FT, "gu1": FT + 2 * NQKV}

            def attention(layer):
                s, pt, small = softmax_bufs[layer]
                ch, cl = concat[layer]
                n, g0 = len(groups[layer]), GROUP0[layer]
                for t in range(n + 3):
                    if t < n:
                        kind, b, jp = groups[layer][t]
                        lo = P if kind == "self" and b == 0 else 0
                        sm = small[:, t % 3]
                        dve.wait_ge(sc_ready, g0 + t + 1)
                        if t >= 3:
                            dve.wait_ge(tp_ready, g0 + t - 2)
                        if kind == "self":
                            for i in range(4):
                                slot = 2 * (2 * jp + i % 2) + i // 2
                                src = score_banks[t % 2][i // 2][:, (i % 2) * 256 + lo:(i % 2) * 256 + 256]
                                ins = dve.tensor_tensor_reduce(
                                    s[:, t % 3, i, lo:], src, bias[:, slot, lo:], 1.0, col("sinks", slot),
                                    ALU.add, ALU.max, sm[:, MAXI, i:i + 1])
                            then_wait(ins)
                            then_wait(dve.tensor_scalar(sm[:, NEG, :], sm[:, MAXI, :], -1.0, None, ALU.mult))
                            sinks = col("sinks", 4 * jp, 4).rearrange("p (j kv) -> p kv j", kv=2)
                            dve.tensor_tensor(sm[:, SINK_D, :].rearrange("p (kv j) -> p kv j", kv=2), sinks,
                                              sm[:, NEG, :].rearrange("p (kv j) -> p kv j", kv=2), ALU.add)\
                               .then_inc(max_ready, 1)
                        else:
                            for half in range(2):
                                ins = dve.tensor_reduce(
                                    sm[:, MAXI, 2 * half:2 * half + 2],
                                    score_banks[t % 2][half][:].rearrange("p (a k) -> p a k", a=2), AX.X, ALU.max)
                            then_wait(ins)
                            dve.tensor_scalar(sm[:, NEG, :], sm[:, MAXI, :], -1.0, None, ALU.mult)\
                               .then_inc(max_ready, 1)
                    if 1 <= t <= n:
                        kind, b, jp = groups[layer][t - 1]
                        lo = P if kind == "self" and b == 0 else 0
                        sm = small[:, (t - 1) % 3]
                        dve.wait_ge(p_ready, g0 + t)
                        total = TOTAL
                        if kind == "self":
                            then_wait(dve.tensor_tensor(sm[:, SINK_D, :], sm[:, TOTAL, :], sm[:, SINK_E, :], ALU.add))
                            total = SINK_D
                        then_wait(dve.reciprocal(sm[:, INV, :], sm[:, total, :]))
                        for i in range(4):
                            p = s[:, (t - 1) % 3, i, lo:]
                            ins = dve.tensor_scalar(p, p, sm[:, INV, i:i + 1], None, ALU.mult)
                        ins.then_inc(pn_ready, 1)
                    if t >= 3:
                        kind, b, jp = groups[layer][t - 3]
                        first = 2 * jp if kind == "self" else 6
                        q = slice(b * P, (b + 1) * P)
                        dve.wait_ge(c_hi, g0 + t - 2)
                        dve.tensor_tensor(cl[:, first:first + 2, q],
                                          mixed[(t - 3) % 2][:, 0:2 * P].rearrange("p (a q) -> p a q", a=2),
                                          ch[:, first:first + 2, q].bitcast(F32), ALU.subtract).then_inc(c_lo, 1)

            def mixer(layer):
                name = f"gu{layer}"
                f0 = layer * FT
                then_wait(dve.memset(graw[:, :, 0:F_TAPS - 1], 0.0))

                def take_tile(j, i):
                    take(name, j, i, graw[:, j // 2, F_TAPS - 1:] if j % 2 == 0 else gup[:, j // 2, :])

                def post(j, i):
                    q, f = j // 2, 2 * i + j // 2
                    if j % 2 == 0:
                        dve.wait_ge(tile_out, TILE0[name] + j + 1 + 4 * i)
                        taps(name, graw[:, q], gacc[:, q, :], q, i,
                             lambda tap: col("conv_f", f + (layer * F_TAPS + tap) * FT), F_TAPS)
                    else:
                        dve.wait_ge(tile_out, TILE0[name] + j + 1 + 4 * i)
                        dve.wait_ge(silu_ready, CONV0[name] + q + 1 + 2 * i)
                        dve.tensor_tensor(gup[:, q, :], gsil[:, q, :], gup[:, q, :], ALU.mult).then_inc(a_ready, 1)
                        dve.wait_ge(a_ready, f0 + q + 1 + 2 * i)
                        dve.wait_ge(a_hi, f0 + q + 1 + 2 * i)
                        dve.tensor_tensor(row(al, f), gup[:, q, :], row(ah, f).bitcast(F32), ALU.subtract)\
                           .then_inc(a_lo, 1)
                slab_steps(dve, name, cut_lo, post, take_tile)

            def deltanet():
                tokens = lambda t: t.unsqueeze(2).to_broadcast([P, NB, VH])
                after(dve, "act", "gate exp")
                then_wait(dve.tensor_scalar(gate[:, BETA], gate[:, EXP_B], 1.0, None, ALU.add))
                step("dve", "beta", None, dve.reciprocal(gate[:, BETA], gate[:, BETA]))
                after(dve, "act", "gate ln")
                then_wait(dve.scalar_tensor_tensor(out=gate[:, SOFT], in0=gate[:, LOGIT], scalar=0.0,
                                                   in1=gate[:, LN], op0=ALU.max, op1=ALU.add))
                ea = gate[:, EXP_A, 0, :].unsqueeze(1).to_broadcast([P, NB, VH])
                step("dve", "g", None, dve.tensor_tensor(gate[:, NEG_G], gate[:, SOFT], ea, ALU.mult))
                after(dve, "pe", "cumsum")
                step("dve", "cumsum", None, dve.tensor_scalar(
                    gate[:, GC].rearrange("p c v -> p (c v)"), stats[:, 128:128 + NB * VH], -1.0, None, ALU.mult))
                def ahead(lv, c):
                    if lv == LEVELS - 2:
                        for v in range(VH):
                            ins = dve.tensor_scalar(attn[:, v, :], con[:, TRI, :], gate[:, NEG_G, c, v:v + 1],
                                                    None, ALU.mult)
                        step("dve", "NG", c, ins)
                    if lv < LEVELS - 1:
                        return
                    after(dve, "pe", "negcum", c)
                    for v in range(VH):
                        ins = dve.scalar_tensor_tensor(
                            out=decay[:, v, :], in0=NEGCUM[v // 3][:, (v % 3) * P:(v % 3 + 1) * P],
                            scalar=gate[:, GC, c, v:v + 1], in1=con[:, CAUSAL, :], op0=ALU.add, op1=ALU.add)
                    step("dve", "log decay", c, ins)
                    for hf, bank in enumerate(NEGCUM):
                        ins = dve.tensor_tensor(tail[:, 0, heads(hf)], third(bank)[:, :, P - 1],
                                                gate[:, GC, c, heads(hf)], ALU.add)
                    step("dve", "tail", c, ins)

                after(dve, "dve", "cumsum")
                ahead(LEVELS - 2, 0)
                ahead(LEVELS - 1, 0)
                for j in L2:
                    r = l2_tile(j)
                    after(dve, "act", f"l2 inverse {j}")
                    if j < QKH:
                        ins = dve.scalar_tensor_tensor(out=qkv[:, j, :], in0=qkv[:, j, :], scalar=DK ** -0.5,
                                                       in1=r, op0=ALU.mult, op1=ALU.mult)
                    else:
                        ins = dve.tensor_tensor(qkv[:, j, :], qkv[:, j, :], r, ALU.mult)
                    step("dve", f"l2 {j}", None, ins)
                after(dve, "act", "exp cumsum")
                step("dve", "nbe", None, dve.scalar_tensor_tensor(
                    out=gate[:, NBE], in0=gate[:, BETA], scalar=-1.0, in1=gate[:, EXP_GC], op0=ALU.mult, op1=ALU.mult))
                after(dve, "dve", "nbe")

                def prepare(c):
                    s2 = c % 2
                    beta = gate[:, BETA, c, :].unsqueeze(2)
                    after(dve, "act", "decay", c)
                    then_wait(dve.tensor_tensor(amat[:], decay[:], beta.to_broadcast([P, VH, P]), ALU.mult))
                    after(dve, "pe", "kk", c)
                    pair = lambda x: x[:].rearrange("p (j e) t -> p j e t", e=2)
                    both = lambda bank: third(bank).unsqueeze(2).to_broadcast([P, 3, 2, P])
                    step("dve", "A", c, dve.tensor_tensor(pair(amat), both(banks[0]), pair(amat), ALU.mult))
                    m0 = con[:, LEVEL0, :].unsqueeze(1).to_broadcast([P, VH, P])
                    idb = ident.unsqueeze(1).to_broadcast([P, VH, P])
                    after(dve, "dve", "A", c)
                    then_wait(dve.tensor_tensor(tmat[:], amat[:], m0, ALU.mult))
                    step("dve", "T0", c, dve.tensor_tensor(tmat[:], idb, tmat[:], ALU.subtract))
                    after(dve, "pe", "qk", c)
                    step("dve", "attn", c, dve.tensor_tensor(pair(attn), both(banks[1]), pair(decay), ALU.mult))
                    if c > 1:
                        finish(c - 2)
                    after(dve, "pe", "v turned", c)
                    for hf in HALF:
                        ins = dve.tensor_tensor(vbeta[:, s2, heads(hf), :], third(banks[3 + hf]),
                                                gate[:, BETA, c, heads(hf)].unsqueeze(2).to_broadcast([P, 3, P]), ALU.mult)
                    step("dve", "vbeta", c, ins)

                def level(lv, c):
                    above = con[:, ABOVE + (lv - 1) // 2, (lv - 1) % 2 * (P // 2):((lv - 1) % 2 + 1) * (P // 2)]
                    above = above.rearrange("p (n b) -> p n b", b=2 ** lv).unsqueeze(1)\
                        .to_broadcast([P, VH, P // 2 // 2 ** lv, 2 ** lv])
                    after(dve, "pe", f"Z {lv}", c)
                    after(dve, "pool", f"clear {lv}", c)
                    step("dve", f"z {lv}", c, dve.tensor_tensor(
                        blocks(zneg[:, lv % 2], lv, 1), packed(banks[0], lv), above, ALU.mult))
                    if lv == LEVELS - 1 and c + 1 < NB:
                        ahead(lv, c + 1)
                    after(dve, "pe", f"UZ {lv}", c)
                    u = blocks(umat[:, c % 2], lv, 1)
                    step("dve", f"U {lv}", c, dve.tensor_tensor(u, packed(banks[1], lv), u, ALU.add))
                    if lv < LEVELS - 1:
                        after(dve, "pe", f"ZT {lv}", c)
                        tt = blocks(tmat[:], lv, 0)
                        step("dve", f"T {lv}", c, dve.tensor_tensor(tt, packed(banks[2], lv), tt, ALU.add))

                def recur(lv, c):
                    s2 = c % 2
                    if lv == 1 and c:
                        after(dve, "pe", "kS", c)
                        for v in range(VH):
                            ins = dve.scalar_tensor_tensor(
                                out=vbeta[:, s2, v, :], in0=banks[3 + v // 3][:, (v % 3) * P:(v % 3 + 1) * P],
                                scalar=gate[:, NBE, c, v:v + 1], in1=vbeta[:, s2, v, :], op0=ALU.mult, op1=ALU.add)
                        step("dve", "R", c, ins)
                    elif lv == 4 and c < NB - 1:
                        after(dve, "pe", "state", c)
                        for v in range(VH):
                            ps = banks[5 + v // 3][:, (v % 3) * P:(v % 3 + 1) * P]
                            if c:
                                ins = dve.scalar_tensor_tensor(out=state[:, v, :], in0=state[:, v, :],
                                                               scalar=last[:, s2, v:v + 1], in1=ps,
                                                               op0=ALU.mult, op1=ALU.add)
                            else:
                                ins = dve.tensor_copy(state[:, v, :], ps)
                        step("dve", "state", c, ins)

                def finish(c):
                    after(dve, "act", "norm inverse", c)
                    if c:
                        after(dve, "dve", "lo", c - 1)
                    for hf in HALF:
                        ins = dve.scalar_tensor_tensor(out=og[:, heads(hf), :], in0=third(banks[3 + hf]),
                                                       scalar=col("out_g"), in1=osq[:, heads(hf), :],
                                                       op0=ALU.mult, op1=ALU.mult)
                    step("dve", "out", c, ins)

                def finish_gated(c):
                    t = slice(c * P, (c + 1) * P)
                    after(dve, "dve", "out", c)
                    step("dve", "gated", c, dve.tensor_tensor(og[:], og[:], zt[:, 0:VH, t], ALU.mult))

                def finish_lo(c):
                    t = slice(c * P, (c + 1) * P)
                    after(dve, "act", "hi", c)
                    step("dve", "lo", c, dve.tensor_tensor(cl1[:, 0:VH, t], og[:], ch1[:, 0:VH, t].bitcast(F32),
                                                           ALU.subtract))

                for c in range(NB + 1):
                    prepare(c) if c < NB else finish(c - 2)
                    for lv in LV:
                        if c < NB:
                            level(lv, c)
                        if c + 1 < NB and lv < LEVELS - 1:
                            ahead(lv, c + 1)
                        if c:
                            recur(lv, c - 1)
                        if c > 1 and lv == 2:
                            finish_gated(c - 2)
                        if c > 1 and lv == 3:
                            finish_lo(c - 2)
                finish(NB - 1)
                finish_gated(NB - 1)
                finish_lo(NB - 1)

            dve.memset(eps[:], EPS).then_inc(eps_set, 1)
            then_wait(dve.memset(brow[:], -BIG))
            dve.wait_ge(mem_sq, 1)
            for n in (4, 2):
                then_wait(dve.tensor_tensor(m_sq[:, 0:n, :], m_sq[:, 0:n, :], m_sq[:, n:2 * n, :], ALU.add))
            dve.tensor_tensor(m_ss[:], m_sq[:, 0, :], m_sq[:, 1, :], ALU.add).then_inc(mem_sum, 1)
            cut_lo(0)
            cut_lo(1)
            dve.wait_ge(mem_root, 1)
            dve.wait_ge(par_in, 32)
            then_wait(dve.reciprocal(m_rms[:], m_rms[:]))
            for i in range(5):
                if i < 4:
                    layer, k0 = i // 2, i % 2 * (KD // 2)
                    for k in range(k0, k0 + KD // 2):
                        ins = dve.scalar_tensor_tensor(out=mn[:, layer, k, :], in0=mT[:, k, :],
                                                       scalar=col("mem_g", layer * KD + k), in1=m_rms[:],
                                                       op0=ALU.mult, op1=ALU.mult)
                    ins.then_inc(mem_norm, 1)
                if i:
                    layer, ks = (i - 1) // 2, slice((i - 1) % 2 * (KD // 2), ((i - 1) % 2 + 1) * (KD // 2))
                    dve.wait_ge(mem_norm, i)
                    dve.wait_ge(mem_hi, i)
                    dve.tensor_tensor(ml[:, layer, ks], mn[:, layer, ks], mh[:, layer, ks].bitcast(F32), ALU.subtract)\
                       .then_inc(mem_lo, 1)
            dve.wait_ge(bias_mm, 1)
            dve.tensor_copy(brow[:, P:2 * P], mixed[0][0:A_HEADS, 0:WINDOW]).then_inc(bias_row, 1)
            then_wait(dve.memset(ssq[:], 0.0))
            dve.wait_ge(x_in, 16)
            for k in range(8):
                layer, part = k // 4, k % 4
                bank = gemm_out[k % 2]
                if part != 2:
                    dve.wait_ge(slab_done, k + 1)
                if part < 2:
                    dve.tensor_scalar(mem_k[:, layer, part, :], bank[:, 0:MEM], DH ** -0.5, None, ALU.mult)\
                       .then_inc(tile_out, 1)
                elif part == 3:
                    for mt in range(MT):
                        dve.tensor_copy(mem_v[:, layer, mt, :], banks[2 + mt][:, 0:2 * P]).then_inc(tile_out, 1)
                cut_lo(k + CUT)
                if k:
                    dve.wait_ge(sq_summed, k)
                sum_and_lo(0, k)
            for n in range(6):
                dve.wait_ge(bias_mm, n + 2)
                dve.tensor_copy(bias[:, 2 * n:2 * n + 2, :].rearrange("p a k -> p (a k)"), banks[2 + n][:])\
                   .then_inc(bias_set, 1)
            dve.wait_ge(bias_out, 16)
            inverse_rms(0)
            slab_steps(dve, "in0", cut_lo, lambda j, i: None, lambda j, i: take(
                "in0", j, i, row(pa, 4 * i + j if j < 4 else j)))
            dve.wait_ge(tile_out, TILE0["out0"])
            then_wait(dve.tensor_scalar(pa[:, 0, :], pa[:, 0, :], DH ** -0.5, None, ALU.mult))
            dve.wait_ge(v_turned, 1)
            dve.tensor_copy(vtok[:].rearrange("p b d -> p (b d)"), turned[0][:]).then_inc(v_tok, 1)
            dve.wait_ge(bias_set, 6)
            attention(0)
            residual("out0", 1)
            inverse_rms(1)
            mixer(0)
            residual("dn0", 2)
            inverse_rms(2)
            dve.wait_ge(ba_in, 16)
            dve.tensor_tensor(wbag[:], wba[:], col("mix_g", KD, KD).unsqueeze(2).to_broadcast([P, KD, 2 * VH]),
                              ALU.mult).then_inc(ba_gain, 1)
            then_wait(dve.memset(craw[:, :, 0:B_TAPS - 1], 0.0))

            def conv_post(k, i):
                dve.wait_ge(tile_out, TILE0["in1"] + k + 1 + 4 * i)
                taps("in1", craw[:, k % 2], cacc[:, k % 2, :], k, i,
                     lambda tap: col("conv_b", 4 * i + (k + tap * NQKV)), B_TAPS)
            with dve.Fori(0, NQKV // 4) as i:
                for j in range(4):
                    take("in1", j, i, craw[:, j % 2, B_TAPS - 1:])
                    cut_lo(SLAB0["in1"] + j + CUT, 4 * i)
                    conv_post(j, i)
            for k in range(NQKV, 20):
                take("in1", k, 0, zt[:, k - NQKV, :])
                cut_lo(SLAB0["in1"] + k + CUT)
            after(dve, "pe", "ba")
            step("dve", "ba scaled", None, dve.tensor_tensor(craw[0:2 * VH, 0, 0:SEQ], stats[0:2 * VH, :],
                                                             rinv[0:2 * VH, :], ALU.mult))
            after(dve, "pe", "ba turned")
            step("dve", "ba", None, dve.tensor_copy(ba[:], banks[6][:, 0:NB * 2 * VH].rearrange("p (b v) -> p b v", b=NB)))
            after(dve, "dve", "ba")
            dt = col("dt_bias", 0, VH).unsqueeze(1).to_broadcast([P, NB, VH])
            step("dve", "gate in", None, dve.tensor_tensor(gate[:, LOGIT], ba[:, :, VH:], dt, ALU.add))
            attention(1)
            deltanet()
            after(dve, "dve", "lo", NB - 1)
            residual("out1", 3)
            inverse_rms(3)
            mixer(1)
            residual("dn1", 4)
            inverse_rms(4)
            for m in range(KD):
                dve.scalar_tensor_tensor(out=h[:, m, :], in0=h[:, m, :], scalar=gain(4, m), in1=rinv[:],
                                         op0=ALU.mult, op1=ALU.mult).then_inc(out_ready, 1)

        @block.tensor
        def _(pe):
            def slab(n, more, out, moving, first=True, last=True, k0=0):
                pe.wait_ge(lo_cut, n + 1 + more)
                count = slab_k(n)
                for k in range(count):
                    w = slice(k * P, (k + 1) * P)
                    xhi, xlo = moving(k0 + k)
                    pe.matmul(out, wh[:, n % CUT, w], xhi, start=first and k == 0, stop=False)
                    pe.matmul(out, wh[:, n % CUT, w], xlo, start=False, stop=False)
                    ins = pe.matmul(out, wl[:, n % CUT, w], xhi, start=False, stop=last and k == count - 1)
                ins.then_inc(slab_done, 1)

            def of(hi, lo):
                return lambda k: (hi[:, k, :], lo[:, k, :])

            def part_of(n, moving, ks, out, first=0, last=KD - 1):
                pe.wait_ge(lo_cut, n + 1)
                for k in ks:
                    w = slice(k * P, (k + 1) * P)
                    xhi, xlo = moving(k)
                    pe.matmul(out, wh[:, n % CUT, w], xhi, start=k == first, stop=False)
                    pe.matmul(out, wh[:, n % CUT, w], xlo, start=False, stop=False)
                    ins = pe.matmul(out, wl[:, n % CUT, w], xhi, start=False, stop=k == last)
                return ins

            def start_early(name, moving, early, first_slabs=(0, 1)):
                pe.wait_ge(tile_out, TILE0[name])
                for j in first_slabs:
                    part_of(SLAB0[name] + j, moving, early, gemm_out[(TILE0[name] + j) % 2][:], early[0], None)

            def products(name, moving, e=None, early=None):
                n0, g0, count = SLAB0[name], TILE0[name], dict(STREAM)[name]

                def one(j, i):
                    pe.wait_ge(tile_out, g0 + j - 1 + 4 * i)
                    slab(n0 + j, 4 * i, gemm_out[(g0 + j) % 2][:], moving)

                if early is not None:
                    rest = [k for k in range(KD) if k not in early]
                    for j in range(2):
                        part_of(n0 + j, moving, rest, gemm_out[(g0 + j) % 2][:], None, rest[-1])\
                            .then_inc(slab_done, 1)
                    one(2, 0)
                    one(3, 0)
                if e is not None:
                    pe.wait_ge(tile_out, g0 - 1)
                    for k in range(KD):
                        pe.wait_ge(x_lo, KD * e + k + 1)
                        if k == KD - 1:
                            if e == 0:
                                pe.wait_ge(bias_set, 6)
                            norm(e)
                        ins = part_of(n0, moving, [k], gemm_out[g0 % 2][:])
                    ins.then_inc(slab_done, 1)
                    for j in range(1, 4):
                        one(j, 0)
                with pe.Fori(1, count // 4) as i:
                    for j in range(4):
                        one(j, i)
                for k in range(count - count % 4, count):
                    one(k, 0)

            def down(layer):
                n0, g0 = SLAB0[f"dn{layer}"], TILE0[f"dn{layer}"]
                with pe.Fori(0, KD // 2) as i:
                    for j in range(8):
                        if j % 4 == 0:
                            pe.wait_ge(tile_out, g0 + j // 4 - 1 + 2 * i)
                        pe.wait_ge(a_lo, FT * layer + DOWN_AT[j % 4] + DOWN_K[j % 4])
                        slab(n0 + j, 8 * i, gemm_out[(g0 + j // 4) % 2][:], of(ah, al), first=j % 4 == 0,
                             last=j % 4 == 3, k0=DOWN_AT[j % 4])

            def norm(e):
                pe.wait_ge(sq_summed, KD * (e + 1))
                pe.matmul(stats[:], ones, ssq[:], start=True, stop=True).then_inc(stat_sum, 1)

            def attention(layer):
                s, pt, small = softmax_bufs[layer]
                n, g0 = len(groups[layer]), GROUP0[layer]
                queries = pa[:, 8:10] if layer == 0 else zt[:, 6:8]
                for t in range(n + 3):
                    if t == n + 1 and layer == 0:
                        pe.wait_ge(c_lo, AJ // 2 * NB)
                        pe.wait_ge(p_ready, n)
                        start_early("out0", of(ch0, cl0), SELF_TILES, [0])
                    if t < n:
                        kind, b, jp = groups[layer][t]
                        q = slice(b * P, (b + 1) * P)
                        if t >= 2:
                            used = max_ready if groups[layer][t - 2][0] == "self" else p_ready
                            pe.wait_ge(used, g0 + t - 1)
                        for i in range(4):
                            half, side = slice((i // 2) * DH, (i // 2 + 1) * DH), (i % 2) * 256
                            out = score_banks[t % 2][i // 2]
                            if kind == "self":
                                lo = P if b == 0 else 0
                                ins = pe.matmul(out[:, side + lo:side + 256], pa[half, 2 + 2 * jp + i % 2, q],
                                                pa[half, 0, (b - 1) * P + lo:(b + 1) * P], start=True, stop=True)
                            else:
                                ins = pe.matmul(out[:, side:side + 256], queries[half, i % 2, q],
                                                mem_k[half, layer, i % 2, :], start=True, stop=True)
                        ins.then_inc(sc_ready, 1)
                    if 2 <= t < n + 2:
                        u = t - 2
                        kind, b, jp = groups[layer][u]
                        pe.wait_ge(pn_ready, g0 + u + 1)
                        if u:
                            pe.wait_ge(pt_ready, g0 + u)
                        for kc in range(1 if kind == "self" and b == 0 else 0, 2):
                            for i in range(4):
                                ins = pe.transpose(turned[kc][:, i * P:(i + 1) * P],
                                                   s[:, u % 3, i, kc * P:(kc + 1) * P], ident)
                        ins.then_inc(tp_ready, 1)
                    if t >= 3:
                        u = t - 3
                        kind, b, jp = groups[layer][u]
                        pe.wait_ge(pt_ready, g0 + u + 1)
                        if u >= 2:
                            pe.wait_ge(c_lo, g0 + u - 1)
                        out, p = mixed[u % 2], pt[:, u % 2]
                        for half in range(2):
                            if kind == "self":
                                d = slice(half * DH, (half + 1) * DH)
                                parts = range(1 if b == 0 else 0, 2)
                                for kc in parts:
                                    ins = pe.matmul(out[d, 0:2 * P], vtok[:, b - 1 + kc, d],
                                                    p[:, kc, 2 * half:2 * half + 2, :].rearrange("p a q -> p (a q)"),
                                                    start=kc == parts[0], stop=kc == 1)
                                continue
                            for a in range(2):
                                hd = 2 * a + half
                                for kc in range(2):
                                    ins = pe.matmul(out[half * DH:(half + 1) * DH, a * P:(a + 1) * P],
                                                    mem_v[:, layer, kc, hd * DH:(hd + 1) * DH],
                                                    p[:, kc, 2 * half + a, :], start=kc == 0, stop=kc == 1)
                        ins.then_inc(ov_ready, 1)
                if layer == 0:
                    start_early("out0", of(ch0, cl0), SELF_TILES, [1])
                pe.wait_ge(c_lo, g0 + n)

            def gates():
                pe.wait_ge(ba_gain, 1)
                for k in range(KD):
                    ins = pe.matmul(stats[0:2 * VH, :], wbag[:, k, :], h[:, k, :], start=k == 0, stop=k == KD - 1)
                step("pe", "ba", None, ins)
                after(pe, "dve", "ba scaled")
                for b in range(NB):
                    ins = pe.transpose(banks[6][:, 2 * VH * b:2 * VH * (b + 1)], craw[0:2 * VH, 0, b * P:(b + 1) * P],
                                       ident[0:2 * VH, 0:2 * VH])
                step("pe", "ba turned", None, ins)

            def keep_clock(bank, n):
                for _ in range(n):
                    pe.matmul(bank[:], con[:, ONES, 0:P // 2].bitcast(BF16),
                              con[:, 0:2, :].rearrange("p a t -> p (a t)").bitcast(BF16), start=True, stop=True)

            def deltanet():
                for j in L2:
                    if j == QKH:
                        after(pe, "dve", "g")
                        step("pe", "cumsum", None, pe.matmul(
                            stats[:, 128:128 + NB * VH], con[:, TRI, :], gate[:, NEG_G].rearrange("p c v -> p (c v)"),
                            start=True, stop=True))
                    after(pe, "pool", f"l2 square {j}")
                    step("pe", f"l2 {j}", None, pe.matmul(banks[j][:], ones, l2_tile(j), start=True, stop=True))

                def tile(bank, v):
                    return bank[:, v * P:(v + 1) * P]

                def ahead(c):
                    after(pe, "dve", "NG", c)
                    for hf, bank in enumerate(NEGCUM):
                        ins = pe.matmul(bank[:, 0:3 * P], ones, flat(attn[:, heads(hf), :]), start=True, stop=True)
                    step("pe", "negcum", c, ins)

                def prepare(c):
                    t = slice(c * P, (c + 1) * P)
                    for j in range(QKH):
                        ins = pe.matmul(tile(banks[0], j), qkv[:, QKH + j, t], qkv[:, QKH + j, t], start=True, stop=True)
                    step("pe", "kk", c, ins)
                    if c > 1:
                        after(pe, "act", "norm ln", c - 2)
                    for j in range(QKH):
                        ins = pe.transpose(tile(banks[5], j), qkv[:, QKH + j, t], ident)
                    step("pe", "k turned", c, ins)
                    if c:
                        after(pe, "dve", f"U {LEVELS - 1}", c - 1)
                    for j in range(QKH):
                        ins = pe.matmul(tile(banks[1], j), qkv[:, j, t], qkv[:, QKH + j, t], start=True, stop=True)
                    step("pe", "qk", c, ins)
                    keep_clock(banks[6], WAIT_T0)
                    after(pe, "dve", "T0", c)
                    for v in range(VH):
                        ins = pe.transpose(tile(TURNED_T[v // 3], v % 3), tmat[:, v, :], ident)
                    step("pe", "T turned", c, ins)
                    after(pe, "dve", "attn", c)
                    after(pe, "act", "last", c)
                    for v in range(VH):
                        ins = pe.transpose(tile(NEGCUM[v // 3], v % 3), attn[:, v, :], ident)
                    step("pe", "attn turned", c, ins)
                    if c > 1:
                        after(pe, "dve", "out", c - 2)
                    for v in range(VH):
                        ins = pe.transpose(tile(banks[3 + v // 3], v % 3), qkv[:, 2 * QKH + v, t], ident)
                    step("pe", "v turned", c, ins)
                    keep_clock(banks[1], WAIT_U0)
                    after(pe, "act", "U0", c)

                def level(lv, c, between):
                    half = slice(0, P // 2)
                    out = lambda bank, v: bank[:, v * P // 2:(v + 1) * P // 2]\
                        .rearrange("p (n b) -> p n b", b=2 ** lv)
                    if lv > 1:
                        after(pe, "dve", f"U {lv - 1}", c)
                    for v in range(VH):
                        ins = pe.matmul(out(banks[0], v), amat[:, v, :], blocks(umat[:, c % 2, v, :], lv, 1),
                                        start=True, stop=True)
                    step("pe", f"Z {lv}", c, ins)
                    if lv == 1:
                        after(pe, "act", "attnT", c)
                    if lv == LEVELS - 1 and c + 1 < NB:
                        ahead(c + 1)
                    else:
                        keep_clock(banks[7], 1 if c and lv < LEVELS - 2 else WAIT_Z)
                    between()
                    after(pe, "dve", f"z {lv}", c)
                    if lv > 1:
                        after(pe, "dve", f"T {lv - 1}", c)
                    for v in range(VH):
                        ins = pe.matmul(out(banks[1], v), tmat[:, v, :], blocks(zneg[:, lv % 2, v, :], lv, 1),
                                        start=True, stop=True)
                    step("pe", f"UZ {lv}", c, ins)
                    if lv < LEVELS - 1:
                        for v in range(VH):
                            ins = pe.matmul(out(banks[2], v), zneg[:, lv % 2, v, :], blocks(tmat[:, v, :], lv, 0),
                                            start=True, stop=True)
                        step("pe", f"ZT {lv}", c, ins)

                def recur(lv, c):
                    s2, t = c % 2, slice(c * P, (c + 1) * P)
                    if lv == 1 and c + 1 < NB:
                        after(pe, "dve", "vbeta", c + 1)
                    if lv == 1 and c:
                        after(pe, "dve", "state", c - 1)
                        after(pe, "dve", "out", c - 1)
                        for v in range(VH):
                            ins = pe.matmul(tile(banks[3 + v // 3], v % 3), qkv[:, QKH + v // 2, t], state[:, v, :],
                                            start=True, stop=True)
                        step("pe", "kS", c, ins)
                    elif lv == 2:
                        if c:
                            after(pe, "dve", "R", c)
                            after(pe, "act", "norm ln", c - 1)
                        for v in range(VH):
                            ins = pe.matmul(tile(banks[5 + v // 3], v % 3), umat[:, s2, v, :], vbeta[:, s2, v, :],
                                            start=True, stop=True)
                        step("pe", "delta", c, ins)
                    elif lv == 3:
                        after(pe, "pool", "qdec", c)
                        after(pe, "act", "delta", c)
                        for v in range(VH):
                            o = tile(banks[3 + v // 3], v % 3)
                            if c:
                                pe.matmul(o, state[:, v, :], qdec[:, s2, v, :], start=True, stop=False)
                            ins = pe.matmul(o, delta[:, v, :], attn_t[:, s2, v, :], start=c == 0, stop=True)
                        step("pe", "out", c, ins)
                    elif lv == 4 and c < NB - 1:
                        for v in range(VH):
                            ins = pe.matmul(tile(banks[5 + v // 3], v % 3), ktail[:, s2, v, :], delta[:, v, :],
                                            start=True, stop=True)
                        step("pe", "state", c, ins)
                    elif lv == 5:
                        if c < NB - 1:
                            after(pe, "dve", "state", c)
                        after(pe, "act", "square", c)
                        for hf in HALF:
                            ins = pe.matmul(banks[5 + hf][:, 0:3 * P], ones, flat(osq[:, heads(hf), :]),
                                            start=True, stop=True)
                        step("pe", "norm", c, ins)

                after(pe, "act", "l2 ln 2")
                ahead(0)
                keep_clock(banks[6], WAIT_L2)
                after(pe, "dve", f"l2 {2 * QKH - 1}")
                for c in range(NB + 1):
                    if c < NB:
                        prepare(c)
                    for lv in LV:
                        between = lambda: recur(lv, c - 1) if c else None
                        if c < NB:
                            level(lv, c, between)
                        else:
                            if lv == 1:
                                after(pe, "dve", f"U {LEVELS - 1}", c - 1)
                            between()
                            keep_clock(banks[7], WAIT_LAST)

            pe.wait_ge(par_in, 32)
            pe.wait_ge(mem_sum, 1)
            pe.matmul(stats[:, 0:MEM], ones, m_ss[:], start=True, stop=True).then_inc(mem_stat, 1)
            pe.wait_ge(rel_in, 32)
            pe.matmul(mixed[0][0:A_HEADS, 0:WINDOW], relb[:], oneh[:], start=True, stop=True).then_inc(bias_mm, 1)
            for k in range(8):
                layer, part = k // 4, k % 4
                if k >= 2:
                    pe.wait_ge(tile_out, k - 1)
                bank = gemm_out[k % 2]
                if part < 2:
                    pe.wait_ge(lo_cut, k + 1)
                    for kk in range(KD):
                        if part == 0 and kk % (KD // 2) == 0:
                            pe.wait_ge(mem_lo, 2 * layer + 2 * kk // KD + 1)
                        w = slice(kk * P, (kk + 1) * P)
                        hi, lo, o = wh[:, k % CUT, w], wl[:, k % CUT, w], bank[:, 0:MEM]
                        pe.matmul(o, hi, mh[:, layer, kk, :], start=kk == 0, stop=False)
                        pe.matmul(o, hi, ml[:, layer, kk, :], start=False, stop=False)
                        ins = pe.matmul(o, lo, mh[:, layer, kk, :], start=False, stop=kk == KD - 1)
                    ins.then_inc(slab_done, 1)
                    continue
                pe.wait_ge(lo_cut, k + 1)
                for mt in range(MT):
                    t, o = slice(mt * P, (mt + 1) * P), banks[2 + mt][:, 0:2 * P]
                    for half_k in range(KD // 2):
                        kk = (part - 2) * (KD // 2) + half_k
                        w = slice(half_k * 2 * P, (half_k + 1) * 2 * P)
                        hi, lo = wh[:, k % CUT, w], wl[:, k % CUT, w]
                        pe.matmul(o, mh[:, layer, kk, t], hi, start=kk == 0, stop=False)
                        pe.matmul(o, mh[:, layer, kk, t], lo, start=False, stop=False)
                        ins = pe.matmul(o, ml[:, layer, kk, t], hi, start=False, stop=kk == KD - 1)
                ins.then_inc(slab_done, 1)
            pe.wait_ge(tile_out, 8)
            pe.wait_ge(bias_in, 16 * A_HEADS)
            for n in range(6):
                pe.matmul(banks[2 + n][:], con[:, FLIP, :],
                          bias_rev[:, 2 * n:2 * n + 2, :].rearrange("p a k -> p (a k)"), start=True, stop=True)\
                  .then_inc(bias_mm, 1)
            products("in0", of(xh, xl), 0)
            pe.wait_ge(tile_out, TILE0["in0"] + 2)
            for b in range(NB):
                ins = pe.transpose(turned[0][:, b * P:(b + 1) * P], pa[:, 1, b * P:(b + 1) * P], ident)
            ins.then_inc(v_turned, 1)
            pe.wait_ge(tile_out, TILE0["out0"])
            pe.wait_ge(v_tok, 1)
            attention(0)
            products("out0", of(ch0, cl0), early=SELF_TILES)
            products("gu0", of(xh, xl), 1)
            down(0)
            products("in1", of(xh, xl), 2)
            gates()
            pe.wait_ge(tile_out, TILE0["out1"])
            attention(1)
            deltanet()
            start_early("out1", of(ch1, cl1), [6, 7])
            after(pe, "dve", "lo", NB - 1)
            products("out1", of(ch1, cl1), early=[6, 7])
            products("gu1", of(xh, xl), 3)
            down(1)
            norm(4)


def head_order():
    return [kv * AJ + j for j in range(AJ) for kv in range(A_KV)]


def bucket_onehot():
    d = np.arange(WINDOW)
    half = N_BUCKETS // 2
    far = half + (np.log(np.maximum(d, 1).astype(np.float32) / np.float32(half))
                  / np.float32(math.log(MAX_DISTANCE / half)) * np.float32(N_BUCKETS - half)).astype(np.int32)
    bucket = np.where(d < half, d, np.minimum(far, N_BUCKETS - 1))
    out = np.zeros((N_BUCKETS, WINDOW), np.float32)
    out[bucket[::-1], d] = 1.0
    return out


def constant_tiles():
    t, s = np.arange(P)[:, None], np.arange(P)[None, :]
    out = np.zeros((NCONST, P, P), np.float32)
    out[IDENT] = t == s
    out[ONES] = 1.0
    out[FLIP] = t + s == P - 1
    out[TRI] = t <= s
    out[CAUSAL] = np.where(s <= t, 0.0, -BIG)
    out[LEVEL0] = (t % 2 == 1) & (s == t - 1)
    out = np.ascontiguousarray(out.transpose(1, 0, 2))
    for lv in range(1, LEVELS):
        b = 2 ** lv
        column = np.arange(P).reshape(-1, 2, b)[:, 1].reshape(1, -1)
        above = -1.0 * (t // b == column // b - 1)
        out[:, ABOVE + (lv - 1) // 2, (lv - 1) % 2 * (P // 2):][:, :P // 2] = above
    return out


def slabs(w):
    *lead, k, c = w.shape
    w = w.reshape(*lead, k // P, P, c // P, P)
    n = len(lead)
    w = w.transpose(*range(n), n + 2, n + 1, n, n + 3)
    return np.ascontiguousarray(w.reshape(*lead, c // P, P, k))


def lay_out(x, mem, rel_bias, norm_mix_g, norm_mem_g, w_mem_kv, w_out, w_in_a, sinks_a, w_in_b,
            conv_qkv_b, a_log_b, dt_bias_b, out_norm_g_b, norm_ffn_g, w_gate_up, ffn_conv_w,
            ffn_conv_b, w_down, final_norm_g):
    order = head_order()
    feat = lambda a: np.moveaxis(a.reshape(*a.shape[:-1], a.shape[-1] // P, P), -1, 0).reshape(P, -1)
    rows = lambda a: np.broadcast_to(a.reshape(1, -1), (P, a.size))
    params = np.concatenate([
        feat(norm_mix_g), feat(norm_mem_g), feat(norm_ffn_g), feat(final_norm_g), feat(conv_qkv_b[0]),
        feat(ffn_conv_w), feat(ffn_conv_b), feat(out_norm_g_b[0]), rows(sinks_a[0][order]),
        rows(dt_bias_b[0]), rows(a_log_b[0])], axis=1)
    nq, nkv = A_HEADS * DH, A_KV * DH
    wa = w_in_a[0]
    q_cols = np.concatenate([np.arange(hd * DH, (hd + 1) * DH) for hd in order])
    wa = np.concatenate([wa[:, nq:nq + 2 * nkv], wa[:, q_cols], wa[:, nq + 2 * nkv:]], axis=1)
    w_o = np.stack([np.concatenate([w_out[0][q_cols], w_out[0][nq:]]), w_out[1]])
    nb = (NQKV + VH) * P
    wb = w_in_b[0]
    w_ba = wb[:, nb:nb + 2 * VH].reshape(KD, P, 2 * VH).transpose(1, 0, 2)
    wb = np.concatenate([wb[:, :nb], wb[:, nb + 2 * VH:]], axis=1)
    gu = slabs(w_gate_up)
    gu = np.stack([gu[:, :FT], gu[:, FT:]], axis=2).reshape(2, 2 * FT, P, D_MODEL)
    w_v = w_mem_kv[..., 2 * P:].reshape(2, 2, KD // 2, P, 2 * P).transpose(0, 1, 3, 2, 4).reshape(2, 2, P, D_MODEL)
    tiles = lambda a: a.T.reshape(KD, P, a.shape[0]).transpose(1, 0, 2)
    return {
        "xT": tiles(x[0]), "memT": tiles(mem[0]), "params": params, "consts": constant_tiles(),
        "rel_bias": rel_bias[:, order], "onehot": bucket_onehot(), "w_mem": np.concatenate([slabs(w_mem_kv[..., :2 * P]), w_v], axis=1),
        "w_in_a": slabs(wa), "w_in_b": slabs(wb), "w_ba": w_ba, "w_out": slabs(w_o), "w_gu": gu,
        "w_dn": slabs(w_down),
    }


def kernel(**inputs):
    import concourse.bacc as bacc
    from concourse.bass_utils import run_bass_kernel_spmd

    nc = bacc.Bacc("TRN2", target_bir_lowering=False, num_devices=1)
    laid = lay_out(**{k: np.asarray(v) for k, v in inputs.items()})
    arrays = {name: np.ascontiguousarray(a) for name, a in laid.items()}
    args = [nc.dram_tensor(name, a.shape, mybir.dt.from_np(a.dtype), kind="ExternalInput").ap()
            for name, a in arrays.items()]
    args.append(nc.dram_tensor("outT", (P, KD, SEQ), F32, kind="ExternalOutput").ap())
    program(nc, *args)
    r = run_bass_kernel_spmd(nc, [arrays], core_ids=[0])
    out = r.results[0]["outT"].reshape(P, KD, SEQ).transpose(2, 1, 0).reshape(1, SEQ, D_MODEL)
    return np.ascontiguousarray(out)
```
